# Optimizing a Trainium2 kernel written in Bass

```python
import functools
import jax, jax.numpy as jnp
from jax import lax
import numpy as np

D_MODEL = 1024
BATCH = 1
SEQ = 1024
DEPTH = 1
DEC_BATCH = 8
DEC_SEQ = 1
PAST_LEN = 1024
PAGE_SIZE = 128

RET_HEADS = 4
RET_DK = 128
RET_DV = 128
RET_CHUNK = 128
SWA_HEADS = 8
SWA_KV_HEADS = 2
SWA_HD = 64
SWA_GROUP = SWA_HEADS // SWA_KV_HEADS
WINDOW = 128
SWA_BLOCK = WINDOW
ROPE_THETA = 10000.0
N_GROUPS = 4
EXPERTS_PER_GROUP = 8
N_EXPERTS = N_GROUPS * EXPERTS_PER_GROUP
TOP_K_INNER = 2
D_EXPERT = 256
MOE_BLOCK = 128
NORM_EPS = 1e-6
IN_SIZES = (RET_HEADS * RET_DK, RET_HEADS * RET_DK, RET_HEADS * RET_DV, RET_HEADS * RET_DV, SWA_HEADS * SWA_HD, SWA_KV_HEADS * SWA_HD, SWA_KV_HEADS * SWA_HD, D_MODEL, D_MODEL)
N_IN = sum(IN_SIZES)

kernel_name = 'hybrid_retention_swa_hmoe_step'

def _rmsnorm(x, g):
    xf = x.astype(jnp.float32)
    y = xf * lax.rsqrt(jnp.mean(xf * xf, axis=-1, keepdims=True) + NORM_EPS)
    return (y * g.astype(jnp.float32)).astype(x.dtype)

def _rope(x, pos):
    d = x.shape[-1]
    inv = ROPE_THETA ** (-jnp.arange(0, d, 2, dtype=jnp.float32) / d)
    ang = pos.astype(jnp.float32)[:, None] * inv[None, :]
    cos = jnp.cos(ang)[None, :, None, :]
    sin = jnp.sin(ang)[None, :, None, :]
    xf = x.astype(jnp.float32)
    x1, x2 = xf[..., : d // 2], xf[..., d // 2:]
    return jnp.concatenate([x1 * cos - x2 * sin, x2 * cos + x1 * sin], axis=-1).astype(x.dtype)

def _retnet_rotate(x, pos):
    d = x.shape[-1]
    inv = 1.0 / (ROPE_THETA ** jnp.linspace(0.0, 1.0, d // 2, dtype=jnp.float32))
    ang = pos.astype(jnp.float32)[:, None] * inv[None, :]
    cos = jnp.cos(ang)[None, :, None, :]
    sin = jnp.sin(ang)[None, :, None, :]
    xf = x.astype(jnp.float32).reshape(x.shape[:-1] + (d // 2, 2))
    x1, x2 = xf[..., 0], xf[..., 1]
    return jnp.stack([x1 * cos - x2 * sin, x2 * cos + x1 * sin], axis=-1).reshape(x.shape).astype(x.dtype)

def _retention(q, k, v, s0, chunk):
    B, T, H, DK = q.shape
    DV = v.shape[-1]
    NC = T // chunk
    ld = jnp.log(1.0 - 2.0 ** (-5.0 - jnp.arange(H, dtype=jnp.float32)))
    qf = q.astype(jnp.float32).reshape(B, NC, chunk, H, DK)
    kf = (k.astype(jnp.float32) * DK ** -0.5).reshape(B, NC, chunk, H, DK)
    vf = v.astype(jnp.float32).reshape(B, NC, chunk, H, DV)
    idx = jnp.arange(chunk, dtype=jnp.float32)
    diff = idx[:, None] - idx[None, :]
    causal = diff >= 0
    dmask = jnp.where(causal[None], jnp.exp(ld[:, None, None] * jnp.where(causal, diff, 0.0)[None]), 0.0)
    att = jnp.einsum('bnihd,bnjhd->bnhij', qf, kf) * dmask[None, None]
    o_intra = jnp.einsum('bnhij,bnjhe->bnihe', att, vf)
    k_dec = jnp.exp(ld[None, :] * (chunk - 1.0 - idx)[:, None])
    kv = jnp.einsum('bnjhd,bnjhe->bnhde', kf * k_dec[:, :, None], vf)
    chunk_decay = jnp.exp(ld * chunk)[None, :, None, None]

    def step(s, kv_c):
        return chunk_decay * s + kv_c, s

    s_final, s_before = lax.scan(step, s0.astype(jnp.float32), jnp.moveaxis(kv, 1, 0))
    s_before = jnp.moveaxis(s_before, 0, 1)
    q_dec = jnp.exp(ld[None, :] * (idx + 1.0)[:, None])
    o_cross = jnp.einsum('bnihd,bnhde->bnihe', qf * q_dec[:, :, None], s_before)
    return (o_intra + o_cross).reshape(B, T, H, DV), s_final

def _sink_probs(s, mask, sink):
    sk = sink.astype(jnp.float32).reshape(SWA_KV_HEADS, SWA_GROUP, 1, 1)
    s = jnp.where(mask, s, -jnp.inf)
    m = jnp.maximum(jnp.max(s, axis=-1, keepdims=True), sk)
    p = jnp.exp(s - m)
    return p / (jnp.sum(p, axis=-1, keepdims=True) + jnp.exp(sk - m))

def _swa_prompt(q, k, v, sink):
    B, T, H, hd = q.shape
    C = SWA_BLOCK
    NB = T // C
    qb = q.reshape(B, NB, C, SWA_KV_HEADS, SWA_GROUP, hd)
    kb = k.reshape(B, NB, C, SWA_KV_HEADS, hd)
    vb = v.reshape(B, NB, C, SWA_KV_HEADS, hd)

    def with_prev(a):
        prev = jnp.concatenate([jnp.zeros_like(a[:, :1]), a[:, :-1]], axis=1)
        return jnp.concatenate([prev, a], axis=2)

    kk, vv = with_prev(kb), with_prev(vb)
    s = jnp.einsum('bnqkgd,bnskd->bnkgqs', qb, kk).astype(jnp.float32) * hd ** -0.5
    blk = jnp.arange(NB)[:, None] * C
    qpos = blk + jnp.arange(C)[None, :]
    kpos = blk - C + jnp.arange(2 * C)[None, :]
    dist = qpos[:, :, None] - kpos[:, None, :]
    mask = (dist >= 0) & (dist < WINDOW) & (kpos[:, None, :] >= 0)
    p = _sink_probs(s, mask[None, :, None, None], sink)
    o = jnp.einsum('bnkgqs,bnskd->bnqkgd', p.astype(vv.dtype), vv).reshape(B, T, H * hd)
    W = min(WINDOW, T)
    return o, k[:, T - W:], v[:, T - W:]

def _swa_sample(q, k, v, k_buf, v_buf, sink):
    DB, L, H, hd = q.shape
    W = k_buf.shape[1]
    kk = jnp.concatenate([k_buf.astype(k.dtype), k], axis=1)
    vv = jnp.concatenate([v_buf.astype(v.dtype), v], axis=1)
    qb = q.reshape(DB, L, SWA_KV_HEADS, SWA_GROUP, hd)
    s = jnp.einsum('bqkgd,bskd->bkgqs', qb, kk).astype(jnp.float32) * hd ** -0.5
    qpos = PAST_LEN + jnp.arange(L)
    kpos = PAST_LEN - W + jnp.arange(W + L)
    dist = qpos[:, None] - kpos[None, :]
    mask = (dist >= 0) & (dist < WINDOW)
    p = _sink_probs(s, mask, sink)
    o = jnp.einsum('bkgqs,bskd->bqkgd', p.astype(vv.dtype), vv).reshape(DB, L, H * hd)
    return o, kk[:, L:], vv[:, L:]

def _moe(h, w_rg, b_rg, w_re, b_re, w1, w3, w2):
    hf = h.astype(jnp.float32)
    g_logits = hf @ w_rg.astype(jnp.float32) + b_rg.astype(jnp.float32)
    g_sel = jnp.argmax(g_logits, axis=-1)
    p_group = jnp.max(jax.nn.softmax(g_logits, axis=-1), axis=-1, keepdims=True)
    e_logits = (hf @ w_re.astype(jnp.float32) + b_re.astype(jnp.float32)).reshape(-1, N_GROUPS, EXPERTS_PER_GROUP)
    e_in = jnp.einsum('tge,tg->te', e_logits, jax.nn.one_hot(g_sel, N_GROUPS, dtype=jnp.float32))
    top_v, top_i = lax.top_k(e_in, TOP_K_INNER)
    w_sel = jax.nn.softmax(top_v, axis=-1) * p_group
    e_id = g_sel[:, None] * EXPERTS_PER_GROUP + top_i
    comb = jnp.sum(jax.nn.one_hot(e_id, N_EXPERTS, dtype=jnp.float32) * w_sel[..., None], axis=1)
    a = jnp.einsum('td,edf->tef', h, w1)
    b = jnp.einsum('td,edf->tef', h, w3)
    hid = jax.nn.silu(a) * b * comb.astype(h.dtype)[:, :, None]
    return jnp.einsum('tef,efd->td', hid, w2)

def _apply_moe(h, blocked, w_rg, b_rg, w_re, b_re, w1, w3, w2):
    B, T, D = h.shape
    flat = h.reshape(-1, D)
    fn = functools.partial(_moe, w_rg=w_rg, b_rg=b_rg, w_re=w_re, b_re=b_re, w1=w1, w3=w3, w2=w2)
    if blocked:
        out = lax.map(fn, flat.reshape(-1, MOE_BLOCK, D))
    else:
        out = fn(flat)
    return out.reshape(B, T, D)

def _split_in(z):
    parts, start = [], 0
    for size in IN_SIZES:
        parts.append(z[..., start:start + size])
        start += size
    return parts

def _layer(x, c, pos, ret_s0, ret_chunk, swa_core, moe_blocked, w_ada, b_ada, n1, n2, w_in, w_up_ret, w_up_swa, w_o, w_rg, b_rg, w_re, b_re, w1, w3, w2):
    B, T, _ = x.shape
    mod = jax.nn.silu(c) @ w_ada + b_ada
    sh1, sc1, g1, sh2, sc2, g2 = [m[:, None, :] for m in jnp.split(mod, 6, axis=-1)]
    h = _rmsnorm(x, n1) * (1 + sc1) + sh1
    rq, rk, rv, rg, sq, sk, sv, za, zb = _split_in(h @ w_in)
    rq = _retnet_rotate(rq.reshape(B, T, RET_HEADS, RET_DK), pos)
    rk = _retnet_rotate(rk.reshape(B, T, RET_HEADS, RET_DK), pos)
    rv = rv.reshape(B, T, RET_HEADS, RET_DV)
    o_ret, ret_state = _retention(rq, rk, rv, ret_s0, ret_chunk)
    o_ret = o_ret * lax.rsqrt(jnp.mean(o_ret * o_ret, axis=-1, keepdims=True) + NORM_EPS)
    y_ret = (o_ret.reshape(B, T, -1).astype(x.dtype) * jax.nn.silu(rg)) @ w_up_ret
    sq = _rope(sq.reshape(B, T, SWA_HEADS, SWA_HD), pos)
    sk = _rope(sk.reshape(B, T, SWA_KV_HEADS, SWA_HD), pos)
    sv = sv.reshape(B, T, SWA_KV_HEADS, SWA_HD)
    o_swa, k_buf, v_buf = swa_core(sq, sk, sv)
    y_swa = o_swa @ w_up_swa
    merged = jax.nn.sigmoid(za) * y_ret + jax.nn.sigmoid(zb) * y_swa
    x = x + g1 * (merged @ w_o)
    h2 = _rmsnorm(x, n2) * (1 + sc2) + sh2
    x = x + g2 * _apply_moe(h2, moe_blocked, w_rg, b_rg, w_re, b_re, w1, w3, w2)
    return x, ret_state, k_buf, v_buf

def setup_inputs(seed: int = 0) -> dict:
    key = jax.random.key(seed)
    ks = jax.random.split(key, 24)
    f32 = jnp.float32
    D = D_MODEL
    W = min(WINDOW, PAST_LEN)

    def nrm(k, shape, scale):
        return jax.random.normal(k, shape, f32) * scale

    return {
        'x_prompt': nrm(ks[0], (BATCH, SEQ, D), 1.0),
        'x_sample': nrm(ks[1], (DEC_BATCH, DEC_SEQ, D), 1.0),
        'c_prompt': nrm(ks[2], (BATCH, D), 1.0),
        'c_sample': nrm(ks[3], (DEC_BATCH, D), 1.0),
        'state_ret': nrm(ks[4], (DEPTH, DEC_BATCH, RET_HEADS, RET_DK, RET_DV), 0.1),
        'cache_swa_k': nrm(ks[5], (DEPTH, DEC_BATCH, W, SWA_KV_HEADS, SWA_HD), 1.0),
        'cache_swa_v': nrm(ks[6], (DEPTH, DEC_BATCH, W, SWA_KV_HEADS, SWA_HD), 1.0),
        'w_ada': nrm(ks[7], (DEPTH, D, 6 * D), 0.2 * D ** -0.5),
        'b_ada': nrm(ks[8], (DEPTH, 6 * D), 0.02),
        'norm1_g': 1.0 + nrm(ks[9], (DEPTH, D), 0.02),
        'norm2_g': 1.0 + nrm(ks[10], (DEPTH, D), 0.02),
        'w_in': nrm(ks[11], (DEPTH, D, N_IN), D ** -0.5),
        'w_up_ret': nrm(ks[12], (DEPTH, RET_HEADS * RET_DV, D), (RET_HEADS * RET_DV) ** -0.5),
        'w_up_swa': nrm(ks[13], (DEPTH, SWA_HEADS * SWA_HD, D), (SWA_HEADS * SWA_HD) ** -0.5),
        'w_o': nrm(ks[14], (DEPTH, D, D), D ** -0.5),
        'sink': nrm(ks[15], (DEPTH, SWA_HEADS), 0.5),
        'w_rg': nrm(ks[16], (DEPTH, D, N_GROUPS), D ** -0.5),
        'b_rg': nrm(ks[17], (DEPTH, N_GROUPS), 0.01),
        'w_re': nrm(ks[18], (DEPTH, D, N_EXPERTS), D ** -0.5),
        'b_re': nrm(ks[19], (DEPTH, N_EXPERTS), 0.01),
        'w1': nrm(ks[20], (DEPTH, N_EXPERTS, D, D_EXPERT), D ** -0.5),
        'w3': nrm(ks[21], (DEPTH, N_EXPERTS, D, D_EXPERT), D ** -0.5),
        'w2': nrm(ks[22], (DEPTH, N_EXPERTS, D_EXPERT, D), D_EXPERT ** -0.5),
        'final_g': 1.0 + nrm(ks[23], (D,), 0.02),
    }

def reference(x_prompt, x_sample, c_prompt, c_sample, state_ret, cache_swa_k, cache_swa_v, w_ada, b_ada, norm1_g, norm2_g, w_in, w_up_ret, w_up_swa, w_o, sink, w_rg, b_rg, w_re, b_re, w1, w3, w2, final_g):
    B, T, _ = x_prompt.shape
    DB, L, _ = x_sample.shape
    pos_p = jnp.arange(T, dtype=jnp.int32)
    pos_s = PAST_LEN + jnp.arange(L, dtype=jnp.int32)
    xp, xs = x_prompt, x_sample
    sp_list, ss_list, kp_list, vp_list, ks_list, vs_list = [], [], [], [], [], []
    for l in range(DEPTH):
        shared = (w_ada[l], b_ada[l], norm1_g[l], norm2_g[l], w_in[l], w_up_ret[l], w_up_swa[l], w_o[l], w_rg[l], b_rg[l], w_re[l], b_re[l], w1[l], w3[l], w2[l])
        s0 = jnp.zeros((B, RET_HEADS, RET_DK, RET_DV), jnp.float32)
        core_p = functools.partial(_swa_prompt, sink=sink[l])
        xp, st_p, kb_p, vb_p = _layer(xp, c_prompt, pos_p, s0, min(RET_CHUNK, T), core_p, True, *shared)
        core_s = functools.partial(_swa_sample, k_buf=cache_swa_k[l], v_buf=cache_swa_v[l], sink=sink[l])
        xs, st_s, kb_s, vb_s = _layer(xs, c_sample, pos_s, state_ret[l], L, core_s, False, *shared)
        sp_list.append(st_p)
        ss_list.append(st_s)
        kp_list.append(kb_p)
        vp_list.append(vb_p)
        ks_list.append(kb_s)
        vs_list.append(vb_s)
    y_prompt = _rmsnorm(xp, final_g)
    y_sample = _rmsnorm(xs, final_g)
    return (y_prompt, y_sample, jnp.stack(sp_list), jnp.stack(ss_list), jnp.stack(kp_list), jnp.stack(vp_list), jnp.stack(ks_list), jnp.stack(vs_list))


_drawn_inputs = setup_inputs


def setup_inputs(seed=0):
    import zlib

    import numpy as np

    out = dict(_drawn_inputs(seed))
    spreads = {}
    factors = {'norm2_g': 8.0, 'w_up_swa': 3.769, 'sink': 8.0, 'b_rg': 8.0, 'b_re': 8.0, 'final_g': 2.906}
    for name, (base, spread) in spreads.items():
        noise = np.random.default_rng([zlib.crc32(name.encode()), seed]).standard_normal(out[name].shape)
        drawn = base * np.exp(spread * noise) if base else spread * noise
        out[name] = __import__('jax').numpy.asarray(drawn.astype(out[name].dtype))
    for name, factor in factors.items():
        out[name] = (out[name] * factor).astype(out[name].dtype)
    return out
```

```python
from contextlib import ExitStack

import numpy as np

import concourse.bass as bass
from concourse import mybir

F32 = mybir.dt.float32
U32 = mybir.dt.uint32
ALU = mybir.AluOpType
ACT = mybir.ActivationFunctionType
AX = mybir.AxisListType

P = 128
D = 1024
KD = D // P
T = 1024
NT = T // P
NS = 8
TA = T + NS
H = 4
HD = 64
NE = 32
NG = 4
EPG = NE // NG
DE = 256
CAP = 96
CHUNK = TA // 3
NOVER = (2 * TA) // CAP
NBLK = NE + NOVER
ZR = 16
MAXOV = (TA - 1) // CAP
EPS = 1e-6
NEG = -1e30
RSC = 128.0 ** -0.5
ASC = HD ** -0.5
WE = 3 * D * DE // P
ADA = 6 * D // 512
NL = NG + NE
GAMMA = [1.0 - 2.0 ** (-5.0 - h) for h in range(H)]

COLS, _n = {}, 0
for _name, _w in (("ident", P), ("dmask", H * P), ("qdec", H * P), ("band", 2 * P), ("tri", P), ("ones", P),
                  ("kdec", H), ("half", 36), ("ec", NE), ("iota", 8), ("thr", MAXOV), ("valid", NT + 1),
                  ("blk", NOVER), ("eye8", 64), ("grp", 2), ("inv_d", 1), ("eps", 1)):
    COLS[_name] = (_n, _n + _w)
    _n += _w
NC = _n


def build(nc, A, O):
    with ExitStack() as ctx:
        def sb(name, cols, dt=F32, rows=P):
            return ctx.enter_context(nc.sbuf_tensor(name, [rows, cols], dt))

        h2_dram = nc.dram_tensor("h2_dram", [TA, D], F32, kind="Internal").ap()
        y_dram = nc.dram_tensor("y_dram", [NBLK * CAP, D], F32, kind="Internal").ap()
        mod_dram = nc.dram_tensor("mod_dram", [9, 6 * D], F32, kind="Internal").ap()
        slot_dram = nc.dram_tensor("slot_dram", [NBLK * CAP, 1], U32, kind="Internal").ap()

        R0 = sb("R0", KD * TA)
        R1 = sb("R1", 2304 * KD)
        R2 = sb("R2", 9 * 512 + 2 * H * TA)
        R3 = sb("R3", 3 * D)
        R4 = sb("R4", 4 * D)
        const = sb("const", NC)
        work = sb("work", 3072)
        small = sb("small", 64)
        cT = sb("cT", KD * 9)
        K2 = sb("K2", 2 * P)
        V2 = sb("V2", 2 * P)
        krot = sb("krot", P)
        band = sb("band", 2 * P)
        sinkr = sb("sinkr", 2 * H)
        sinkc = sb("sinkc", 1, F32, NS)
        brow = sb("brow", NL)
        rwt = sb("rwt", KD * NL)
        slotT = sb("slotT", NBLK, U32, CAP)
        posu = sb("posu", 2 * (NT + 1), U32)
        tok = sb("tok", NT + 1, U32)
        idxc = sb("idxc", 2, U32)
        wsel = sb("wsel", 2 * (NT + 1))
        nover = sb("nover", NOVER + 1, U32, 1)

        def cst(name, rows=P):
            a, b = COLS[name]
            return const[0:rows, a:b]

        ident = cst("ident")
        mod = R0[0:9, 0:6 * D]
        wada = R2[:, 0:8192].rearrange("p (s k c) -> p s k c", s=2, k=KD)
        bst = work[0:9, 0:1024].rearrange("p (s c) -> p s c", s=2)
        crow = R4[0:9, 0:D]
        csig = R4[0:9, D:2 * D]
        hT = R0[:, :].rearrange("p (k t) -> p k t", k=KD)
        wqh = R1[:, 0:H * 4096].rearrange("p (h k c) -> p h k c", h=H, k=KD)
        wkv = R1[:, H * 4096:].rearrange("p (k c) -> p k c", k=KD)
        o_all = R2[:, 0:9 * 512].rearrange("p (t c) -> p t c", t=9)
        oswT = R2[:, 4608:4608 + H * TA].rearrange("p (h t) -> p h t", h=H)
        oretT = R2[:, 4608 + H * TA:].rearrange("p (h t) -> p h t", h=H)
        yzero = R2[0:NOVER * CAP // ZR, 4608 + H * TA:4608 + H * TA + D]
        A1, B1, NGR = R3[:, 0:D], R3[:, D:2 * D], R3[:, 2 * D:3 * D]
        xt, hrow = R4[:, 0:D], R4[:, D:2 * D]
        hst = R4[:, 2 * D:3 * D].rearrange("p (k t) -> p k t", k=KD)
        rope = R4[:, 3 * D:3 * D + 384]
        S = R4[:, 3 * D + 384:3 * D + 896].rearrange("p (h e) -> p h e", h=H)
        t1, t2, rot = work[:, 0:384], work[:, 384:768], work[:, 768:1152]
        qkT, qdT, attT = work[:, 1152:1536], work[:, 1536:1664], work[:, 1664:1792]
        vb, kd = work[:, 1792:1920], work[:, 1920:2048]
        pr = work[:, 2048:2560].rearrange("p (g s) -> p g s", g=2)
        prT = work[:, 2560:3072].rearrange("p (g b t) -> p g b t", g=2, b=2)
        mneg, mx, es, den, den2, rden, m2 = (small[:, 2 * j:2 * j + 2] for j in range(7))
        ms, msb, rstd = small[:, 14:15], small[:, 15:16], small[:, 16:17]
        rots = R4[0:NS, 0:4 * 384].rearrange("p (h c) -> p h c", h=H)
        vs = R4[0:NS, 1536:2048].rearrange("p (h c) -> p h c", h=H)
        qsT = work[:, 0:64]
        qM = work[:, 64:320].rearrange("p (h b c) -> p h b c", h=H, b=NS)
        qB = work[:, 320:384].rearrange("p (b h g) -> p b h g", b=NS, h=H)
        pTs = work[:, 384:448].rearrange("p (b c) -> p b c", b=NS)
        qk8 = work[0:NS, 448:452]
        tmp8 = work[0:NS, 512:640]
        junk8 = work[0:NS, 640:768]
        ks8 = work[0:NS, 768:1280].rearrange("p (h c) -> p h c", h=H)
        pS = work[0:NS, 2048:3072].rearrange("p (b s) -> p b s", b=NS)
        mx8, m8, es8, den8, rd8 = (work[0:NS, 1280 + 8 * j:1288 + 8 * j] for j in range(5))
        st = R2[:, 4608 + H * TA:4608 + H * TA + 4096].rearrange("p (h b e) -> p h b e", h=H, b=NS)
        vM = R1[0:NS, 4096:8192].rearrange("p (h b e) -> p h b e", h=H, b=NS)
        kwin = R1[:, 14400:15424].rearrange("p (b c) -> p b c", b=NS)
        vwin = R1[:, 15424:16448].rearrange("p (b c) -> p b c", b=NS)
        kwT = R1[:, 16448:17472].rearrange("p (b c) -> p b c", b=NS)
        wrg = R1[:, 0:4096].rearrange("p (k c) -> p k c", k=KD)
        sg = work[:, 0:1376].rearrange("p (s c) -> p s c", s=4)
        osq, osq8 = R4[:, :], work[:, 1536:2048]
        oms = work[:, 2048:2084]
        omb = work[:, 2084:2120]
        orstd = work[:, 2120:2156]
        onrm = R4[:, 0:1024].rearrange("p (s h c) -> p s h c", s=2, h=H)
        mT = R1[:, 0:KD * TA].rearrange("p (m t) -> p m t", m=KD)
        wl = R1[:, 8256:14400].rearrange("p (s k c) -> p s k c", s=2, k=24)
        g2b = work[:, 0:2752].rearrange("p (q s c) -> p q s c", q=2, s=4)
        wo = R0[:, 0:8192].rearrange("p (k c) -> p k c", k=KD)
        x1 = R2[:, 0:9 * D].rearrange("p (t c) -> p t c", t=9)
        G1, A2, B2 = A1, B1, NGR
        n2row, ojunk = R1[:, 14400:15424], work[:, D:2 * D]
        h2T = R4[:, 3 * D:4 * D].rearrange("p (k t) -> p k t", k=KD)
        lg = work[:, 2048:2048 + 9 * NL].rearrange("p (t e) -> p t e", t=9)
        def rv(n, k, w=None):
            a = R4[:, n:n + 9 * k]
            return a.rearrange("p (t e) -> p t e", t=9)
        gsh, eq4, cnd4, oh4 = rv(0, 4), rv(36, 4), rv(72, 4), rv(108, 4)
        gmx, gix, gsum, pgr = rv(144, 1), rv(153, 1), rv(162, 1), rv(171, 1)
        ep = R4[:, 180:180 + 288].rearrange("p (t g j) -> p t g j", t=9, g=NG)
        ein, e2, eqv, cnd, oh1, oh2 = rv(468, 8), rv(540, 8), rv(612, 8), rv(684, 8), rv(756, 8), rv(828, 8)
        v1, i1, v2_, i2, dv = rv(900, 1), rv(909, 1), rv(918, 1), rv(927, 1), rv(936, 1)
        mk1, mk2, mk, pos = rv(960, 32), rv(1248, 32), rv(1536, 32), rv(1824, 32)
        pre, ge, adj = rv(2112, 32), rv(2400, 32), rv(2688, 32)
        cnt, nbx, obx, obc = (R4[:, 2976 + 32 * j:3008 + 32 * j] for j in range(4))
        pf = R4[:, 3104:3122].rearrange("p (t j) -> p t j", t=9)
        emap = R4[0:1, 3136:3136 + NOVER + 1]
        thr_t = R0[:, 0:NE * MAXOV].rearrange("p (e j) -> p e j", e=NE)
        cum_t = R0[:, 512:512 + 1024].rearrange("p (e f) -> p e f", e=NE)
        cumc = R0[:, 1536:1536 + 1024].rearrange("p (e f) -> p e f", e=NE)
        blk_t = R0[0:1, 2560:2560 + NOVER * NE].rearrange("p (b e) -> p b e", b=NOVER)
        slotl = R0[0:NBLK, 3328:3328 + CAP].bitcast(U32)
        slotf = R0[0:NBLK, 3456:3456 + CAP]
        we = [R1[:, 6144 * j:6144 * (j + 1)] for j in range(3)]
        xg = R0[:, 4096:6144].rearrange("p (s c) -> p s c", s=2)
        xgT = R0[:, 6144:6144 + KD * CAP].rearrange("p (k t) -> p k t", k=KD)
        hid = R0[:, 6912:6912 + 2 * CAP].rearrange("p (f t) -> p f t", f=2)
        sgh = R0[:, 7104:7104 + 2 * CAP].rearrange("p (f t) -> p f t", f=2)
        yb = R0[:, 0:2048].rearrange("p (s c) -> p s c", s=2)
        G2, FG = A1, B1
        yg = R1[:, 0:4096].rearrange("p (s j c) -> p s j c", s=2, j=2)
        yo = R1[:, 4096:6144].rearrange("p (s c) -> p s c", s=2)
        cj = R1[:, 6144:7168]

        def bank(name):
            return ctx.enter_context(nc.psum_tensor(name, [P, 512], F32))

        p0, p1, p2 = bank("p0"), bank("p1"), bank("p2")
        psS = ctx.enter_context(nc.psum_tensor("psS", [P, 2, 512], F32))
        p5, p6, p7 = bank("p5"), bank("p6"), bank("p7")
        pj_bank = (p0, p1)
        rg_bank = (p0, p1, p2, p6)
        g_bank = (p7, p5)
        lift = (p0, p1, p2, psS[:, 0, :], psS[:, 1, :], p5, p6, p7)

        s = {}

        def sem(name):
            if name not in s:
                s[name] = ctx.enter_context(nc.semaphore(name))
            return s[name]

        class Chain:

            def __init__(self, eng, name):
                self.eng, self.sm, self.base, self.n = eng, sem(name), 0, 0

            def __call__(self, ins):
                self.n += 1
                ins.then_inc(self.sm, 1)
                self.wait()

            def mark(self, ins):
                self.n += 1
                ins.then_inc(self.sm, 1)

            def wait(self):
                self.eng.wait_ge(self.sm, self.base + self.n)

            def loop(self, i, per):
                self.base, self.start = self.n + i * per, self.n
                self.at, self.n, self.per = self.n, 0, per

            def end(self, rounds):
                assert self.n == self.per, (self.n, self.per)
                self.base, self.n = 0, self.at + rounds * self.per

        for n in ("const_in band_in misc_in crow_in c_sig c_silu cT_t cT_r ada_in0 ada_in1 ada_mm mod_r mod_st tab_in "
                  "tab_r wq_in x_in rope_in x_sq rs_r h_r hT_t hT_e hT_c kv_mm k_r v_e kT_t kT_e pj rot v_c kd_r "
                  "qk_t qk_e att_s nm_r ex_r pn_r pT_e st_u osT_t os_r win yz yz_st init cache_st stp_st "
                  "spj srot sv_c sq_t sq_e sqm sst_in socr so_r sst_r sst_st swin_c swin_n swin_st skT_t skT_e kwin oa pT_t ssc ssm sex spn spT_t "
                  "spT_e spv sosw rg_in lw_in0 lw_in1 rg_mm rg_s rg_r o_sq om_r or_r on_r g_t g_r mg_mm mg_s mg_r wo_in xr_in m_c wo_mm "
                  "x1_r x1_sq rs2_r h2_r h2_t h2_e h2_st rt_mm lg_r zero slot_z slot_w slot_in gsh_r gex_r dv_r dex_r mk_r "
                  "rk_mm ov_n pos_r slotf_r slotT_t slotT_r w13_in0 w13_in1 w2_in0 w2_in1 xg_in0 xg_in1 xgT_t xgT_e s1 s2 hs "
                  "h_a hid_r y_e y_st0 y_st1 ov_idx y_done yg_in0 yg_in1 yg_r x2_r x2_sq rs3_r yo_r out_st0 out_st1").split():
            sem(n)

        block = ctx.enter_context(nc.Block())

        def ts(t):
            return bass.ds(t * P, P)

        @block.sync
        def _(sp):
            sp.dma_start(crow, A["c"]).then_inc(s["crow_in"], 16)
            sp.dma_start(const[:, :], A["const"]).then_inc(s["const_in"], 16)

            def ada_chunk(j, slot):
                sp.dma_start(R2[:, slot * 4096:(slot + 1) * 4096], A["w_ada"][bass.ds(j, 1)].rearrange("o p c -> (o p) c")
                             ).then_inc(s[f"ada_in{slot}"], 16)
                sp.dma_start(bst[:, slot, :], A["b_ada"][bass.ds(j, 1), :].to_broadcast([9, 512])
                             ).then_inc(s[f"ada_in{slot}"], 16)

            def ada_again(j, slot):
                sp.wait_ge(s["ada_mm"], j - 1)
                sp.wait_ge(s["mod_r"], j - 1)
                ada_chunk(j, slot)

            ada_chunk(0, 0)
            ada_chunk(1, 1)
            ada_again(2, 0)
            ada_again(3, 1)
            with sp.Fori(2, ADA // 2) as j2:
                ada_again(2 * j2, 0)
                ada_again(2 * j2 + 1, 1)
            for g in range(9):
                a, b = (g * 2048, (g + 1) * 2048)
                sp.dma_start(R1[:, a:b], A["w_qkv"][:, a:b]).then_inc(s["wq_in"], 16)
            sp.wait_ge(s["yz"], 1)
            sp.dma_start(y_dram[NE * CAP:, :].rearrange("(a p) c -> p a c", a=ZR),
                         yzero.rearrange("p (o c) -> p o c", o=1).to_broadcast([NOVER * CAP // ZR, ZR, D])
                         ).then_inc(s["yz_st"], 16)
            sp.wait_ge(s["c_silu"], 1)
            sp.dma_start(xt, A["x"][0]).then_inc(s["x_in"], 16)
            sp.dma_start(rope, A["rope"][0]).then_inc(s["rope_in"], 16)
            sp.wait_ge(s["h_r"], 1)
            sp.dma_start(xt, A["x"][1]).then_inc(s["x_in"], 16)

            def mix(i, last):
                if not last:
                    sp.wait_ge(s["h_r"], i + 2)
                    sp.dma_start(xt, A["x"][bass.ds(i + 2, 1)].rearrange("o p c -> (o p) c")).then_inc(s["x_in"], 16)
                sp.wait_ge(s["rot"], 4 * i + 4)
                sp.dma_start(rope, A["rope"][bass.ds(i + 1, 1)].rearrange("o p c -> (o p) c")).then_inc(s["rope_in"], 16)

            with sp.Fori(0, NT - 1) as i:
                mix(i, False)
            mix(NT - 1, True)
            sp.wait_ge(s["st_u"], 4 * NT)
            sp.dma_start(O["st_p"], S.rearrange("p h e -> p (h e)")).then_inc(s["stp_st"], 16)
            sp.wait_ge(s["yz_st"], 16)
            sp.dma_start(R2[:, 4608 + H * TA:4608 + H * TA + 4096], A["state"]).then_inc(s["sst_in"], 16)
            sp.wait_ge(s["spj"], H)
            sp.dma_start(kwin[0:P - 1], A["ck"][1:P]).then_inc(s["swin_c"], 16)
            sp.dma_start(vwin[0:P - 1], A["cv"][1:P]).then_inc(s["swin_c"], 16)
            sp.wait_ge(s["k_r"], NT + 1)
            sp.wait_ge(s["v_e"], NT + 1)
            sp.dma_start(kwin[P - 1:P], krot[0:NS, :]).then_inc(s["swin_n"], 16)
            sp.dma_start(vwin[P - 1:P], V2[0:NS, P:2 * P]).then_inc(s["swin_n"], 16)
            sp.wait_ge(s["swin_c"], 32)
            sp.wait_ge(s["swin_n"], 32)
            sp.dma_start(O["ks"], kwin).then_inc(s["swin_st"], 16)
            sp.dma_start(O["vs"], vwin).then_inc(s["swin_st"], 16)
            sp.dma_start(R1[:, 0:4096], A["w_rg_gate"]).then_inc(s["rg_in"], 16)

            def lift_in(m, slot):
                sp.dma_start(R1[:, 8256 + 3072 * slot:8256 + 3072 * (slot + 1)],
                             A["lift"][bass.ds(m, 1)].rearrange("o p c -> (o p) c")).then_inc(s[f"lw_in{slot}"], 16)

            lift_in(0, 0)
            lift_in(1, 1)
            sp.wait_ge(s["sst_r"], H)
            sp.dma_start(O["st_s"], R2[:, 4608 + H * TA:4608 + H * TA + 4096]).then_inc(s["sst_st"], 16)
            with sp.Fori(1, KD // 2) as m2_:
                for slot in range(2):
                    sp.wait_ge(s["mg_mm"], 3 * (2 * m2_ + slot - 1))
                    lift_in(2 * m2_ + slot, slot)
            sp.wait_ge(s["mg_mm"], 3 * KD)
            sp.dma_start(R0[:, 0:8192], A["w_o"]).then_inc(s["wo_in"], 16)
            sp.dma_start(xt, A["x"][0]).then_inc(s["xr_in"], 16)

            def out_rows(t, rows=P):
                sp.wait_ge(s["h2_r"], t + 1)
                sp.dma_start(h2_dram[bass.ds(t * P, rows), :], hrow[0:rows]).then_inc(s["h2_st"], 16)

            with sp.Fori(0, NT) as t:
                sp.wait_ge(s["x1_r"], t + 1)
                sp.dma_start(xt, A["x"][bass.ds(t + 1, 1)].rearrange("o p c -> (o p) c")).then_inc(s["xr_in"], 16)
                out_rows(t)
            out_rows(NT, NS)

            def weights(e, slot):
                sp.dma_start(we[slot][:, 0:4096], A["we"][bass.ds(e, 1), :, 0:4096].rearrange("o p c -> (o p) c")
                             ).then_inc(s[f"w13_in{slot}"], 16)

            def weights2(e, slot):
                sp.dma_start(we[slot][:, 4096:6144], A["we"][bass.ds(e, 1), :, 4096:6144].rearrange("o p c -> (o p) c")
                             ).then_inc(s[f"w2_in{slot}"], 16)

            sp.wait_ge(s["wo_mm"], NT + 1)
            sp.wait_ge(s["m_c"], NT + 1)
            sp.wait_ge(s["lg_r"], NT + 1)
            for slot in range(2):
                weights(slot, slot)
                weights2(slot, slot)
            sp.wait_ge(s["zero"], 1)
            sp.dma_start(slot_dram.rearrange("(b r) o -> b (r o)", r=CAP), slotl).then_inc(s["slot_z"], 16)
            sp.wait_ge(s["slot_w"], 16 * 2 * (NT + 1))
            sp.dma_start(slotl, slot_dram.rearrange("(b r) o -> b (r o)", r=CAP)).then_inc(s["slot_in"], 16)
            with sp.Fori(1, NE // 2) as b2:
                for slot in range(2):
                    sp.wait_ge(s["s1"], 2 * b2 + slot - 1)
                    weights(2 * b2 + slot, slot)
                    sp.wait_ge(s["s2"], 2 * b2 + slot - 1)
                    weights2(2 * b2 + slot, slot)
            sp.wait_ge(s["ov_n"], 1)
            n_over = sp.value_load(nover[0:1, NOVER:NOVER + 1], min_val=0, max_val=NOVER)
            with sp.Fori(0, NOVER) as b:
                with sp.If(b < n_over):
                    e = sp.value_load(nover[0:1, bass.ds(b, 1)], min_val=0, max_val=NE - 1)
                    sp.wait_ge(s["s2"], NE + b)
                    weights(e, 0)
                    weights2(e, 0)
            def rows_out(t, slot, rows=P):
                sp.wait_ge(s["yo_r"], t + 1)
                dst = O["y"][bass.ds(t * P, rows), :]
                sp.dma_start(dst, yo[0:rows, slot]).then_inc(s[f"out_st{slot}"], 16)

            with sp.Fori(0, NT // 2) as t2_:
                rows_out(2 * t2_, 0)
                rows_out(2 * t2_ + 1, 1)
            rows_out(NT, 0, NS)
            sp.wait_ge(s["out_st0"], 16 * (NT // 2 + 1))
            sp.wait_ge(s["out_st1"], 16 * (NT // 2))
            sp.wait_ge(s["cache_st"], 32)
            sp.wait_ge(s["stp_st"], 16)
            sp.wait_ge(s["swin_st"], 32)
            sp.wait_ge(s["sst_st"], 16)
            sp.wait_ge(s["h2_st"], 16 * (NT + 1))

        @block.gpsimd
        def _(pool):
            link = Chain(pool, "pool_own")
            pool.dma_start(band[:, :], A["band0"]).then_inc(s["band_in"], 16)
            pool.dma_start(sinkr[:, :], A["sinkr"]).then_inc(s["misc_in"], 16)
            pool.dma_start(sinkc[:, :], A["sinkc"]).then_inc(s["misc_in"], 16)
            pool.dma_start(tok[:, :], A["tok"]).then_inc(s["misc_in"], 16)
            pool.dma_start(rwt[:, :], A["rw"]).then_inc(s["misc_in"], 16)
            pool.dma_start(brow[:, :], A["brow"]).then_inc(s["misc_in"], 16)
            nc.gpsimd.memset(yzero, 0.0).then_inc(s["yz"], 1)
            nc.gpsimd.memset(K2[:, :], 0.0).then_inc(s["init"], 1)
            nc.gpsimd.memset(V2[:, :], 0.0).then_inc(s["init"], 1)
            nc.gpsimd.memset(S, 0.0).then_inc(s["init"], 1)
            pool.wait_ge(s["ada_mm"], ADA)
            nc.gpsimd.memset(o_all[:, NT, :], 0.0).then_inc(s["init"], 1)
            pool.wait_ge(s["const_in"], 16)

            def rstd_of(rows, done):
                link(nc.gpsimd.tensor_tensor(msb[0:rows], ms[0:rows], cst("inv_d", rows), ALU.mult))
                link(nc.gpsimd.tensor_tensor(msb[0:rows], msb[0:rows], cst("eps", rows), ALU.add))
                nc.gpsimd.tensor_tensor(rstd[0:rows], msb[0:rows], cst("half", rows)[:, 0:1], ALU.pow).then_inc(s[done], 1)

            def rs(n):
                pool.wait_ge(s["x_sq"], n)
                rstd_of(P, "rs_r")

            rs(1)
            pool.wait_ge(s["hT_e"], 2)
            nc.gpsimd.tensor_copy(hT[:, :, 0:P], hst).then_inc(s["hT_c"], 1)

            def mix(i, last):
                rs(i + 2)
                pool.wait_ge(s["hT_e"], 2 * i + 4)
                w = NS if last else P
                nc.gpsimd.tensor_copy(hT[:, :, bass.ds((i + 1) * P, w)], hst[:, :, 0:w]).then_inc(s["hT_c"], 1)

            with pool.Fori(0, NT - 1) as i:
                link.loop(i, 2)
                mix(i, False)
            link.end(NT - 1)
            mix(NT - 1, True)
            pool.wait_ge(s["om_r"], 1)
            link(nc.gpsimd.tensor_scalar(omb, oms, 1.0 / P, EPS, ALU.mult, ALU.add))
            nc.gpsimd.tensor_tensor(orstd, omb, cst("half"), ALU.pow).then_inc(s["or_r"], 1)

            def stage(t, w=P):
                if not isinstance(t, int) or t:
                    pool.wait_ge(s["wo_mm"], t)
                nc.gpsimd.tensor_copy(hst[:, :, 0:w], mT[:, :, bass.ds(t * P, w)]).then_inc(s["m_c"], 1)

            def rs2(t, rows=P):
                pool.wait_ge(s["x1_sq"], t + 1)
                rstd_of(rows, "rs2_r")

            pool.wait_ge(s["mg_r"], 3 * KD)
            stage(0)
            with pool.Fori(0, NT - 1) as t:
                link.loop(t, 2)
                stage(t + 1)
                rs2(t)
            link.end(NT - 1)
            stage(NT, NS)
            rs2(NT - 1)
            rs2(NT, NS)
            pool.wait_ge(s["wo_mm"], NT + 1)
            nc.gpsimd.memset(slotl, 0).then_inc(s["zero"], 1)
            pool.wait_ge(s["slot_z"], 16)
            pool.wait_ge(s["pos_r"], 1)
            for t in range(NT + 1):
                r = P if t < NT else NS
                for j in range(2):
                    pool.indirect_dma_start(out=slot_dram, out_offset=bass.IndirectOffsetOnAxis(
                        ap=posu[0:r, 2 * t + j:2 * t + j + 1], axis=0), in_=tok[0:r, t:t + 1], in_offset=None
                    ).then_inc(s["slot_w"], 16)

            def gather(dst, src, col, rows, done):
                pool.indirect_dma_start(out=dst, out_offset=None, in_=src,
                                        in_offset=bass.IndirectOffsetOnAxis(ap=col[0:rows], axis=0)
                                        ).then_inc(s[done], 16)

            def gather_block(b, slot):
                gather(xg[0:CAP, slot], h2_dram, slotT[:, b:b + 1], CAP, f"xg_in{slot}")

            pool.wait_ge(s["slotT_r"], 1)
            pool.wait_ge(s["h2_st"], 16 * (NT + 1))
            for b in range(NE):
                if b >= 2:
                    pool.wait_ge(s["xgT_t"], b - 1)
                gather_block(b, b % 2)
            n_over = pool.value_load(nover[0:1, NOVER:NOVER + 1], min_val=0, max_val=NOVER)
            for b in range(NOVER):
                with pool.If(n_over > b):
                    pool.wait_ge(s["s2"], NE + b)
                    gather_block(NE + b, 0)
            pool.wait_ge(s["y_done"], 1)

            def fetch(t, rows=P):
                for j in range(2):
                    gather(yg[0:rows, t % 2, j], y_dram, posu[:, 2 * t + j:2 * t + j + 1], rows, f"yg_in{t % 2}")

            def rs3(t, rows=P):
                pool.wait_ge(s["x2_sq"], t + 1)
                rstd_of(rows, "rs3_r")

            fetch(0)
            fetch(1)
            for t in range(NT + 1):
                rs3(t, P if t < NT else NS)
                if t + 2 <= NT:
                    fetch(t + 2, P if t + 2 < NT else NS)

        @block.scalar
        def _(act):
            link = Chain(act, "act_own")
            act.wait_ge(s["crow_in"], 16)
            nc.scalar.activation(csig, crow, ACT.Sigmoid).then_inc(s["c_sig"], 1)

            def table(dst, col, rows, src=None):
                if rows == P:
                    r = mod_dram[0:1, col * D:(col + 1) * D].to_broadcast([P, D])
                else:
                    r = mod_dram[1:9, col * D:(col + 1) * D]
                act.dma_start(dst[0:rows], r).then_inc(s["tab_in"], 16)

            act.wait_ge(s["mod_r"], ADA)
            act.dma_start(mod_dram, mod).then_inc(s["mod_st"], 16)
            act.wait_ge(s["mod_st"], 16)
            table(A1, 1, P)
            table(B1, 0, P)
            act.dma_start(NGR, A["n1"].to_broadcast([P, D])).then_inc(s["tab_in"], 16)

            def square(n):
                act.wait_ge(s["x_in"], 16 * n)
                if not isinstance(n, int):
                    act.wait_ge(s["hT_t"], 2 * (n - 1))
                nc.scalar.activation(hrow, xt, ACT.Square, accum_out=ms).then_inc(s["x_sq"], 1)

            def hT_out(half, n):
                act.wait_ge(s["hT_t"], 2 * n + half + 1)
                nc.scalar.copy(hst[:, 4 * half:4 * half + 4, :], (p6, p5)[half][:, :].rearrange("p (k t) -> p k t", k=4)
                               ).then_inc(s["hT_e"], 1)

            def v_out(n):
                act.wait_ge(s["k_r"], n + 1)
                nc.scalar.copy(V2[:, P:2 * P], p6[:, P:2 * P]).then_inc(s["v_e"], 1)

            act.wait_ge(s["tab_in"], 48)
            square(1)
            hT_out(0, 0)
            hT_out(1, 0)
            act.wait_ge(s["init"], 4)
            v_out(0)
            act.wait_ge(s["const_in"], 16)

            def v_kd(n, h):
                act.wait_ge(s["rot"], n + 1)
                nc.scalar.copy(vb, pj_bank[h % 2][:, 256:384]).then_inc(s["v_c"], 1)
                nc.scalar.mul(kd, rot[:, P:2 * P], cst("kdec")[:, h:h + 1]).then_inc(s["kd_r"], 1)

            def qk_out(n):
                act.wait_ge(s["qk_t"], n + 1)
                nc.scalar.copy(qkT, p2[:, 0:384]).then_inc(s["qk_e"], 1)

            def exps(n):
                act.wait_ge(s["nm_r"], n + 1)
                for g in range(2):
                    nc.scalar.activation(pr[:, g, :], pr[:, g, :], ACT.Exp, bias=mneg[:, g:g + 1], scale=ASC,
                                         accum_out=den[:, g:g + 1])
                nc.scalar.activation(es, es, ACT.Exp).then_inc(s["ex_r"], 1)

            def probs_out(n):
                act.wait_ge(s["pT_t"], n + 1)
                nc.scalar.copy(work[:, 2560:3072], p5[:, :]).then_inc(s["pT_e"], 1)

            def mix(i, first, last):
                if last:
                    act.wait_ge(s["k_r"], NT)
                    act.dma_start(O["kp"], krot[:, :]).then_inc(s["cache_st"], 16)
                    act.wait_ge(s["v_e"], NT)
                    act.dma_start(O["vp"], V2[:, P:2 * P]).then_inc(s["cache_st"], 16)
                    act.wait_ge(s["h_r"], NT)
                    table(A1, 1, NS)
                    table(B1, 0, NS)
                for h in range(1, H):
                    n = 4 * i + h
                    v_kd(n - 1, h - 1)
                    if h == 1:
                        act.wait_ge(s["kT_t"], i + 1)
                        if not first:
                            act.wait_ge(s["kwin"], i)
                        nc.scalar.copy(K2[:, P:2 * P], p6[:, 256:384]).then_inc(s["kT_e"], 1)
                    qk_out(n - 1)
                    if h == 1:
                        square(i + 2)
                    else:
                        probs_out(n - 2)
                    if h == 3:
                        act.wait_ge(s["hT_c"], i + 1)
                        hT_out(0, i + 1)
                        hT_out(1, i + 1)
                    exps(n - 1)
                n = 4 * i + 3
                v_kd(n, 3)
                qk_out(n)
                probs_out(n - 1)
                exps(n)
                probs_out(n)
                act.wait_ge(s["win"], i + 1)
                if last:
                    act.wait_ge(s["cache_st"], 32)
                v_out(i + 1)

            mix(0, True, False)
            with act.Fori(1, NT - 1) as i:
                mix(i, False, False)
            mix(NT - 1, False, True)
            for h in range(H):
                act.wait_ge(s["srot"], h + 1)
                nc.scalar.copy(vs[:, h, :], pj_bank[h % 2][0:NS, 256:384]).then_inc(s["sv_c"], 1)
            act.wait_ge(s["sq_t"], 1)
            nc.scalar.copy(qsT, p2[:, 0:64]).then_inc(s["sq_e"], 1)
            act.wait_ge(s["skT_t"], 1)
            nc.scalar.copy(kwT[:, 0:4], psS[:, 0, :].rearrange("p (b c) -> p b c", b=4)).then_inc(s["skT_e"], 1)
            nc.scalar.copy(kwT[:, 4:8], psS[:, 1, :].rearrange("p (b c) -> p b c", b=4)).then_inc(s["skT_e"], 1)
            act.wait_ge(s["ssm"], 1)
            nc.scalar.activation(pS, pS, ACT.Exp)
            nc.scalar.activation(es8, es8, ACT.Exp).then_inc(s["sex"], 1)
            act.wait_ge(s["spT_t"], 1)
            nc.scalar.copy(work[:, 384:448], p5[:, 0:64]).then_inc(s["spT_e"], 1)
            def rg(c):
                for m in range(H):
                    act.wait_ge(s["rg_mm"], 4 * c + m + 1)
                    nc.scalar.activation(sg[:, m, :], rg_bank[m][:, 0:CHUNK], ACT.Sigmoid).then_inc(s["rg_s"], 1)

            with act.Fori(0, 3) as c:
                rg(c)
            act.wait_ge(s["so_r"], H)
            act.wait_ge(s["os_r"], 4 * NT)
            act.wait_ge(s["stp_st"], 16)
            nc.scalar.activation(osq, R2[:, 0:4096], ACT.Square).then_inc(s["o_sq"], 1)
            nc.scalar.activation(osq8, R2[:, 4096:4608], ACT.Square).then_inc(s["o_sq"], 1)
            act.wait_ge(s["h_r"], NT + 1)
            table(G1, 2, P)
            table(A2, 4, P)
            table(B2, 3, P)
            act.wait_ge(s["swin_st"], 32)
            act.dma_start(n2row, A["n2"].to_broadcast([P, D])).then_inc(s["tab_in"], 16)

            def merge(m, slot):
                for c in range(3):
                    g = 3 * m + c
                    q = (3 * slot + c) % 2
                    bz = lift[4 * q:]
                    act.wait_ge(s["mg_mm"], g + 1)
                    for j in range(2):
                        nc.scalar.activation(g2b[:, q, j, :], bz[j][:, 0:CHUNK], ACT.Sigmoid).then_inc(s["mg_s"], 1)

            with act.Fori(0, KD // 2) as m2_:
                merge(2 * m2_, 0)
                merge(2 * m2_ + 1, 1)

            def h2T_out(t, w=P):
                act.wait_ge(s["h2_t"], t + 1)
                for j, b in enumerate((p5, p6)):
                    nc.scalar.copy(h2T[:, 4 * j:4 * j + 4, 0:w], b[:, :].rearrange("p (k t) -> p k t", k=4)[:, :, 0:w]
                                   ).then_inc(s["h2_e"], 1)

            def square2(t, rows=P, first=False):
                act.wait_ge(s["x1_r"], t + 1)
                if not first:
                    act.wait_ge(s["rs2_r"], t)
                nc.scalar.activation(ojunk[0:rows], x1[0:rows, bass.ds(t, 1), :], ACT.Square, accum_out=ms[0:rows]
                                     ).then_inc(s["x1_sq"], 1)

            square2(0, first=True)
            with act.Fori(1, NT) as t:
                h2T_out(t - 1)
                square2(t)
            act.wait_ge(s["h2_r"], NT)
            table(G1, 2, NS)
            table(A2, 4, NS)
            table(B2, 3, NS)
            h2T_out(NT - 1)
            square2(NT, NS)
            h2T_out(NT, NS)
            act.wait_ge(s["gsh_r"], 1)
            nc.scalar.activation(gsh, gsh, ACT.Exp).then_inc(s["gex_r"], 1)
            act.wait_ge(s["dv_r"], 1)
            nc.scalar.activation(dv, dv, ACT.Exp).then_inc(s["dex_r"], 1)
            act.wait_ge(s["h2_r"], NT + 1)
            table(G2, 5, P)
            act.dma_start(FG, A["fg"].to_broadcast([P, D])).then_inc(s["tab_in"], 16)

            def expert(b, slot, st):
                act.wait_ge(s["s1"], b + 1)
                nc.scalar.activation(sgh, pj_bank[slot][:, 0:2 * CAP].rearrange("p (f t) -> p f t", f=2), ACT.Sigmoid
                                     ).then_inc(s["hs"], 1)
                act.wait_ge(s["s2"], b + 1)
                if st is not None:
                    act.wait_ge(s[f"y_st{slot}"], st)
                nc.scalar.copy(yb[0:CAP, slot].rearrange("p (a c) -> p a c", a=2), psS[0:CAP, :, :]).then_inc(s["y_e"], 1)
                act.wait_ge(s["y_e"], b + 1)
                act.dma_start(y_dram[bass.ds(b * CAP, CAP), :], yb[0:CAP, slot]).then_inc(s[f"y_st{slot}"], 16)

            expert(0, 0, None)
            expert(1, 1, None)
            with act.Fori(1, NE // 2) as b2:
                expert(2 * b2, 0, 16 * b2)
                expert(2 * b2 + 1, 1, 16 * b2)
            n_over = act.value_load(nover[0:1, NOVER:NOVER + 1], min_val=0, max_val=NOVER)
            with act.Fori(0, NOVER) as b:
                with act.If(b < n_over):
                    expert(NE + b, 0, 8 * NE + 16 * b)
            act.wait_ge(s["y_st1"], 8 * NE)
            act.wait_ge(s["y_st0"], n_over * 16 + 8 * NE)
            nc.scalar.copy(small[:, 20:21], small[:, 16:17]).then_inc(s["y_done"], 1)
            def square3(t, rows=P, first=False):
                act.wait_ge(s["x2_r"], t + 1)
                if not first:
                    act.wait_ge(s["rs3_r"], t)
                nc.scalar.activation(cj[0:rows], x1[0:rows, bass.ds(t, 1), :], ACT.Square, accum_out=ms[0:rows]
                                     ).then_inc(s["x2_sq"], 1)

            square3(0, first=True)
            with act.Fori(1, NT) as t:
                square3(t)
            act.wait_ge(s["x2_r"], NT)
            table(G2, 5, NS)
            square3(NT, NS)

        @block.vector
        def _(dve):
            link = Chain(dve, "dve_own")
            dve.wait_ge(s["c_sig"], 1)
            nc.vector.tensor_tensor(csig, crow, csig, ALU.mult).then_inc(s["c_silu"], 1)
            dve.wait_ge(s["cT_t"], 1)
            nc.vector.tensor_copy(cT[:, :], p2[:, 0:72]).then_inc(s["cT_r"], 1)

            def ada(j, slot):
                dve.wait_ge(s["ada_mm"], j + 1)
                nc.vector.tensor_tensor(mod[:, bass.ds(j * 512, 512)], pj_bank[slot][0:9, :], bst[:, slot, :],
                                        ALU.add).then_inc(s["mod_r"], 1)

            with dve.Fori(0, ADA // 2) as j2:
                ada(2 * j2, 0)
                ada(2 * j2 + 1, 1)
            dve.wait_ge(s["tab_in"], 48)
            nc.vector.scalar_tensor_tensor(A1, A1, 1.0, NGR, ALU.add, ALU.mult).then_inc(s["tab_r"], 1)
            dve.wait_ge(s["tab_r"], 1)

            def h_scale(n):
                dve.wait_ge(s["rs_r"], n)
                link(nc.vector.scalar_tensor_tensor(hrow, xt, rstd, A1, ALU.mult, ALU.mult))

            def h_shift():
                nc.vector.tensor_tensor(hrow, hrow, B1, ALU.add).then_inc(s["h_r"], 1)

            def rotate(src, cols, kind, out, rows=P):
                a, b = cols
                n = (b - a) // (P if kind == "ret" else HD)
                w = P if kind == "ret" else HD
                c0 = 0 if kind == "ret" else 256
                cos = rope[0:rows, c0:c0 + w].rearrange("p (o c) -> p o c", o=1).to_broadcast([rows, n, w])
                x = src.rearrange("p (n c) -> p n c", n=n)
                link.mark(nc.vector.tensor_tensor(t1[0:rows, out:out + b - a].rearrange("p (n c) -> p n c", n=n), x, cos,
                                             ALU.mult))
                sin = rope[0:rows, c0 + w:c0 + 2 * w]
                if kind == "ret":
                    x4 = src.rearrange("p (n j t) -> p n j t", n=n, t=2)
                    o4 = t2[0:rows, out:out + b - a].rearrange("p (n j t) -> p n j t", n=n, t=2)
                    s4 = sin.rearrange("p (o j t) -> p o j t", o=1, t=2)
                    for e in range(2):
                        link.mark(nc.vector.tensor_tensor(o4[:, :, :, e], x4[:, :, :, 1 - e],
                                                     s4[:, :, :, e].to_broadcast([rows, n, HD]), ALU.mult))
                else:
                    x4 = src.rearrange("p (n t j) -> p n t j", n=n, t=2)
                    o4 = t2[0:rows, out:out + b - a].rearrange("p (n t j) -> p n t j", n=n, t=2)
                    s4 = sin.rearrange("p (o t j) -> p o t j", o=1, t=2)
                    for e in range(2):
                        link.mark(nc.vector.tensor_tensor(o4[:, :, e, :], x4[:, :, 1 - e, :],
                                                     s4[:, :, e, :].to_broadcast([rows, n, 32]), ALU.mult))

            def keys(n, last=False):
                dve.wait_ge(s["kv_mm"], n + 1)
                dve.wait_ge(s["rope_in"], 16 * (n + 1))
                rotate(p6[:, 0:P], (0, P), "swa", 0)
                link.wait()
                if last:
                    dve.wait_ge(s["cache_st"], 32)
                nc.vector.tensor_tensor(krot[:, :], t1[:, 0:P], t2[:, 0:P], ALU.add).then_inc(s["k_r"], 1)

            h_scale(1)
            h_shift()
            dve.wait_ge(s["init"], 4)
            dve.wait_ge(s["misc_in"], 80)
            dve.wait_ge(s["band_in"], 16)
            keys(0)

            def rotation(n, h, i):
                dve.wait_ge(s["pj"], n + 1)
                if h == 0:
                    dve.wait_ge(s["k_r"], i + 1)
                bank_ = pj_bank[h % 2]
                rotate(bank_[:, 0:256], (0, 256), "ret", 0)
                rotate(bank_[:, 384:512], (384, 512), "swa", 256)
                link.wait()
                nc.vector.tensor_tensor(rot, t1, t2, ALU.add).then_inc(s["rot"], 1)

            def weigh(n, h):
                dve.wait_ge(s["qk_e"], n + 1)
                link(nc.vector.tensor_tensor(qdT, qkT[:, 0:P], cst("qdec")[:, h * P:(h + 1) * P], ALU.mult))
                dve.wait_ge(s["att_s"], n + 1)
                nc.vector.tensor_tensor(pr, psS[:, :, 0:256],
                                        band[:, :].rearrange("p (o c) -> p o c", o=1).to_broadcast([P, 2, 256]),
                                        ALU.add)
                link(nc.vector.tensor_tensor(attT, p2[:, 384:512], cst("dmask")[:, h * P:(h + 1) * P], ALU.mult))
                link(nc.vector.tensor_reduce(mx, pr, AX.X, ALU.max))
                sink = sinkr[:, 2 * h:2 * h + 2]
                link(nc.vector.scalar_tensor_tensor(m2, mx, ASC, sink, ALU.mult, ALU.max))
                nc.vector.tensor_scalar(mneg, m2, -1.0, None, ALU.mult)
                nc.vector.tensor_tensor(es, sink, m2, ALU.subtract).then_inc(s["nm_r"], 1)

            def normalise(n):
                dve.wait_ge(s["ex_r"], n + 1)
                link(nc.vector.tensor_tensor(den2, den, es, ALU.add))
                link(nc.vector.reciprocal(rden, den2))
                nc.vector.tensor_tensor(pr, pr, rden.rearrange("p (g o) -> p g o", o=1).to_broadcast([P, 2, 256]), ALU.mult
                                        ).then_inc(s["pn_r"], 1)

            def retention_out(n, h, i):
                dve.wait_ge(s["oa"], n + 1)
                nc.vector.tensor_copy(o_all[:, bass.ds(i, 1), h * P:(h + 1) * P],
                                      p7[:, 0:P].rearrange("p (o c) -> p o c", o=1))
                nc.vector.scalar_tensor_tensor(S[:, h, :], S[:, h, :], GAMMA[h] ** P, p7[:, P:2 * P],
                                               ALU.mult, ALU.add).then_inc(s["st_u"], 1)

            def window_out(n, h, i):
                dve.wait_ge(s["osT_t"], n + 1)
                nc.vector.tensor_copy(oswT[:, h, bass.ds(i * P, P)], p7[:, 256:384]).then_inc(s["os_r"], 1)

            def mix(i, last):
                for h in range(1, H):
                    n = 4 * i + h
                    rotation(n - 1, h - 1, i)
                    if h == 1:
                        if last:
                            dve.wait_ge(s["tab_in"], 80)
                            link(nc.vector.scalar_tensor_tensor(A1[0:NS], A1[0:NS], 1.0, NGR[0:NS], ALU.add, ALU.mult))
                        h_scale(i + 2)
                    else:
                        normalise(n - 2)
                        if h == 2:
                            h_shift()
                        window_out(n - 2, h - 2, i)
                    weigh(n - 1, h - 1)
                    retention_out(n - 1, h - 1, i)
                n = 4 * i + 3
                rotation(n, 3, i)
                normalise(n - 1)
                window_out(n - 1, 2, i)
                weigh(n, 3)
                nc.vector.tensor_copy(K2[:, 0:P], K2[:, P:2 * P])
                nc.vector.tensor_copy(band[:, :], cst("band")).then_inc(s["kwin"], 1)
                normalise(n)
                retention_out(n, 3, i)
                keys(i + 1, last)
                window_out(n, 3, i)
                nc.vector.tensor_copy(V2[:, 0:P], V2[:, P:2 * P]).then_inc(s["win"], 1)

            with dve.Fori(0, NT - 1) as i:
                link.loop(i, 4 * (6 + 4 + 2) + 1 + 3)
                mix(i, False)
            link.end(NT - 1)
            mix(NT - 1, True)
            dve.wait_ge(s["k_r"], NT + 1)
            for h in range(H):
                dve.wait_ge(s["spj"], h + 1)
                dve.wait_ge(s["srot"], h)
                bank_ = pj_bank[h % 2][0:NS, :]
                rotate(bank_[:, 0:256], (0, 256), "ret", 0, NS)
                rotate(bank_[:, 384:512], (384, 512), "swa", 256, NS)
                link.wait()
                nc.vector.tensor_tensor(rots[:, h, :], t1[0:NS], t2[0:NS], ALU.add).then_inc(s["srot"], 1)
            dve.wait_ge(s["srot"], H)
            dve.wait_ge(s["sv_c"], H)
            for h in range(H):
                link(nc.vector.tensor_scalar(ks8[:, h, :], rots[:, h, P:2 * P], RSC, None, ALU.mult))
                link(nc.vector.tensor_tensor_reduce(junk8, rots[:, h, 0:P], ks8[:, h, :], 1.0, 0.0, ALU.mult, ALU.add,
                                                    qk8[:, h:h + 1]))
                nc.vector.tensor_tensor(vM[:, h], vs[:, h, :].rearrange("p (o c) -> p o c", o=1).to_broadcast([NS, NS, P]),
                                        ident[0:NS, 0:NS].rearrange("p (b o) -> p b o", o=1).to_broadcast([NS, NS, P]),
                                        ALU.mult).then_inc(s["sqm"], 1)
            dve.wait_ge(s["sq_e"], 1)
            e8 = cst("eye8").rearrange("p (b c) -> p b c", b=NS)
            for h in range(H):
                nc.vector.tensor_tensor(qM[:, h], qsT[:, 8 * h:8 * h + 8].rearrange("p (o c) -> p o c", o=1)
                                        .to_broadcast([P, NS, NS]), e8, ALU.mult).then_inc(s["sqm"], 1)
            for g in range(2):
                nc.vector.tensor_scalar(qB[:, :, :, g], qsT[:, 32:64].rearrange("p (h b) -> p b h", h=H),
                                        cst("grp")[:, g:g + 1], None, ALU.mult).then_inc(s["sqm"], 1)
            dve.wait_ge(s["sst_in"], 16)
            for h in range(H):
                dve.wait_ge(s["socr"], h + 1)
                stv = st[:, h].rearrange("p (a b) e -> p a (b e)", a=2)
                nc.vector.scalar_tensor_tensor(stv, stv, GAMMA[h], psS[:, :, :], ALU.mult, ALU.add
                                               ).then_inc(s["sst_r"], 1)
                link(nc.vector.tensor_scalar(tmp8, p7[0:NS, 0:P], GAMMA[h], None, ALU.mult))
                nc.vector.scalar_tensor_tensor(o_all[0:NS, NT, h * P:(h + 1) * P], vs[:, h, :], qk8[:, h:h + 1], tmp8,
                                               ALU.mult, ALU.add).then_inc(s["so_r"], 1)
            dve.wait_ge(s["ssc"], 1)
            sc8 = psS[0:NS, :, :].rearrange("p a (b c) -> p (a b) c", b=4)
            link(nc.vector.tensor_reduce(mx8, sc8, AX.X, ALU.max))
            link(nc.vector.tensor_scalar(m8, mx8, ASC, sinkc[:, :], ALU.mult, ALU.max))
            link(nc.vector.scalar_tensor_tensor(pS, sc8, ASC, m8.rearrange("p (b o) -> p b o", o=1).to_broadcast([NS, NS, P]),
                                                ALU.mult, ALU.subtract))
            nc.vector.tensor_scalar(es8, m8, -1.0, sinkc[:, :], ALU.mult, ALU.add).then_inc(s["ssm"], 1)
            dve.wait_ge(s["sex"], 1)
            link(nc.vector.tensor_reduce(den8, pS, AX.X, ALU.add))
            link(nc.vector.tensor_tensor(den8, den8, es8, ALU.add))
            link(nc.vector.reciprocal(rd8, den8))
            nc.vector.tensor_tensor(pS, pS, rd8.rearrange("p (b o) -> p b o", o=1).to_broadcast([NS, NS, P]), ALU.mult
                                    ).then_inc(s["spn"], 1)
            dve.wait_ge(s["spv"], 1)
            pv = p5[:, 64:128].rearrange("p (b h g) -> p h b g", b=NS, h=H)
            for g in range(2):
                r = slice(g * HD, (g + 1) * HD)
                nc.vector.tensor_copy(oswT[r, :, T:TA], pv[r, :, :, g]).then_inc(s["sosw"], 1)
            dve.wait_ge(s["sst_st"], 16)
            with dve.Fori(0, 3) as c:
                for m in range(H):
                    dve.wait_ge(s["rg_s"], 4 * c + m + 1)
                    nc.vector.tensor_tensor(oretT[:, m, bass.ds(c * CHUNK, CHUNK)], rg_bank[m][:, 0:CHUNK], sg[:, m, :],
                                            ALU.mult).then_inc(s["rg_r"], 1)
            dve.wait_ge(s["o_sq"], 2)
            nc.vector.tensor_reduce(oms[:, 0:32], osq.rearrange("p (a c) -> p a c", c=P), AX.X, ALU.add)
            nc.vector.tensor_reduce(oms[:, 32:36], osq8.rearrange("p (a c) -> p a c", c=P), AX.X, ALU.add
                                    ).then_inc(s["om_r"], 1)
            dve.wait_ge(s["or_r"], 1)

            def norm_o(t, slot):
                nc.vector.tensor_tensor(onrm[:, slot], o_all[:, bass.ds(t, 1), :].rearrange("p o (h c) -> p (o h) c", h=H),
                                        orstd[:, bass.ds(4 * t, 4)].rearrange("p (h o) -> p h o", o=1).to_broadcast([P, H, P]),
                                        ALU.mult).then_inc(s["on_r"], 1)

            def gate_o(t, slot, w=P):
                dve.wait_ge(s["g_t"], t + 1)
                dst = oretT[:, :, bass.ds(t * P, w)]
                nc.vector.tensor_tensor(dst, dst, g_bank[slot][:, :].rearrange("p (h c) -> p h c", h=H)[:, :, 0:w], ALU.mult
                                        ).then_inc(s["g_r"], 1)

            with dve.Fori(0, NT // 2) as t2_:
                norm_o(2 * t2_, 0)
                norm_o(2 * t2_ + 1, 1)
                gate_o(2 * t2_, 0)
                gate_o(2 * t2_ + 1, 1)
            norm_o(NT, 0)
            gate_o(NT, 0, NS)

            def merge(m, slot):
                for c in range(3):
                    g = 3 * m + c
                    q = (3 * slot + c) % 2
                    by = lift[4 * q:]
                    dve.wait_ge(s["mg_s"], 2 * g + 2)
                    for j in range(2):
                        link(nc.vector.tensor_tensor(g2b[:, q, 2 + j, :], by[2 + j][:, 0:CHUNK], g2b[:, q, j, :], ALU.mult))
                    nc.vector.tensor_tensor(mT[:, bass.ds(m, 1), bass.ds(c * CHUNK, CHUNK)],
                                            g2b[:, q, 2:3, :], g2b[:, q, 3:4, :], ALU.add).then_inc(s["mg_r"], 1)

            with dve.Fori(0, KD // 2) as m2_:
                link.loop(m2_, 12)
                merge(2 * m2_, 0)
                merge(2 * m2_ + 1, 1)
            link.end(KD // 2)
            dve.wait_ge(s["tab_in"], 80 + 64)
            link(nc.vector.scalar_tensor_tensor(A2, A2, 1.0, n2row, ALU.add, ALU.mult))
            link(nc.vector.memset(lg[:, NT, :], 0.0))

            def resid(t, rows=P):
                dve.wait_ge(s["wo_mm"], t + 1)
                xd = x1[0:rows, bass.ds(t, 1), :].rearrange("p o c -> p (o c)")
                link(nc.vector.tensor_tensor(xd.rearrange("p (a c) -> p a c", a=2), psS[0:rows, :, :],
                                             G1[0:rows].rearrange("p (a c) -> p a c", a=2), ALU.mult))
                dve.wait_ge(s["xr_in"], 16 * t + 16)
                nc.vector.tensor_tensor(xd, xd, xt[0:rows], ALU.add).then_inc(s["x1_r"], 1)

            def norm2(t, rows=P, first=False):
                dve.wait_ge(s["rs2_r"], t + 1)
                if not first:
                    dve.wait_ge(s["h2_t"], t)
                    dve.wait_ge(s["h2_st"], 16 * t)
                xd = x1[0:rows, bass.ds(t, 1), :].rearrange("p o c -> p (o c)")
                link(nc.vector.scalar_tensor_tensor(hrow[0:rows], xd, rstd[0:rows], A2[0:rows], ALU.mult, ALU.mult))
                nc.vector.tensor_tensor(hrow[0:rows], hrow[0:rows], B2[0:rows], ALU.add).then_inc(s["h2_r"], 1)

            def logits(t, rows=P):
                dve.wait_ge(s["rt_mm"], t + 1)
                nc.vector.tensor_tensor(lg[0:rows, bass.ds(t, 1), :], p7[0:rows, 0:NL].rearrange("p (o c) -> p o c", o=1),
                                        brow[0:rows].rearrange("p (o c) -> p o c", o=1), ALU.add).then_inc(s["lg_r"], 1)

            resid(0)
            norm2(0, first=True)
            with dve.Fori(1, NT) as t:
                link.loop(t - 1, 2)
                resid(t)
                logits(t - 1)
                norm2(t)
            link.end(NT - 1)
            dve.wait_ge(s["tab_in"], 144 + 48)
            link(nc.vector.scalar_tensor_tensor(A2[0:NS], A2[0:NS], 1.0, n2row[0:NS], ALU.add, ALU.mult))
            resid(NT, NS)
            logits(NT - 1)
            norm2(NT, NS)
            logits(NT, NS)

            dve.wait_ge(s["lg_r"], NT + 1)
            dve.wait_ge(s["h2_st"], 16 * (NT + 1))
            tt, n9 = nc.vector.tensor_tensor, NT + 1

            def b3(a, k):
                return a.to_broadcast([P, n9, k])

            iota = cst("iota").rearrange("p (o e) -> p o e", o=1)

            def first_max(x, k, mxv, eq, cn, ix, oh):
                link(nc.vector.tensor_reduce(mxv, x, AX.X, ALU.max))
                link(tt(eq, x, b3(mxv, k), ALU.is_equal))
                link(nc.vector.scalar_tensor_tensor(cn, eq, -64.0, b3(iota[:, :, 0:k], k), ALU.mult, ALU.add))
                link(nc.vector.tensor_reduce(ix, cn, AX.X, ALU.min))
                link(tt(oh, cn, b3(ix, k), ALU.is_equal))

            g4 = lg[:, :, 0:NG]
            first_max(g4, NG, gmx, eq4, cnd4, gix, oh4)
            tt(gsh, g4, b3(gmx, NG), ALU.subtract).then_inc(s["gsh_r"], 1)
            link(tt(ep, lg[:, :, NG:NL].rearrange("p t (g j) -> p t g j", g=NG),
                    oh4.rearrange("p t (g o) -> p t g o", o=1).to_broadcast([P, n9, NG, EPG]), ALU.mult))
            link(nc.vector.tensor_reduce(ein, ep.rearrange("p t g j -> p t j g"), AX.X, ALU.add))
            first_max(ein, EPG, v1, eqv, cnd, i1, oh1)
            link(nc.vector.scalar_tensor_tensor(e2, oh1, NEG, ein, ALU.mult, ALU.add))
            first_max(e2, EPG, v2_, eqv, cnd, i2, oh2)
            tt(dv, v2_, v1, ALU.subtract).then_inc(s["dv_r"], 1)
            for mkj, ohj in ((mk1, oh1), (mk2, oh2)):
                link(tt(mkj.rearrange("p t (g j) -> p t g j", g=NG),
                        oh4.rearrange("p t (g o) -> p t g o", o=1).to_broadcast([P, n9, NG, EPG]),
                        ohj.rearrange("p t (o j) -> p t o j", o=1).to_broadcast([P, n9, NG, EPG]), ALU.mult))
            link(tt(mk, mk1, mk2, ALU.add))
            tt(mk, mk, b3(cst("valid").rearrange("p (t o) -> p t o", o=1), NE), ALU.mult).then_inc(s["mk_r"], 1)
            dve.wait_ge(s["rk_mm"], 1)
            link(nc.vector.memset(pre[:, 0, :], 0.0))
            tot = p1[:, 0:9 * NE].rearrange("p (t e) -> p t e", t=9)
            for t in range(NT):
                link(tt(pre[:, t + 1, :], pre[:, t, :], tot[:, t, :], ALU.add))
            link(tt(cnt, pre[:, NT, :], tot[:, NT, :], ALU.add))
            link(tt(pre, pre, p0[:, 0:9 * NE].rearrange("p (t e) -> p t e", t=9), ALU.add))
            link(tt(thr_t, cnt.rearrange("p (e o) -> p e o", o=1).to_broadcast([P, NE, MAXOV]),
                    cst("thr").rearrange("p (o j) -> p o j", o=1).to_broadcast([P, NE, MAXOV]), ALU.is_gt))
            link(nc.vector.tensor_reduce(nbx, thr_t, AX.X, ALU.add))
            a, b = obx, obc
            link(nc.vector.tensor_copy(a, nbx))
            for sh in (1, 2, 4, 8, 16):
                link(nc.vector.tensor_copy(b[:, 0:sh], a[:, 0:sh]))
                link(tt(b[:, sh:NE], a[:, sh:NE], a[:, 0:NE - sh], ALU.add))
                a, b = b, a
            incl, free = a, b
            link(tt(blk_t, incl[0:1].rearrange("p (o e) -> p o e", o=1).to_broadcast([1, NOVER, NE]),
                    cst("blk", 1).rearrange("p (b o) -> p b o", o=1).to_broadcast([1, NOVER, NE]), ALU.is_le))
            link(nc.vector.tensor_reduce(emap[:, 0:NOVER], blk_t, AX.X, ALU.add))
            link(nc.vector.tensor_scalar(emap[:, 0:NOVER], emap[:, 0:NOVER], float(NE - 1), None, ALU.min))
            link(nc.vector.tensor_copy(emap[:, NOVER:NOVER + 1], incl[0:1, NE - 1:NE]))
            nc.vector.tensor_copy(nover[:, :], emap).then_inc(s["ov_n"], 1)
            link(tt(free, incl, nbx, ALU.subtract))
            link(nc.vector.tensor_scalar(free, free, float(CAP), float((NE - 1) * CAP), ALU.mult, ALU.add))
            link(tt(free, free, cst("ec"), ALU.subtract))
            link(nc.vector.tensor_scalar(ge, pre, float(CAP), None, ALU.is_ge))
            link(tt(adj, ge, free.rearrange("p (o e) -> p o e", o=1).to_broadcast([P, n9, NE]), ALU.mult))
            link(tt(pos, pre, cst("ec").rearrange("p (o e) -> p o e", o=1).to_broadcast([P, n9, NE]), ALU.add))
            link(tt(pos, pos, adj, ALU.add))
            for j, mkj in enumerate((mk1, mk2)):
                link(tt(adj, pos, mkj, ALU.mult))
                link(nc.vector.tensor_reduce(pf[:, :, j:j + 1], adj, AX.X, ALU.add))
            nc.vector.tensor_copy(posu[:, :].rearrange("p (t j) -> p t j", j=2), pf).then_inc(s["pos_r"], 1)
            dve.wait_ge(s["gex_r"], 1)
            link(nc.vector.tensor_reduce(gsum, gsh, AX.X, ALU.add))
            link(nc.vector.reciprocal(pgr, gsum))
            dve.wait_ge(s["dex_r"], 1)
            link(nc.vector.tensor_scalar(v1, dv, 1.0, None, ALU.add))
            link(nc.vector.reciprocal(v2_, v1))
            wv = wsel[:, :].rearrange("p (t j) -> p t j", j=2)
            link(tt(wv[:, :, 0:1], pgr, v2_, ALU.mult))
            link(tt(wv[:, :, 1:2], wv[:, :, 0:1], dv, ALU.mult))
            dve.wait_ge(s["slot_in"], 16)
            nc.vector.tensor_copy(slotf, slotl).then_inc(s["slotf_r"], 1)
            dve.wait_ge(s["slotT_t"], 1)
            nc.vector.tensor_copy(slotT[:, :], p2[0:CAP, 0:NBLK]).then_inc(s["slotT_r"], 1)

            def turn_out(b):
                dve.wait_ge(s["xgT_t"], b + 1)
                for j, bk in enumerate((p5, p6)):
                    nc.vector.tensor_copy(xgT[:, 4 * j:4 * j + 4, :], bk[:, 0:4 * CAP].rearrange("p (k t) -> p k t", k=4)
                                          ).then_inc(s["xgT_e"], 1)

            def hidden(b, slot):
                bk = pj_bank[slot][:, 0:4 * CAP].rearrange("p (f t) -> p f t", f=4)
                dve.wait_ge(s["hs"], b + 1)
                nc.vector.tensor_tensor(hid, bk[:, 0:2, :], sgh, ALU.mult).then_inc(s["h_a"], 1)
                dve.wait_ge(s["h_a"], b + 1)
                nc.vector.tensor_tensor(hid, hid, bk[:, 2:4, :], ALU.mult).then_inc(s["hid_r"], 1)

            turn_out(0)
            with dve.Fori(0, NE // 2 - 1) as b2:
                for slot in range(2):
                    hidden(2 * b2 + slot, slot)
                    turn_out(2 * b2 + slot + 1)
            hidden(NE - 2, 0)
            turn_out(NE - 1)
            hidden(NE - 1, 1)
            n_over = dve.value_load(nover[0:1, NOVER:NOVER + 1], min_val=0, max_val=NOVER)
            with dve.Fori(0, NOVER) as b:
                with dve.If(b < n_over):
                    turn_out(NE + b)
                    hidden(NE + b, 0)
            dve.wait_ge(s["tab_in"], 192 + 32)

            def combine(t, slot, t2_, rows=P):
                dve.wait_ge(s[f"yg_in{slot}"], 32 * (t2_ + 1))
                w = wsel[0:rows, bass.ds(2 * t, 2)]
                link(nc.vector.tensor_scalar(yg[0:rows, slot, 0], yg[0:rows, slot, 0], w[:, 0:1], None, ALU.mult))
                link(nc.vector.scalar_tensor_tensor(yg[0:rows, slot, 0], yg[0:rows, slot, 1], w[:, 1:2],
                                                    yg[0:rows, slot, 0], ALU.mult, ALU.add))
                link(nc.vector.tensor_tensor(yg[0:rows, slot, 0], yg[0:rows, slot, 0], G2[0:rows], ALU.mult))
                xd = x1[0:rows, bass.ds(t, 1), :].rearrange("p o c -> p (o c)")
                nc.vector.tensor_tensor(xd, xd, yg[0:rows, slot, 0], ALU.add).then_inc(s["x2_r"], 1)

            def finish(t, slot, stored, rows=P):
                dve.wait_ge(s["rs3_r"], t + 1)
                if stored is not None:
                    dve.wait_ge(s[f"out_st{slot}"], stored)
                xd = x1[0:rows, bass.ds(t, 1), :].rearrange("p o c -> p (o c)")
                nc.vector.scalar_tensor_tensor(yo[0:rows, slot], xd, rstd[0:rows], FG[0:rows], ALU.mult, ALU.mult
                                               ).then_inc(s["yo_r"], 1)

            for t in range(2):
                combine(t, t, 0)
                finish(t, t, None)
            with dve.Fori(1, NT // 2) as t2_:
                link.loop(t2_ - 1, 6)
                for slot in range(2):
                    combine(2 * t2_ + slot, slot, t2_)
                    finish(2 * t2_ + slot, slot, 16 * t2_)
            link.end(NT // 2 - 1)
            dve.wait_ge(s["tab_in"], 224 + 16)
            combine(NT, 0, NT // 2, NS)
            finish(NT, 0, 8 * NT, NS)

        @block.tensor
        def _(pe):
            mm = nc.tensor.matmul
            pe.wait_ge(s["const_in"], 16)
            pe.wait_ge(s["c_silu"], 1)
            for k in range(KD):
                last = nc.tensor.transpose(p2[:, 9 * k:9 * k + 9], csig[:, k * P:(k + 1) * P], ident[0:9, 0:9])
            last.then_inc(s["cT_t"], 1)
            pe.wait_ge(s["cT_r"], 1)
            cTv = cT[:, :].rearrange("p (k c) -> p k c", k=KD)

            def ada(j2, slot, free):
                if free:
                    pe.wait_ge(s["mod_r"], 2 * j2 + slot - 1)
                pe.wait_ge(s[f"ada_in{slot}"], 32 * (j2 + 1))
                for k in range(KD):
                    last = mm(pj_bank[slot][0:9, :], cTv[:, k, :], wada[:, slot, k, :], start=k == 0, stop=k == KD - 1)
                last.then_inc(s["ada_mm"], 1)

            ada(0, 0, False)
            ada(0, 1, False)
            with pe.Fori(1, ADA // 2) as j2:
                ada(j2, 0, True)
                ada(j2, 1, True)

            def h_turn(half):
                for k in range(4):
                    kk = 4 * half + k
                    last = nc.tensor.transpose((p6, p5)[half][:, k * P:(k + 1) * P], hrow[:, kk * P:(kk + 1) * P], ident)
                last.then_inc(s["hT_t"], 1)

            def kv(ks):
                for k in ks:
                    last = mm(p6[:, 0:256], hst[:, k, :], wkv[:, k, :], start=k == 0, stop=k == KD - 1)
                if k == KD - 1:
                    last.then_inc(s["kv_mm"], 1)

            pe.wait_ge(s["h_r"], 1)
            h_turn(0)
            h_turn(1)
            pe.wait_ge(s["hT_e"], 2)
            pe.wait_ge(s["wq_in"], 144)
            kv(range(KD))

            def turn_qk(n, h):
                pe.wait_ge(s["rot"], n + 1)
                for j in range(3):
                    last = nc.tensor.transpose(p2[:, j * P:(j + 1) * P], rot[:, j * P:(j + 1) * P], ident)
                last.then_inc(s["qk_t"], 1)

            def scores(n, i):
                pe.wait_ge(s["qk_e"], n + 1)
                mm(p2[:, 384:512], qkT[:, P:2 * P], qkT[:, 0:P], start=True, stop=True)
                pe.wait_ge(s["kT_e"], i + 1)
                for g in range(2):
                    r = slice(g * HD, (g + 1) * HD)
                    last = mm(psS[:, g, 0:256], qkT[r, 256:384], K2[r, :], start=True, stop=True)
                last.then_inc(s["att_s"], 1)

            def outputs(n, h):
                pe.wait_ge(s["v_c"], n + 1)
                pe.wait_ge(s["kd_r"], n + 1)
                pe.wait_ge(s["nm_r"], n + 1)
                mm(p7[:, 0:P], attT, vb, start=True, stop=False)
                mm(p7[:, 0:P], qdT, S[:, h, :], start=False, stop=True)
                mm(p7[:, P:2 * P], kd, vb, start=True, stop=True).then_inc(s["oa"], 1)

            def turn_probs(n):
                pe.wait_ge(s["pn_r"], n + 1)
                for g in range(2):
                    for b in range(2):
                        last = nc.tensor.transpose(p5[:, (2 * g + b) * P:(2 * g + b + 1) * P],
                                                   pr[:, g, b * P:(b + 1) * P], ident)
                last.then_inc(s["pT_t"], 1)

            def window(n, i):
                pe.wait_ge(s["pT_e"], n + 1)
                pe.wait_ge(s["st_u"], n + 1)
                pe.wait_ge(s["v_e"], i + 1)
                for g in range(2):
                    r = slice(g * HD, (g + 1) * HD)
                    for b in range(2):
                        last = mm(p7[r, 256:384], V2[:, b * P + g * HD:b * P + (g + 1) * HD], prT[:, g, b, :],
                                  start=b == 0, stop=b == 1)
                last.then_inc(s["osT_t"], 1)

            def project_h(h, ks, rows=P, done="pj"):
                for k in ks:
                    last = mm(pj_bank[h % 2][0:rows, :], hst[:, k, 0:rows], wqh[:, h, k, :], start=k == 0, stop=k == KD - 1)
                if k == KD - 1:
                    last.then_inc(s[done], 1)

            def mix(i, last_):
                for h in range(1, H):
                    n = 4 * i + h
                    project_h(h, (0, 1))
                    if h == 1:
                        pe.wait_ge(s["k_r"], i + 1)
                        pe.wait_ge(s["v_e"], i + 1)
                        nc.tensor.transpose(p6[:, 256:384], krot[:, :], ident).then_inc(s["kT_t"], 1)
                    project_h(h, (2, 3))
                    turn_qk(n - 1, h - 1)
                    if h > 1:
                        turn_probs(n - 2)
                    project_h(h, (4, 5))
                    if h > 1:
                        window(n - 2, i)
                    scores(n - 1, i)
                    project_h(h, (6, 7))
                    outputs(n - 1, h - 1)
                n = 4 * i + 3
                rows, done = (NS, "spj") if last_ else (P, "pj")
                pe.wait_ge(s["h_r"], i + 2)
                h_turn(0)
                h_turn(1)
                pe.wait_ge(s["hT_e"], 2 * i + 3)
                project_h(0, (0, 1), rows, done)
                turn_qk(n, 3)
                project_h(0, (2, 3), rows, done)
                pe.wait_ge(s["hT_e"], 2 * i + 4)
                turn_probs(n - 1)
                project_h(0, (4, 5), rows, done)
                window(n - 1, i)
                scores(n, i)
                kv(range(KD))
                outputs(n, 3)
                project_h(0, (6,), rows, done)
                turn_probs(n)
                project_h(0, (7,), rows, done)
                window(n, i)

            project_h(0, range(KD))
            with pe.Fori(0, NT - 1) as i:
                mix(i, False)
            mix(NT - 1, True)
            for h in range(1, H):
                if h >= 2:
                    pe.wait_ge(s["sv_c"], h - 1)
                project_h(h, range(KD), NS, "spj")
            pe.wait_ge(s["srot"], H)
            pe.wait_ge(s["nm_r"], 4 * NT)
            for h in range(H):
                nc.tensor.transpose(p2[:, 8 * h:8 * h + 8], rots[:, h, 0:P], ident[0:NS, 0:NS])
                last = nc.tensor.transpose(p2[:, 32 + 8 * h:40 + 8 * h], rots[:, h, 256:384], ident[0:NS, 0:NS])
            last.then_inc(s["sq_t"], 1)
            pe.wait_ge(s["sst_in"], 16)
            pe.wait_ge(s["sqm"], 2 * H + 2)
            pe.wait_ge(s["os_r"], 4 * NT)
            for h in range(H):
                if h:
                    pe.wait_ge(s["sst_r"], h)
                    pe.wait_ge(s["so_r"], h)
                for b in range(NS):
                    mm(p7[0:NS, 0:P], qM[:, h, b, :], st[:, h, b, :], start=b == 0, stop=b == NS - 1)
                for a in range(2):
                    last = mm(psS[:, a, :], ks8[:, h, :], vM[:, h, 4 * a:4 * a + 4, :], start=True, stop=True)
                last.then_inc(s["socr"], 1)
            pe.wait_ge(s["swin_c"], 32)
            pe.wait_ge(s["swin_n"], 32)
            pe.wait_ge(s["sst_r"], H)
            for b in range(NS):
                last = nc.tensor.transpose(psS[:, b // 4, (b % 4) * P:(b % 4 + 1) * P], kwin[:, b, :], ident)
            last.then_inc(s["skT_t"], 1)
            pe.wait_ge(s["skT_e"], 2)
            for b in range(NS):
                last = mm(psS[0:NS, b // 4, (b % 4) * P:(b % 4 + 1) * P], qB[:, b].rearrange("p h g -> p (h g)"),
                          kwT[:, b, :], start=True, stop=True)
            last.then_inc(s["ssc"], 1)
            pe.wait_ge(s["spn"], 1)
            for b in range(NS):
                last = nc.tensor.transpose(p5[:, 8 * b:8 * b + 8], pS[:, b, :], ident[0:NS, 0:NS])
            last.then_inc(s["spT_t"], 1)
            pe.wait_ge(s["spT_e"], 1)
            for b in range(NS):
                last = mm(p5[:, 64 + 8 * b:72 + 8 * b], vwin[:, b, :], pTs[:, b, :], start=True, stop=True)
            last.then_inc(s["spv"], 1)
            pe.wait_ge(s["rg_in"], 16)
            pe.wait_ge(s["hT_c"], NT + 1)
            pe.wait_ge(s["sosw"], 2)
            pe.wait_ge(s["sv_c"], H)

            def rg(c, free):
                for m in range(H):
                    if free:
                        pe.wait_ge(s["rg_r"], 4 * c + m - 3)
                    for k in range(KD):
                        last = mm(rg_bank[m][:, 0:CHUNK], wrg[:, k, m * P:(m + 1) * P],
                                  hT[:, k, bass.ds(c * CHUNK, CHUNK)], start=k == 0, stop=k == KD - 1)
                    last.then_inc(s["rg_mm"], 1)

            rg(0, False)
            with pe.Fori(1, 3) as c:
                rg(c, True)

            def turn_o(t, slot, free, rows=P):
                pe.wait_ge(s["on_r"], t + 1)
                if free:
                    pe.wait_ge(s["g_r"], t - 1)
                for h in range(H):
                    last = nc.tensor.transpose(g_bank[slot][:, h * P:h * P + rows], onrm[0:rows, slot, h], ident[0:rows, 0:rows])
                last.then_inc(s["g_t"], 1)

            turn_o(0, 0, False)
            turn_o(1, 1, False)
            with pe.Fori(1, NT // 2) as t2_:
                turn_o(2 * t2_, 0, True)
                turn_o(2 * t2_ + 1, 1, True)
            turn_o(NT, 0, True, NS)

            def merge(m2_, slot, free):
                pe.wait_ge(s[f"lw_in{slot}"], 16 * (m2_ + 1))
                for c in range(3):
                    g = 3 * (2 * m2_ + slot) + c
                    if free or 3 * slot + c >= 2:
                        pe.wait_ge(s["mg_r"], g - 1)
                    elif c == 0:
                        pe.wait_ge(s["g_r"], NT + 1)
                        pe.wait_ge(s["rg_r"], 12)
                    bs = lift[4 * ((3 * slot + c) % 2):]
                    cols = bass.ds(c * CHUNK, CHUNK)
                    for j in range(2):
                        for k in range(KD):
                            mm(bs[j][:, 0:CHUNK], wl[:, slot, 8 * j + k, :], hT[:, k, cols], start=k == 0, stop=k == KD - 1)
                    for j, src in enumerate((oretT, oswT)):
                        for k in range(H):
                            last = mm(bs[2 + j][:, 0:CHUNK], wl[:, slot, 16 + 4 * j + k, :], src[:, k, cols],
                                      start=k == 0, stop=k == H - 1)
                    last.then_inc(s["mg_mm"], 1)

            merge(0, 0, False)
            merge(0, 1, False)
            with pe.Fori(1, KD // 2) as m2_:
                merge(m2_, 0, True)
                merge(m2_, 1, True)

            def project(t, rows=P, first=False):
                pe.wait_ge(s["m_c"], t + 1)
                if not first:
                    pe.wait_ge(s["x1_r"], t)
                for n in range(2):
                    for k in range(KD):
                        last = mm(psS[0:rows, n, :], hst[:, k, 0:rows], wo[:, k, n * 512:(n + 1) * 512],
                                  start=k == 0, stop=k == KD - 1)
                last.then_inc(s["wo_mm"], 1)

            def router(t, rows=P):
                pe.wait_ge(s["h2_r"], t + 1)
                for k in range(KD):
                    last = nc.tensor.transpose((p5, p6)[k // 4][:, (k % 4) * P:(k % 4) * P + rows],
                                               hrow[0:rows, k * P:(k + 1) * P], ident[0:rows, 0:rows])
                last.then_inc(s["h2_t"], 1)
                pe.wait_ge(s["h2_e"], 2 * t + 2)
                for k in range(KD):
                    last = mm(p7[0:rows, 0:NL], h2T[:, k, 0:rows], rwt[:, k * NL:(k + 1) * NL], start=k == 0, stop=k == KD - 1)
                last.then_inc(s["rt_mm"], 1)

            pe.wait_ge(s["mg_r"], 3 * KD)
            pe.wait_ge(s["wo_in"], 16)
            project(0, first=True)
            with pe.Fori(1, NT) as t:
                project(t)
                router(t - 1)
            project(NT, NS)
            router(NT - 1)
            router(NT, NS)
            pe.wait_ge(s["mk_r"], 1)
            mkf = R4[:, 1536:1536 + 9 * NE]
            mm(p0[:, 0:9 * NE], cst("tri"), mkf, start=True, stop=True)
            mm(p1[:, 0:9 * NE], cst("ones"), mkf, start=True, stop=True).then_inc(s["rk_mm"], 1)
            pe.wait_ge(s["slotf_r"], 1)
            nc.tensor.transpose(p2[0:CAP, 0:NBLK], slotf, ident[0:NBLK, 0:NBLK]).then_inc(s["slotT_t"], 1)

            def turn(b, slot, n):
                pe.wait_ge(s[f"xg_in{slot}"], 16 * n)
                for k in range(KD):
                    last = nc.tensor.transpose((p5, p6)[k // 4][:, (k % 4) * CAP:(k % 4 + 1) * CAP],
                                               xg[0:CAP, slot, k * P:(k + 1) * P], ident[0:CAP, 0:CAP])
                last.then_inc(s["xgT_t"], 1)

            def up(b, slot, n):
                pe.wait_ge(s[f"w13_in{slot}"], 16 * n)
                pe.wait_ge(s["xgT_e"], 2 * b + 2)
                for f in range(4):
                    for k in range(KD):
                        c0 = (f // 2) * 2048 + k * DE + (f % 2) * P
                        last = mm(pj_bank[slot][:, f * CAP:(f + 1) * CAP], we[slot][:, c0:c0 + P], xgT[:, k, :],
                                  start=k == 0, stop=k == KD - 1)
                last.then_inc(s["s1"], 1)

            def down(b, slot, n):
                pe.wait_ge(s[f"w2_in{slot}"], 16 * n)
                pe.wait_ge(s["hid_r"], b + 1)
                for nn in range(2):
                    for f in range(2):
                        c0 = 4096 + f * D + nn * 512
                        last = mm(psS[0:CAP, nn, :], hid[:, f, :], we[slot][:, c0:c0 + 512], start=f == 0, stop=f == 1)
                last.then_inc(s["s2"], 1)

            turn(0, 0, 1)
            pe.wait_ge(s["ov_n"], 1)
            with pe.Fori(0, NE // 2 - 1) as b2:
                for slot in range(2):
                    b = 2 * b2 + slot
                    up(b, slot, b2 + 1)
                    turn(b + 1, 1 - slot, b2 + 1 + slot)
                    down(b, slot, b2 + 1)
            up(NE - 2, 0, NE // 2)
            turn(NE - 1, 1, NE // 2)
            down(NE - 2, 0, NE // 2)
            up(NE - 1, 1, NE // 2)
            down(NE - 1, 1, NE // 2)
            n_over = pe.value_load(nover[0:1, NOVER:NOVER + 1], min_val=0, max_val=NOVER)
            with pe.Fori(0, NOVER) as b:
                with pe.If(b < n_over):
                    turn(NE + b, 0, NE // 2 + 1 + b)
                    up(NE + b, 0, NE // 2 + 1 + b)
                    down(NE + b, 0, NE // 2 + 1 + b)


def constants():
    f = np.float32
    c = np.zeros((P, NC), f)

    def put(name, a):
        lo, hi = COLS[name]
        c[:, lo:hi] = a

    i = np.arange(P)
    ld = np.log(np.asarray(GAMMA))
    put("ident", np.eye(P))
    d = i[None, :] - i[:, None]
    put("dmask", np.concatenate([np.where(d >= 0, np.exp(ld[h] * np.maximum(d, 0)) * RSC, 0.0) for h in range(H)], 1))
    put("qdec", np.tile(np.concatenate([np.exp(ld[h] * (i + 1.0)) for h in range(H)])[None], (P, 1)))
    put("kdec", np.stack([np.exp(ld[h] * (P - 1.0 - i)) * RSC for h in range(H)], 1))
    dist = i[:, None] - (np.arange(2 * P)[None, :] - P)
    band = np.where((dist >= 0) & (dist < P), 0.0, NEG).astype(f)
    put("band", band)
    band0 = band.copy()
    band0[:, :P] = NEG
    put("tri", (i[:, None] < i[None, :]).astype(f))
    put("ones", 1.0)
    put("half", -0.5)
    put("ec", np.arange(NE) * CAP)
    put("iota", np.arange(8))
    put("thr", np.arange(1, MAXOV + 1) * CAP)
    valid = np.ones((P, NT + 1), f)
    valid[NS:, NT] = 0
    put("valid", valid)
    put("blk", np.arange(NOVER))
    put("eye8", np.tile(np.eye(8).reshape(1, 64), (P, 1)))
    put("grp", np.stack([(i < HD), (i >= HD)], 1).astype(f))
    put("inv_d", 1.0 / D)
    put("eps", EPS)
    pos = np.full((NT + 1) * P, T, np.float64)
    pos[:T] = np.arange(T)
    inv_r = (1.0 / (f(10000.0) ** np.linspace(0.0, 1.0, 64, dtype=f))).astype(f)
    inv_s = (f(10000.0) ** (-np.arange(0, HD, 2, dtype=f) / f(HD))).astype(f)
    rope = np.zeros(((NT + 1) * P, 384), f)
    ang = (pos.astype(f)[:, None] * inv_r).astype(np.float64)
    rope[:, 0:128] = np.repeat(np.cos(ang), 2, 1)
    rope[:, 128:256] = np.stack([-np.sin(ang), np.sin(ang)], 2).reshape(-1, 128)
    ang = (pos.astype(f)[:, None] * inv_s).astype(np.float64)
    rope[:, 256:320] = np.tile(np.cos(ang), (1, 2))
    rope[:, 320:384] = np.concatenate([-np.sin(ang), np.sin(ang)], 1)
    tok = (np.arange(NT + 1)[None, :] * P + i[:, None]).astype(np.uint32)
    return c, band0, rope.reshape(NT + 1, P, 384), tok


def kernel(**x):
    from concourse import bacc
    from concourse.bass_utils import run_bass_kernel_spmd

    x = {k: np.asarray(a) for k, a in x.items()}
    c, band0, rope, tok = constants()
    tiles = np.zeros((NT + 1, P, D), np.float32)
    tiles[:NT] = x["x_prompt"].reshape(NT, P, D)
    tiles[NT, :NS] = x["x_sample"].reshape(NS, D)

    def ktiles(w):
        return w.reshape(-1, P, w.shape[1]).transpose(1, 0, 2)

    w_in = x["w_in"][0]
    rq, rk, rv, rg, sq, sk, sv, za, zb = np.split(w_in, np.cumsum([512, 512, 512, 512, 512, 128, 128, D])[:], axis=1)
    groups = []
    for h in range(H):
        a = slice(h * P, (h + 1) * P)
        groups.append(np.concatenate([rq[:, a], rk[:, a], rv[:, a], sq[:, h * HD:(h + 1) * HD],
                                      sq[:, (h + 4) * HD:(h + 5) * HD]], 1))
    w_qkv = np.concatenate([ktiles(g).reshape(P, -1) for g in groups] +
                           [ktiles(np.concatenate([sk, sv], 1)).reshape(P, -1)], 1)
    up_s = x["w_up_swa"][0].reshape(2, H, HD, D).transpose(1, 0, 2, 3).reshape(H * P, D)
    lift = np.concatenate([ktiles(w).reshape(P, -1, KD, P).transpose(2, 0, 1, 3)
                           for w in (za, zb, x["w_up_ret"][0], up_s)], 2).reshape(KD, P, 24 * P)
    we = np.concatenate([
        x["w1"][0].reshape(NE, KD, P, DE).transpose(0, 2, 1, 3).reshape(NE, P, -1),
        x["w3"][0].reshape(NE, KD, P, DE).transpose(0, 2, 1, 3).reshape(NE, P, -1),
        x["w2"][0].reshape(NE, 2, P, D).transpose(0, 2, 1, 3).reshape(NE, P, -1)], 2)
    sink = x["sink"][0].reshape(2, H).T.reshape(-1)
    ins = {
        "const": c, "band0": band0, "rope": rope, "tok": tok, "x": tiles,
        "c": np.concatenate([x["c_prompt"], x["c_sample"]], 0),
        "w_ada": x["w_ada"][0].reshape(KD, P, ADA, 512).transpose(2, 1, 0, 3).reshape(ADA, P, KD * 512),
        "b_ada": x["b_ada"][0].reshape(ADA, 512),
        "n1": x["norm1_g"], "n2": x["norm2_g"], "fg": x["final_g"].reshape(1, D),
        "w_qkv": w_qkv, "w_rg_gate": ktiles(rg).reshape(P, -1), "lift": lift,
        "w_o": ktiles(x["w_o"][0]).reshape(P, -1), "we": we,
        "rw": ktiles(np.concatenate([x["w_rg"][0], x["w_re"][0]], 1)).reshape(P, -1),
        "brow": np.tile(np.concatenate([x["b_rg"][0], x["b_re"][0]])[None], (P, 1)),
        "sinkr": np.tile(sink[None], (P, 1)), "sinkc": sink.reshape(NS, 1),
        "state": x["state_ret"][0].transpose(2, 1, 0, 3).reshape(P, -1),
        "ck": x["cache_swa_k"][0].transpose(1, 0, 2, 3).reshape(P, NS, P),
        "cv": x["cache_swa_v"][0].transpose(1, 0, 2, 3).reshape(P, NS, P),
    }
    outs = {"y": (TA, D), "st_p": (P, H * P), "st_s": (P, H * NS * P), "kp": (P, P), "vp": (P, P),
            "ks": (P, NS, P), "vs": (P, NS, P)}
    nc = bacc.Bacc("TRN2", target_bir_lowering=False, num_devices=1)
    arrays, A, O = {}, {}, {}
    for name, a in ins.items():
        a = np.ascontiguousarray(a)
        arrays[f"in_{name}"] = a
        A[name] = nc.dram_tensor(f"in_{name}", a.shape, mybir.dt.from_np(a.dtype), kind="ExternalInput").ap()
    for name, shape in outs.items():
        O[name] = nc.dram_tensor(f"out_{name}", shape, F32, kind="ExternalOutput").ap()
    build(nc, A, O)
    r = run_bass_kernel_spmd(nc, [arrays], core_ids=[0]).results[0]
    o = {name: np.asarray(r[f"out_{name}"]) for name in outs}
    return (o["y"][:T].reshape(1, T, D), o["y"][T:].reshape(NS, 1, D),
            np.ascontiguousarray(o["st_p"].reshape(P, H, P).transpose(1, 0, 2)).reshape(1, 1, H, P, P),
            np.ascontiguousarray(o["st_s"].reshape(P, H, NS, P).transpose(2, 1, 0, 3)).reshape(1, NS, H, P, P),
            o["kp"].reshape(1, 1, P, 2, HD), o["vp"].reshape(1, 1, P, 2, HD),
            np.ascontiguousarray(o["ks"].transpose(1, 0, 2)).reshape(1, NS, P, 2, HD),
            np.ascontiguousarray(o["vs"].transpose(1, 0, 2)).reshape(1, NS, P, 2, HD))
```

```python
from contextlib import ExitStack

import numpy as np

import concourse.bass as bass
from concourse import mybir

F32 = mybir.dt.float32
U32 = mybir.dt.uint32
ALU = mybir.AluOpType
ACT = mybir.ActivationFunctionType
AX = mybir.AxisListType

P = 128
D = 1024
KD = D // P
T = 1024
NT = T // P
NS = 8
TA = T + NS
H = 4
HD = 64
NE = 32
NG = 4
EPG = NE // NG
DE = 256
CAP = 96
CHUNK = TA // 3
NOVER = (2 * TA) // CAP
NBLK = NE + NOVER
ZR = 16
MAXOV = (TA - 1) // CAP
EPS = 1e-6
NEG = -1e30
RSC = 128.0 ** -0.5
ASC = HD ** -0.5
WE = 3 * D * DE // P
ADA = 6 * D // 512
ADA1 = 2 * D // 512
NL = NG + NE
YG = (0, 1, 2, 2, 3, 3, 4, 4, 4)
GAMMA = [1.0 - 2.0 ** (-5.0 - h) for h in range(H)]

COLS, _n = {}, 0
for _name, _w in (("ident", P), ("dmask", H * P), ("qdec", H * P), ("band", 2 * P), ("tri", P), ("ones", P),
                  ("kdec", H), ("half", 36), ("ec", NE), ("iota", 8), ("thr", MAXOV), ("valid", NT + 1),
                  ("blk", NOVER), ("eye8", 64), ("grp", 2), ("inv_d", 1), ("eps", 1)):
    COLS[_name] = (_n, _n + _w)
    _n += _w
NC = _n


def build(nc, A, O):
    with ExitStack() as ctx:
        def sb(name, cols, dt=F32, rows=P):
            return ctx.enter_context(nc.sbuf_tensor(name, [rows, cols], dt))

        h2_dram = nc.dram_tensor("h2_dram", [TA, D], F32, kind="Internal").ap()
        y_dram = nc.dram_tensor("y_dram", [NBLK * CAP, D], F32, kind="Internal").ap()
        mod_dram = nc.dram_tensor("mod_dram", [9, 6 * D], F32, kind="Internal").ap()

        R0 = sb("R0", KD * TA)
        R1 = sb("R1", 2304 * KD)
        R2 = sb("R2", 9 * 512 + 2 * H * TA)
        R3 = sb("R3", 3 * D)
        R4 = sb("R4", 4 * D)
        const = sb("const", NC)
        work = sb("work", 3072)
        small = sb("small", 64)
        cT = sb("cT", KD * 9)
        K2 = sb("K2", 2 * P)
        V2 = sb("V2", 2 * P)
        krot = sb("krot", P)
        band = sb("band", 2 * P)
        sinkr = sb("sinkr", 2 * H)
        sinkc = sb("sinkc", 1, F32, NS)
        brow = sb("brow", NL)
        rwt = sb("rwt", KD * NL)
        slotT = sb("slotT", NBLK, U32, CAP)
        posu = sb("posu", 2 * (NT + 1), U32)
        tok = sb("tok", NT + 1)
        wsel = sb("wsel", 2 * (NT + 1))
        nover = sb("nover", NOVER + 1, U32, 1)

        def cst(name, rows=P):
            a, b = COLS[name]
            return const[0:rows, a:b]

        ident = cst("ident")
        mod = R0[0:9, 4096:4096 + 2 * D]
        wada1 = [R2[:, 4096 * j:4096 * (j + 1)] for j in range(3)] + [R0[:, 0:4096]]
        bst = work[0:9, 0:2 * D]
        crow = R4[0:9, 0:D]
        csig = R4[0:9, D:2 * D]
        hT = R0[:, :].rearrange("p (k t) -> p k t", k=KD)
        wqh = R1[:, 0:H * 4096].rearrange("p (h k c) -> p h k c", h=H, k=KD)
        wkv = R1[:, H * 4096:].rearrange("p (k c) -> p k c", k=KD)
        o_all = R2[:, 0:9 * 512].rearrange("p (t c) -> p t c", t=9)
        oswT = R2[:, 4608:4608 + H * TA].rearrange("p (h t) -> p h t", h=H)
        oretT = R2[:, 4608 + H * TA:].rearrange("p (h t) -> p h t", h=H)
        wada2 = R2[:, 4608 + H * TA:4608 + H * TA + 4096]
        mod2 = o_all[0:9, NT, :]
        yzero = R1[0:NOVER * CAP // ZR, 17472:17472 + D // 2]
        A1, B1, NGR = R3[:, 0:D], R3[:, D:2 * D], R3[:, 2 * D:3 * D]
        xt, hrow = R4[:, 0:D], R4[:, D:2 * D]
        hst = R4[:, 2 * D:3 * D].rearrange("p (k t) -> p k t", k=KD)
        rope = R4[:, 3 * D:3 * D + 384]
        S = R4[:, 3 * D + 384:3 * D + 896].rearrange("p (h e) -> p h e", h=H)
        t1, t2, rot = work[:, 0:384], work[:, 384:768], work[:, 768:1152]
        qkT, qdT, attT = work[:, 1152:1536], work[:, 1536:1664], work[:, 1664:1792]
        vb, kd = work[:, 1792:1920], work[:, 1920:2048]
        pr = work[:, 2048:2560].rearrange("p (g s) -> p g s", g=2)
        prT = work[:, 2560:3072].rearrange("p (g b t) -> p g b t", g=2, b=2)
        mneg, mx, es, den, den2, rden, m2 = (small[:, 2 * j:2 * j + 2] for j in range(7))
        ms, msb, rstd = small[:, 14:15], small[:, 15:16], small[:, 16:17]
        rots = R4[0:NS, 0:4 * 384].rearrange("p (h c) -> p h c", h=H)
        vs = R4[0:NS, 1536:2048].rearrange("p (h c) -> p h c", h=H)
        qsT = work[:, 0:64]
        qM = work[:, 64:320].rearrange("p (h b c) -> p h b c", h=H, b=NS)
        qB = work[:, 320:384].rearrange("p (b h g) -> p b h g", b=NS, h=H)
        pTs = work[:, 384:448].rearrange("p (b c) -> p b c", b=NS)
        qk8 = work[0:NS, 448:452]
        tmp8 = work[0:NS, 512:640]
        junk8 = work[0:NS, 640:768]
        ks8 = work[0:NS, 768:1280].rearrange("p (h c) -> p h c", h=H)
        pS = work[0:NS, 2048:3072].rearrange("p (b s) -> p b s", b=NS)
        mx8, m8, es8, den8, rd8 = (work[0:NS, 1280 + 8 * j:1288 + 8 * j] for j in range(5))
        st_all = R1[:, 8192:12288]
        st = st_all.rearrange("p (h b e) -> p h b e", h=H, b=NS)
        vM = R1[0:NS, 4096:8192].rearrange("p (h b e) -> p h b e", h=H, b=NS)
        kwin = R1[:, 14400:15424].rearrange("p (b c) -> p b c", b=NS)
        vwin = R1[:, 15424:16448].rearrange("p (b c) -> p b c", b=NS)
        kwT = R1[:, 16448:17472].rearrange("p (b c) -> p b c", b=NS)
        wrg = R1[:, 0:4096].rearrange("p (k c) -> p k c", k=KD)
        sg = R1[:, 12288:12288 + H * CHUNK].rearrange("p (s c) -> p s c", s=H)
        osq, osq8 = R2[:, 4608 + H * TA:4608 + H * TA + 4096], R1[:, 13696:14208]
        oms, omb, orstd = K2[:, 0:36], K2[:, 36:72], K2[:, 72:108]
        mT = R1[:, 0:KD * TA].rearrange("p (m t) -> p m t", m=KD)
        wl = R1[:, 8256:14400].rearrange("p (s k c) -> p s k c", s=2, k=24)
        g2b = work[:, 0:2752].rearrange("p (q s c) -> p q s c", q=2, s=4)
        wo_early = R1[:, 15424:17472]
        wo = [wo_early[:, k * D:(k + 1) * D] if k < 2 else R0[:, k * D:(k + 1) * D] for k in range(KD)]
        mst = (hst, R1[:, 8256:9280].rearrange("p (k t) -> p k t", k=KD))
        x1 = R2[:, 0:9 * D].rearrange("p (t c) -> p t c", t=9)
        G1, A2, B2 = A1, B1, NGR
        n2row, ojunk = R1[:, 14400:15424], work[:, D:2 * D]
        h2T = R4[:, 3 * D:4 * D].rearrange("p (k t) -> p k t", k=KD)
        lg = work[:, 2048:2048 + 9 * NL].rearrange("p (t e) -> p t e", t=9)
        def rv(n, k, w=None):
            a = R4[:, n:n + 9 * k]
            return a.rearrange("p (t e) -> p t e", t=9)
        gsh, eq4, cnd4, oh4 = rv(0, 4), rv(36, 4), rv(72, 4), rv(108, 4)
        gmx, gix, gsum, pgr = rv(144, 1), rv(153, 1), rv(162, 1), rv(171, 1)
        ep = R4[:, 180:180 + 288].rearrange("p (t g j) -> p t g j", t=9, g=NG)
        ein, e2, eqv, cnd, oh1, oh2 = rv(468, 8), rv(540, 8), rv(612, 8), rv(684, 8), rv(756, 8), rv(828, 8)
        v1, i1, v2_, i2, dv = rv(900, 1), rv(909, 1), rv(918, 1), rv(927, 1), rv(936, 1)
        mk1, mk2, mk, pos = rv(960, 32), rv(1248, 32), rv(1536, 32), rv(1824, 32)
        pre, ge, adj = rv(2112, 32), rv(2400, 32), rv(2688, 32)
        cnt, nbx, obx, obc = (R4[:, 2976 + 32 * j:3008 + 32 * j] for j in range(4))
        pf = R4[:, 3104:3122].rearrange("p (t j) -> p t j", t=9)
        emap = R4[0:1, 3136:3136 + NOVER + 1]
        thr_t = R0[:, 0:NE * MAXOV].rearrange("p (e j) -> p e j", e=NE)
        blk_t = R0[0:1, 2560:2560 + NOVER * NE].rearrange("p (b e) -> p b e", b=NOVER)
        slot_tab = R0[:, 4096:4096 + NBLK + 1 + CAP]
        blk0, place = slot_tab[:, 0:NBLK + 1], slot_tab[:, NBLK + 1:]
        N2 = 2 * (NT + 1)
        def r0(n, k):
            return R0[:, n:n + N2 * k].rearrange("p (t e) -> p t e", t=N2)
        o1 = 4096 + NBLK + 1 + CAP
        o2 = o1 + N2 * (NBLK + 1)
        past, inblk, atplace = r0(o1, NBLK + 1), r0(o2, NBLK), r0(o2 + N2 * NBLK, CAP)
        nblk18, place18 = R4[:, 3200:3200 + N2], R4[:, 3232:3232 + N2]
        we = [R1[:, 6144 * j:6144 * (j + 1)] for j in range(3)]
        xg = R0[:, 4096:6144].rearrange("p (s c) -> p s c", s=2)
        xgT = R0[:, 6144:6144 + KD * CAP].rearrange("p (k t) -> p k t", k=KD)
        hid = R0[:, 6912:6912 + 2 * CAP].rearrange("p (f t) -> p f t", f=2)
        sgh = R0[:, 7104:7104 + 2 * CAP].rearrange("p (f t) -> p f t", f=2)
        yb = R0[:, 0:2048].rearrange("p (s c) -> p s c", s=2)
        G2, FG = A1, B1
        G2s = work[0:NS, 0:D]
        yg = R1[:, :].rearrange("p (t j c) -> p t j c", t=NT + 1, j=2)
        yo = R0[:, 0:2 * D].rearrange("p (s c) -> p s c", s=2)
        cj = R0[:, 2 * D:3 * D]
        ms3, rstd3 = small[:, 24:26], small[:, 26:28]

        def bank(name):
            return ctx.enter_context(nc.psum_tensor(name, [P, 512], F32))

        p0, p1, p2 = bank("p0"), bank("p1"), bank("p2")
        psS = ctx.enter_context(nc.psum_tensor("psS", [P, 2, 512], F32))
        p5, p6, p7 = bank("p5"), bank("p6"), bank("p7")
        pj_bank = (p0, p1)
        ada_bank = (p0[0:9, :], p1[0:9, :], psS[0:9, 0, :], psS[0:9, 1, :])
        rg_bank = (p0, p1, p2, p6)
        g_bank = (p7, p5)
        RG_ORDER = (0, 1, 3, 2)
        lift = (p0, p1, p2, psS[:, 0, :], psS[:, 1, :], p5, p6, p7)

        s = {}

        def sem(name):
            if name not in s:
                s[name] = ctx.enter_context(nc.semaphore(name))
            return s[name]

        class Chain:

            def __init__(self, eng, name):
                self.eng, self.sm, self.base, self.n = eng, sem(name), 0, 0

            def __call__(self, ins):
                self.n += 1
                ins.then_inc(self.sm, 1)
                self.wait()

            def mark(self, ins):
                self.n += 1
                ins.then_inc(self.sm, 1)

            def wait(self):
                self.eng.wait_ge(self.sm, self.base + self.n)

            def loop(self, i, per):
                self.base, self.start = self.n + i * per, self.n
                self.at, self.n, self.per = self.n, 0, per

            def end(self, rounds):
                assert self.n == self.per, (self.n, self.per)
                self.base, self.n = 0, self.at + rounds * self.per

        for n in ("const_in misc_in crow_in c_sig c_silu cT_t cT_r ada_in0 ada_in1 ada_in2 ada_in3 b_in ada_w "
                  "ada_b ada_mm mod_r mod_st tab_in wq_in0 wq_in1 wq_in2 wq_in3 wkv_in x_in rope_in x_sq rs_r h_r "
                  "hT_t hT_e hT_c kv_mm k_r v_e kT_t kT_e pj rot v_c kd_r qk_t qk_e att_s nm_r ex_r pn_r pT_e st_u "
                  "osT_t os_r win yz yz_st init cache_st stp_st spj srot sv_c sq_t sq_e sqm sst_in socr so_r sst_r "
                  "sst_st swin_c swin_n swin_st skT_t skT_e kwin oa pT_t ssc ssm sex spn spT_t spT_e spv sosw rg_in "
                  "lw_in0 lw_in1 rg_mm rg_s rg_r o_sq om_r or_r on_r g_t g_e wo_in0 wo_in1 wo_in2 mg_mm mg_s mg_r xr_in m_c wo_mm x1_r "
                  "x1_sq rs2_r h2_r h2_t h2_e h2_st rt_mm lg_r gsh_r gex_r dv_r dex_r mk_r "
                  "rk_mm ov_n pos_r slotT_t slotT_r w13_in0 w13_in1 w2_in0 w2_in1 xg_in0 xg_in1 xgT_t xgT_e s1 "
                  "s2 hs h_a hid_r y_e y_st0 y_st1 y_done y0_r w_r stab_in oh_r yg_in0 yg_in1 yg_in2 yg_in3 yg_in4 "
                  "x2_r x2_sq rs3_r yo_r out_st0 out_st1").split():
            sem(n)

        block = ctx.enter_context(nc.Block())

        def ts(t):
            return bass.ds(t * P, P)

        @block.sync
        def _(sp):
            sp.dma_start(crow, A["c"]).then_inc(s["crow_in"], 16)
            sp.dma_start(const[:, :], A["const"]).then_inc(s["const_in"], 16)

            for j in range(ADA1):
                sp.dma_start(wada1[j], A["w_ada"][j]).then_inc(s[f"ada_in{j}"], 16)
            sp.wait_ge(s["cT_r"], 1)
            sp.dma_start(xt, A["x"][0]).then_inc(s["x_in"], 16)
            sp.dma_start(rope, A["rope"][0]).then_inc(s["rope_in"], 16)
            sp.dma_start(R1[:, H * 4096:], A["w_qkv"][:, H * 4096:]).then_inc(s["wkv_in"], 16)
            for h in range(H):
                if h == 1:
                    sp.wait_ge(s["tab_in"], 48)
                cols = slice(h * 4096, (h + 1) * 4096)
                sp.dma_start(R1[:, cols], A["w_qkv"][:, cols]).then_inc(s[f"wq_in{h}"], 16)

            def ada_weights(j):
                sp.dma_start(wada2, A["w_ada"][bass.ds(j, 1)].rearrange("o p c -> (o p) c")).then_inc(s["ada_w"], 16)

            def ada_bias(j):
                sp.dma_start(mod2, A["b_ada"][:, bass.ds(j * 512, 512)].to_broadcast([9, 512])).then_inc(s["ada_b"], 16)

            sp.wait_ge(s["ada_mm"], ADA1)
            ada_weights(ADA1)
            sp.wait_ge(s["init"], 4)
            ada_bias(ADA1)
            sp.wait_ge(s["h_r"], 1)
            sp.dma_start(xt, A["x"][1]).then_inc(s["x_in"], 16)

            def mix(i, last):
                sp.wait_ge(s["mod_r"], ADA1 + 1 + i)
                sp.dma_start(mod_dram[:, bass.ds((ADA1 + i) * 512, 512)], mod2).then_inc(s["mod_st"], 16)
                if not last:
                    ada_weights(ADA1 + 1 + i)
                    sp.wait_ge(s["mod_st"], 16 * (i + 2))
                    ada_bias(ADA1 + 1 + i)
                if not last:
                    sp.wait_ge(s["h_r"], i + 2)
                    sp.dma_start(xt, A["x"][bass.ds(i + 2, 1)].rearrange("o p c -> (o p) c")).then_inc(s["x_in"], 16)
                sp.wait_ge(s["rot"], 4 * i + 4)
                sp.dma_start(rope, A["rope"][bass.ds(i + 1, 1)].rearrange("o p c -> (o p) c")).then_inc(s["rope_in"], 16)

            with sp.Fori(0, NT - 1) as i:
                mix(i, False)
            mix(NT - 1, True)
            sp.wait_ge(s["st_u"], 4 * NT)
            sp.dma_start(O["st_p"], S.rearrange("p h e -> p (h e)")).then_inc(s["stp_st"], 16)
            sp.wait_ge(s["spj"], 1)
            sp.dma_start(R1[:, 0:4096], A["w_rg_gate"]).then_inc(s["rg_in"], 16)
            sp.wait_ge(s["spj"], 3)
            sp.dma_start(st_all, A["state"]).then_inc(s["sst_in"], 16)
            sp.wait_ge(s["spj"], H)
            sp.dma_start(kwin[0:P - 1], A["ck"][1:P]).then_inc(s["swin_c"], 16)
            sp.dma_start(vwin[0:P - 1], A["cv"][1:P]).then_inc(s["swin_c"], 16)
            sp.wait_ge(s["k_r"], NT + 1)
            sp.wait_ge(s["v_e"], NT + 1)
            sp.dma_start(kwin[P - 1:P], krot[0:NS, :]).then_inc(s["swin_n"], 16)
            sp.dma_start(vwin[P - 1:P], V2[0:NS, P:2 * P]).then_inc(s["swin_n"], 16)
            sp.wait_ge(s["swin_c"], 32)
            sp.wait_ge(s["swin_n"], 32)
            sp.dma_start(O["ks"], kwin).then_inc(s["swin_st"], 16)
            sp.dma_start(O["vs"], vwin).then_inc(s["swin_st"], 16)
            sp.wait_ge(s["yz"], 1)
            sp.dma_start(y_dram[NE * CAP:, :].rearrange("(p a) (b c) -> p (a b) c", a=ZR, b=2),
                         yzero.rearrange("p (o c) -> p o c", o=1).to_broadcast([NOVER * CAP // ZR, 2 * ZR, D // 2])
                         ).then_inc(s["yz_st"], 16)
            sp.wait_ge(s["sst_r"], H)
            sp.dma_start(O["st_s"], st_all).then_inc(s["sst_st"], 16)

            def lift_in(m, slot):
                sp.dma_start(R1[:, 8256 + 3072 * slot:8256 + 3072 * (slot + 1)],
                             A["lift"][bass.ds(m, 1)].rearrange("o p c -> (o p) c")).then_inc(s[f"lw_in{slot}"], 16)

            sp.wait_ge(s["sst_st"], 16)
            lift_in(0, 0)
            sp.wait_ge(s["rg_r"], 12)
            lift_in(1, 1)
            sp.dma_start(xt, A["x"][0]).then_inc(s["xr_in"], 16)
            sp.dma_start(wo_early, A["w_o"][:, 0:2 * D]).then_inc(s["wo_in0"], 16)
            with sp.Fori(1, KD // 2) as m2_:
                for slot in range(2):
                    sp.wait_ge(s["mg_mm"], 3 * (2 * m2_ + slot - 1))
                    lift_in(2 * m2_ + slot, slot)
            sp.wait_ge(s["mg_mm"], 3 * KD)
            for j in (1, 2):
                cols = slice((3 * j - 1) * D, (3 * j + 2) * D)
                sp.dma_start(R0[:, cols], A["w_o"][:, cols]).then_inc(s[f"wo_in{j}"], 16)

            def out_rows(t, rows=P):
                sp.wait_ge(s["h2_r"], t + 1)
                sp.dma_start(h2_dram[bass.ds(t * P, rows), :], hrow[0:rows]).then_inc(s["h2_st"], 16)

            with sp.Fori(0, NT) as t:
                sp.wait_ge(s["x1_r"], t + 1)
                sp.dma_start(xt, A["x"][bass.ds(t + 1, 1)].rearrange("o p c -> (o p) c")).then_inc(s["xr_in"], 16)
                out_rows(t)
            out_rows(NT, NS)

            def weights(e, slot):
                sp.dma_start(we[slot][:, 0:4096], A["we"][bass.ds(e, 1), :, 0:4096].rearrange("o p c -> (o p) c")
                             ).then_inc(s[f"w13_in{slot}"], 16)

            def weights2(e, slot):
                sp.dma_start(we[slot][:, 4096:6144], A["we"][bass.ds(e, 1), :, 4096:6144].rearrange("o p c -> (o p) c")
                             ).then_inc(s[f"w2_in{slot}"], 16)

            sp.wait_ge(s["wo_mm"], NT + 1)
            sp.wait_ge(s["m_c"], NT + 1)
            sp.wait_ge(s["lg_r"], NT + 1)
            sp.dma_start(slot_tab, A["slots"]).then_inc(s["stab_in"], 16)
            for slot in range(2):
                weights(slot, slot)
                weights2(slot, slot)
            with sp.Fori(1, NE // 2) as b2:
                for slot in range(2):
                    sp.wait_ge(s["s1"], 2 * b2 + slot - 1)
                    weights(2 * b2 + slot, slot)
                    sp.wait_ge(s["s2"], 2 * b2 + slot - 1)
                    weights2(2 * b2 + slot, slot)
            sp.wait_ge(s["ov_n"], 1)
            n_over = sp.value_load(nover[0:1, NOVER:NOVER + 1], min_val=0, max_val=NOVER)
            with sp.If(n_over > 0):
                with sp.Fori(0, NOVER) as b:
                    with sp.If(b < n_over):
                        e = sp.value_load(nover[0:1, bass.ds(b, 1)], min_val=0, max_val=NE - 1)
                        sp.wait_ge(s["s2"], NE + b)
                        weights(e, 0)
                        weights2(e, 0)
            def rows_out(t, slot, rows=P):
                sp.wait_ge(s["yo_r"], t + 1)
                dst = O["y"][bass.ds(t * P, rows), :]
                sp.dma_start(dst, yo[0:rows, slot]).then_inc(s[f"out_st{slot}"], 16)

            with sp.Fori(0, NT // 2) as t2_:
                rows_out(2 * t2_, 0)
                rows_out(2 * t2_ + 1, 1)
            rows_out(NT, 0, NS)
            sp.wait_ge(s["out_st0"], 16 * (NT // 2 + 1))
            sp.wait_ge(s["out_st1"], 16 * (NT // 2))
            sp.wait_ge(s["cache_st"], 32)
            sp.wait_ge(s["stp_st"], 16)
            sp.wait_ge(s["swin_st"], 32)
            sp.wait_ge(s["sst_st"], 16)
            sp.wait_ge(s["h2_st"], 16 * (NT + 1))
            sp.wait_ge(s["yz_st"], 16)

        @block.gpsimd
        def _(pool):
            link = Chain(pool, "pool_own")
            pool.dma_start(band[:, :], A["band0"]).then_inc(s["misc_in"], 16)
            pool.dma_start(sinkr[:, :], A["sinkr"]).then_inc(s["misc_in"], 16)
            pool.dma_start(sinkc[:, :], A["sinkc"]).then_inc(s["misc_in"], 16)
            pool.dma_start(tok[:, :], A["tok"]).then_inc(s["misc_in"], 16)
            pool.dma_start(rwt[:, :], A["rw"]).then_inc(s["misc_in"], 16)
            pool.dma_start(brow[:, :], A["brow"]).then_inc(s["misc_in"], 16)
            nc.gpsimd.memset(K2[:, :], 0.0).then_inc(s["init"], 1)
            nc.gpsimd.memset(V2[:, :], 0.0).then_inc(s["init"], 1)
            nc.gpsimd.memset(S, 0.0).then_inc(s["init"], 1)
            pool.wait_ge(s["ada_mm"], ADA1)
            nc.gpsimd.memset(o_all[:, NT, :], 0.0).then_inc(s["init"], 1)
            pool.wait_ge(s["const_in"], 16)

            def rstd_of(rows, done):
                link(nc.gpsimd.tensor_tensor(msb[0:rows], ms[0:rows], cst("inv_d", rows), ALU.mult))
                link(nc.gpsimd.tensor_tensor(msb[0:rows], msb[0:rows], cst("eps", rows), ALU.add))
                nc.gpsimd.tensor_tensor(rstd[0:rows], msb[0:rows], cst("half", rows)[:, 0:1], ALU.pow).then_inc(s[done], 1)

            def rs(n):
                pool.wait_ge(s["x_sq"], n)
                rstd_of(P, "rs_r")

            rs(1)
            pool.wait_ge(s["hT_e"], 2)
            nc.gpsimd.tensor_copy(hT[:, :, 0:P], hst).then_inc(s["hT_c"], 1)

            def mix(i, last):
                rs(i + 2)
                pool.wait_ge(s["hT_e"], 2 * i + 4)
                w = NS if last else P
                nc.gpsimd.tensor_copy(hT[:, :, bass.ds((i + 1) * P, w)], hst[:, :, 0:w]).then_inc(s["hT_c"], 1)

            with pool.Fori(0, NT - 1) as i:
                link.loop(i, 2)
                mix(i, False)
            link.end(NT - 1)
            mix(NT - 1, True)
            for n, (a, b) in enumerate(((0, 4 * NT), (4 * NT, 4 * NT + H))):
                pool.wait_ge(s["om_r"], n + 1)
                link(nc.gpsimd.tensor_scalar(omb[:, a:b], oms[:, a:b], 1.0 / P, EPS, ALU.mult, ALU.add))
                nc.gpsimd.tensor_tensor(orstd[:, a:b], omb[:, a:b], cst("half")[:, a:b], ALU.pow).then_inc(s["or_r"], 1)
                if n == 0:
                    pool.wait_ge(s["spj"], H)
                    nc.gpsimd.memset(yzero, 0.0).then_inc(s["yz"], 1)

            def stage(t, slot, w=P, free=True):
                if free:
                    pool.wait_ge(s["wo_mm"], t - 1)
                nc.gpsimd.tensor_copy(mst[slot][:, :, 0:w], mT[:, :, bass.ds(t * P, w)]).then_inc(s["m_c"], 1)

            def rs2(t, rows=P):
                pool.wait_ge(s["x1_sq"], t + 1)
                rstd_of(rows, "rs2_r")

            pool.wait_ge(s["mg_r"], 3 * (KD - 1))
            nc.gpsimd.tensor_copy(mst[0][:, 0:KD - 1, :], mT[:, 0:KD - 1, 0:P])
            pool.wait_ge(s["mg_r"], 3 * KD)
            nc.gpsimd.tensor_copy(mst[0][:, KD - 1:KD, :], mT[:, KD - 1:KD, 0:P]).then_inc(s["m_c"], 1)
            stage(1, 1, free=False)
            with pool.Fori(0, NT // 2 - 1) as t2_:
                link.loop(t2_, 4)
                for slot in range(2):
                    stage(2 * t2_ + slot + 2, slot)
                    rs2(2 * t2_ + slot)
            link.end(NT // 2 - 1)
            stage(NT, 0, NS)
            rs2(NT - 2)
            rs2(NT - 1)
            rs2(NT, NS)
            def gather(dst, src, col, rows, done):
                pool.indirect_dma_start(out=dst, out_offset=None, in_=src,
                                        in_offset=bass.IndirectOffsetOnAxis(ap=col[0:rows], axis=0)
                                        ).then_inc(s[done], 16)

            def gather_block(b, slot):
                gather(xg[0:CAP, slot], h2_dram, slotT[:, b:b + 1], CAP, f"xg_in{slot}")

            pool.wait_ge(s["slotT_r"], 1)
            pool.wait_ge(s["h2_st"], 16 * (NT + 1))
            for b in range(NE):
                if b >= 2:
                    pool.wait_ge(s["xgT_t"], b - 1)
                gather_block(b, b % 2)
            n_over = pool.value_load(nover[0:1, NOVER:NOVER + 1], min_val=0, max_val=NOVER)
            for b in range(NOVER):
                with pool.If(n_over > b):
                    pool.wait_ge(s["s2"], NE + b)
                    gather_block(NE + b, 0)
            pool.wait_ge(s["y_done"], 1)

            pool.wait_ge(s["pos_r"], 1)
            for t in range(NT + 1):
                r = P if t < NT else NS
                for j in range(2):
                    gather(yg[0:r, t, j], y_dram, posu[:, 2 * t + j:2 * t + j + 1], r, f"yg_in{YG[t]}")
            for t in range(NT + 1):
                pool.wait_ge(s["x2_sq"], t + 1)
                r = P if t < NT else NS
                link(nc.gpsimd.tensor_tensor(msb[0:r], ms3[0:r, t % 2:t % 2 + 1], cst("inv_d", r), ALU.mult))
                link(nc.gpsimd.tensor_tensor(msb[0:r], msb[0:r], cst("eps", r), ALU.add))
                nc.gpsimd.tensor_tensor(rstd3[0:r, t % 2:t % 2 + 1], msb[0:r], cst("half", r)[:, 0:1], ALU.pow
                                        ).then_inc(s["rs3_r"], 1)

        @block.scalar
        def _(act):
            act.wait_ge(s["crow_in"], 16)
            nc.scalar.activation(csig, crow, ACT.Sigmoid).then_inc(s["c_sig"], 1)
            act.dma_start(NGR, A["n1"].to_broadcast([P, D])).then_inc(s["tab_in"], 16)
            act.dma_start(bst, A["b_ada"][:, 0:2 * D].to_broadcast([9, 2 * D])).then_inc(s["b_in"], 16)

            def table(dst, col, rows, src=None):
                if rows == P:
                    r = mod_dram[0:1, col * D:(col + 1) * D].to_broadcast([P, D])
                else:
                    r = mod_dram[1:9, col * D:(col + 1) * D]
                act.dma_start(dst[0:rows], r).then_inc(s["tab_in"], 16)

            def square(n, first=False):
                act.wait_ge(s["x_in"], 16 * n)
                if not first:
                    act.wait_ge(s["hT_t"], 2 * (n - 1))
                nc.scalar.activation(hrow, xt, ACT.Square, accum_out=ms).then_inc(s["x_sq"], 1)

            square(1, first=True)
            act.wait_ge(s["mod_r"], ADA1)
            act.dma_start(mod_dram[:, 0:2 * D], mod).then_inc(s["mod_st"], 16)
            act.wait_ge(s["mod_st"], 16)
            table(A1, 1, P)
            table(B1, 0, P)

            def hT_out(half, n):
                act.wait_ge(s["hT_t"], 2 * n + half + 1)
                nc.scalar.copy(hst[:, 4 * half:4 * half + 4, :], (p6, p5)[half][:, :].rearrange("p (k t) -> p k t", k=4)
                               ).then_inc(s["hT_e"], 1)

            def v_out(n):
                act.wait_ge(s["k_r"], n + 1)
                nc.scalar.copy(V2[:, P:2 * P], p6[:, P:2 * P]).then_inc(s["v_e"], 1)

            hT_out(0, 0)
            hT_out(1, 0)
            act.wait_ge(s["init"], 4)
            v_out(0)
            act.wait_ge(s["const_in"], 16)

            def v_kd(n, h):
                act.wait_ge(s["rot"], n + 1)
                nc.scalar.copy(vb, pj_bank[h % 2][:, 256:384]).then_inc(s["v_c"], 1)
                nc.scalar.mul(kd, rot[:, P:2 * P], cst("kdec")[:, h:h + 1]).then_inc(s["kd_r"], 1)

            def qk_out(n):
                act.wait_ge(s["qk_t"], n + 1)
                nc.scalar.copy(qkT, p2[:, 0:384]).then_inc(s["qk_e"], 1)

            def exps(n):
                act.wait_ge(s["nm_r"], n + 1)
                for g in range(2):
                    nc.scalar.activation(pr[:, g, :], pr[:, g, :], ACT.Exp, bias=mneg[:, g:g + 1], scale=ASC,
                                         accum_out=den[:, g:g + 1])
                nc.scalar.activation(es, es, ACT.Exp).then_inc(s["ex_r"], 1)

            def probs_out(n):
                act.wait_ge(s["pT_t"], n + 1)
                nc.scalar.copy(work[:, 2560:3072], p5[:, :]).then_inc(s["pT_e"], 1)

            def mix(i, first, last):
                if last:
                    act.wait_ge(s["k_r"], NT)
                    act.dma_start(O["kp"], krot[:, :]).then_inc(s["cache_st"], 16)
                    act.wait_ge(s["v_e"], NT)
                    act.dma_start(O["vp"], V2[:, P:2 * P]).then_inc(s["cache_st"], 16)
                    act.wait_ge(s["h_r"], NT)
                    table(A1, 1, NS)
                    table(B1, 0, NS)
                for h in range(1, H):
                    n = 4 * i + h
                    v_kd(n - 1, h - 1)
                    if h == 1:
                        act.wait_ge(s["kT_t"], i + 1)
                        if not first:
                            act.wait_ge(s["kwin"], i)
                        nc.scalar.copy(K2[:, P:2 * P], p6[:, 256:384]).then_inc(s["kT_e"], 1)
                    qk_out(n - 1)
                    if h == 1:
                        square(i + 2)
                    else:
                        probs_out(n - 2)
                    if h == 3:
                        act.wait_ge(s["hT_c"], i + 1)
                        hT_out(0, i + 1)
                        hT_out(1, i + 1)
                    exps(n - 1)
                n = 4 * i + 3
                v_kd(n, 3)
                qk_out(n)
                probs_out(n - 1)
                exps(n)
                probs_out(n)
                act.wait_ge(s["win"], i + 1)
                if last:
                    act.wait_ge(s["cache_st"], 32)
                v_out(i + 1)

            mix(0, True, False)
            with act.Fori(1, NT - 1) as i:
                mix(i, False, False)
            mix(NT - 1, False, True)
            act.wait_ge(s["st_u"], 4 * NT)
            act.wait_ge(s["ada_mm"], ADA)
            nc.scalar.activation(osq, R2[:, 0:4096], ACT.Square).then_inc(s["o_sq"], 1)
            for h in range(H):
                act.wait_ge(s["srot"], h + 1)
                nc.scalar.copy(vs[:, h, :], pj_bank[h % 2][0:NS, 256:384]).then_inc(s["sv_c"], 1)
            act.wait_ge(s["sq_t"], 1)
            nc.scalar.copy(qsT, p2[:, 0:64]).then_inc(s["sq_e"], 1)

            def o_out(t, w=P):
                act.wait_ge(s["g_t"], t + 1)
                nc.scalar.copy(oretT[:, :, t * P:t * P + w], g_bank[t % 2][:, :].rearrange("p (h c) -> p h c", h=H)[:, :, 0:w]
                               ).then_inc(s["g_e"], 1)

            def rg(n):
                act.wait_ge(s["rg_mm"], n + 1)
                m = RG_ORDER[n % 4]
                nc.scalar.activation(sg[:, m, :], rg_bank[m][:, 0:CHUNK], ACT.Sigmoid).then_inc(s["rg_s"], 1)

            for t in range(NT):
                o_out(t)
            for n in range(4):
                rg(n)
            act.wait_ge(s["so_r"], H)
            nc.scalar.activation(osq8, R2[:, 4096:4608], ACT.Square).then_inc(s["o_sq"], 1)
            act.wait_ge(s["skT_t"], 1)
            nc.scalar.copy(kwT[:, 0:4], psS[:, 0, :].rearrange("p (b c) -> p b c", b=4)).then_inc(s["skT_e"], 1)
            nc.scalar.copy(kwT[:, 4:8], psS[:, 1, :].rearrange("p (b c) -> p b c", b=4)).then_inc(s["skT_e"], 1)
            rg(4)
            act.wait_ge(s["ssm"], 1)
            nc.scalar.activation(pS, pS, ACT.Exp)
            nc.scalar.activation(es8, es8, ACT.Exp).then_inc(s["sex"], 1)
            rg(5)
            rg(6)
            act.wait_ge(s["spT_t"], 1)
            nc.scalar.copy(work[:, 384:448], p5[:, 0:64]).then_inc(s["spT_e"], 1)
            rg(7)
            o_out(NT, NS)
            for n in range(8, 12):
                rg(n)
            act.wait_ge(s["h_r"], NT + 1)
            act.wait_ge(s["mod_st"], 16 * (1 + NT))
            table(G1, 2, P)
            table(A2, 4, P)
            table(B2, 3, P)
            act.wait_ge(s["swin_st"], 32)
            act.dma_start(n2row, A["n2"].to_broadcast([P, D])).then_inc(s["tab_in"], 16)

            def merge(m, slot):
                for c in range(3):
                    g = 3 * m + c
                    q = (3 * slot + c) % 2
                    bz = lift[4 * q:]
                    act.wait_ge(s["mg_mm"], g + 1)
                    for j in range(2):
                        nc.scalar.activation(g2b[:, q, j, :], bz[j][:, 0:CHUNK], ACT.Sigmoid).then_inc(s["mg_s"], 1)

            with act.Fori(0, KD // 2) as m2_:
                merge(2 * m2_, 0)
                merge(2 * m2_ + 1, 1)

            def h2T_out(t, w=P):
                act.wait_ge(s["h2_t"], t + 1)
                for j, b in enumerate((p5, p6)):
                    nc.scalar.copy(h2T[:, 4 * j:4 * j + 4, 0:w], b[:, :].rearrange("p (k t) -> p k t", k=4)[:, :, 0:w]
                                   ).then_inc(s["h2_e"], 1)

            def square2(t, rows=P, first=False):
                act.wait_ge(s["x1_r"], t + 1)
                if not first:
                    act.wait_ge(s["rs2_r"], t)
                nc.scalar.activation(ojunk[0:rows], x1[0:rows, bass.ds(t, 1), :], ACT.Square, accum_out=ms[0:rows]
                                     ).then_inc(s["x1_sq"], 1)

            square2(0, first=True)
            with act.Fori(1, NT) as t:
                h2T_out(t - 1)
                square2(t)
            act.wait_ge(s["h2_r"], NT)
            table(G1, 2, NS)
            table(A2, 4, NS)
            table(B2, 3, NS)
            h2T_out(NT - 1)
            square2(NT, NS)
            h2T_out(NT, NS)
            act.wait_ge(s["gsh_r"], 1)
            nc.scalar.activation(gsh, gsh, ACT.Exp).then_inc(s["gex_r"], 1)
            act.wait_ge(s["dv_r"], 1)
            nc.scalar.activation(dv, dv, ACT.Exp).then_inc(s["dex_r"], 1)
            act.wait_ge(s["h2_r"], NT + 1)
            table(G2, 5, P)
            act.dma_start(G2s, mod_dram[1:9, 5 * D:6 * D]).then_inc(s["tab_in"], 16)
            act.dma_start(FG, A["fg"].to_broadcast([P, D])).then_inc(s["tab_in"], 16)

            def expert(b, slot, st):
                act.wait_ge(s["s1"], b + 1)
                nc.scalar.activation(sgh, pj_bank[slot][:, 0:2 * CAP].rearrange("p (f t) -> p f t", f=2), ACT.Sigmoid
                                     ).then_inc(s["hs"], 1)
                act.wait_ge(s["s2"], b + 1)
                if st is not None:
                    act.wait_ge(s[f"y_st{slot}"], st)
                nc.scalar.copy(yb[0:CAP, slot].rearrange("p (a c) -> p a c", a=2), psS[0:CAP, :, :]).then_inc(s["y_e"], 1)
                act.wait_ge(s["y_e"], b + 1)
                act.dma_start(y_dram[bass.ds(b * CAP, CAP), :], yb[0:CAP, slot]).then_inc(s[f"y_st{slot}"], 16)

            expert(0, 0, None)
            expert(1, 1, None)
            with act.Fori(1, NE // 2) as b2:
                expert(2 * b2, 0, 16 * b2)
                expert(2 * b2 + 1, 1, 16 * b2)
            n_over = act.value_load(nover[0:1, NOVER:NOVER + 1], min_val=0, max_val=NOVER)
            with act.If(n_over > 0):
                with act.Fori(0, NOVER) as b:
                    with act.If(b < n_over):
                        expert(NE + b, 0, 8 * NE + 16 * b)
            act.wait_ge(s["y_st1"], 8 * NE)
            act.wait_ge(s["y_st0"], n_over * 16 + 8 * NE)
            nc.scalar.copy(small[:, 20:21], small[:, 16:17]).then_inc(s["y_done"], 1)
            def scale_first(t):
                r = P if t < NT else NS
                act.wait_ge(s[f"yg_in{YG[t]}"], 32 * YG.count(YG[t]))
                nc.scalar.mul(yg[0:r, t, 0], yg[0:r, t, 0], wsel[0:r, 2 * t:2 * t + 1]).then_inc(s["y0_r"], 1)

            act.wait_ge(s["w_r"], 1)
            scale_first(0)
            for t in range(NT + 1):
                if t < NT:
                    scale_first(t + 1)
                r = P if t < NT else NS
                act.wait_ge(s["x2_r"], t + 1)
                if t:
                    act.wait_ge(s["rs3_r"], t)
                nc.scalar.activation(cj[0:r], x1[0:r, t, :], ACT.Square, accum_out=ms3[0:r, t % 2:t % 2 + 1]
                                     ).then_inc(s["x2_sq"], 1)

        @block.vector
        def _(dve):
            link = Chain(dve, "dve_own")
            dve.wait_ge(s["c_sig"], 1)
            nc.vector.tensor_tensor(csig, crow, csig, ALU.mult).then_inc(s["c_silu"], 1)
            dve.wait_ge(s["cT_t"], 1)
            nc.vector.tensor_copy(cT[:, :], p2[:, 0:72]).then_inc(s["cT_r"], 1)

            dve.wait_ge(s["b_in"], 16)
            for j in range(ADA1):
                dve.wait_ge(s["ada_mm"], j + 1)
                cols = slice(j * 512, (j + 1) * 512)
                nc.vector.tensor_tensor(mod[:, cols], ada_bank[j], bst[:, cols], ALU.add).then_inc(s["mod_r"], 1)
            dve.wait_ge(s["tab_in"], 48)
            link(nc.vector.scalar_tensor_tensor(A1, A1, 1.0, NGR, ALU.add, ALU.mult))

            def h_scale(n):
                dve.wait_ge(s["rs_r"], n)
                link(nc.vector.scalar_tensor_tensor(hrow, xt, rstd, A1, ALU.mult, ALU.mult))

            def h_shift():
                nc.vector.tensor_tensor(hrow, hrow, B1, ALU.add).then_inc(s["h_r"], 1)

            def rotate(src, cols, kind, out, rows=P):
                a, b = cols
                n = (b - a) // (P if kind == "ret" else HD)
                w = P if kind == "ret" else HD
                c0 = 0 if kind == "ret" else 256
                cos = rope[0:rows, c0:c0 + w].rearrange("p (o c) -> p o c", o=1).to_broadcast([rows, n, w])
                x = src.rearrange("p (n c) -> p n c", n=n)
                link.mark(nc.vector.tensor_tensor(t1[0:rows, out:out + b - a].rearrange("p (n c) -> p n c", n=n), x, cos,
                                             ALU.mult))
                sin = rope[0:rows, c0 + w:c0 + 2 * w]
                if kind == "ret":
                    x4 = src.rearrange("p (n j t) -> p n j t", n=n, t=2)
                    o4 = t2[0:rows, out:out + b - a].rearrange("p (n j t) -> p n j t", n=n, t=2)
                    s4 = sin.rearrange("p (o j t) -> p o j t", o=1, t=2)
                    for e in range(2):
                        link.mark(nc.vector.tensor_tensor(o4[:, :, :, e], x4[:, :, :, 1 - e],
                                                     s4[:, :, :, e].to_broadcast([rows, n, HD]), ALU.mult))
                else:
                    x4 = src.rearrange("p (n t j) -> p n t j", n=n, t=2)
                    o4 = t2[0:rows, out:out + b - a].rearrange("p (n t j) -> p n t j", n=n, t=2)
                    s4 = sin.rearrange("p (o t j) -> p o t j", o=1, t=2)
                    for e in range(2):
                        link.mark(nc.vector.tensor_tensor(o4[:, :, e, :], x4[:, :, 1 - e, :],
                                                     s4[:, :, e, :].to_broadcast([rows, n, 32]), ALU.mult))

            def keys(n, last=False):
                dve.wait_ge(s["kv_mm"], n + 1)
                dve.wait_ge(s["rope_in"], 16 * (n + 1))
                rotate(p6[:, 0:P], (0, P), "swa", 0)
                link.wait()
                if last:
                    dve.wait_ge(s["cache_st"], 32)
                nc.vector.tensor_tensor(krot[:, :], t1[:, 0:P], t2[:, 0:P], ALU.add).then_inc(s["k_r"], 1)

            h_scale(1)
            h_shift()
            dve.wait_ge(s["init"], 4)
            dve.wait_ge(s["misc_in"], 96)
            keys(0)

            def rotation(n, h, i):
                dve.wait_ge(s["pj"], n + 1)
                if h == 0:
                    dve.wait_ge(s["k_r"], i + 1)
                bank_ = pj_bank[h % 2]
                rotate(bank_[:, 0:256], (0, 256), "ret", 0)
                rotate(bank_[:, 384:512], (384, 512), "swa", 256)
                link.wait()
                nc.vector.tensor_tensor(rot, t1, t2, ALU.add).then_inc(s["rot"], 1)

            def weigh(n, h):
                dve.wait_ge(s["qk_e"], n + 1)
                link(nc.vector.tensor_tensor(qdT, qkT[:, 0:P], cst("qdec")[:, h * P:(h + 1) * P], ALU.mult))
                dve.wait_ge(s["att_s"], n + 1)
                nc.vector.tensor_tensor(pr, psS[:, :, 0:256],
                                        band[:, :].rearrange("p (o c) -> p o c", o=1).to_broadcast([P, 2, 256]),
                                        ALU.add)
                link(nc.vector.tensor_tensor(attT, p2[:, 384:512], cst("dmask")[:, h * P:(h + 1) * P], ALU.mult))
                link(nc.vector.tensor_reduce(mx, pr, AX.X, ALU.max))
                sink = sinkr[:, 2 * h:2 * h + 2]
                link(nc.vector.scalar_tensor_tensor(m2, mx, ASC, sink, ALU.mult, ALU.max))
                nc.vector.tensor_scalar(mneg, m2, -1.0, None, ALU.mult)
                nc.vector.tensor_tensor(es, sink, m2, ALU.subtract).then_inc(s["nm_r"], 1)

            def normalise(n):
                dve.wait_ge(s["ex_r"], n + 1)
                link(nc.vector.tensor_tensor(den2, den, es, ALU.add))
                link(nc.vector.reciprocal(rden, den2))
                nc.vector.tensor_tensor(pr, pr, rden.rearrange("p (g o) -> p g o", o=1).to_broadcast([P, 2, 256]), ALU.mult
                                        ).then_inc(s["pn_r"], 1)

            def retention_out(n, h, i):
                dve.wait_ge(s["oa"], n + 1)
                nc.vector.tensor_copy(o_all[:, bass.ds(i, 1), h * P:(h + 1) * P],
                                      p7[:, 0:P].rearrange("p (o c) -> p o c", o=1))
                nc.vector.scalar_tensor_tensor(S[:, h, :], S[:, h, :], GAMMA[h] ** P, p7[:, P:2 * P],
                                               ALU.mult, ALU.add).then_inc(s["st_u"], 1)

            def window_out(n, h, i):
                dve.wait_ge(s["osT_t"], n + 1)
                nc.vector.tensor_copy(oswT[:, h, bass.ds(i * P, P)], p7[:, 256:384]).then_inc(s["os_r"], 1)

            def mix(i, last):
                for h in range(1, H):
                    n = 4 * i + h
                    rotation(n - 1, h - 1, i)
                    if h == 1:
                        if last:
                            dve.wait_ge(s["tab_in"], 80)
                            link(nc.vector.scalar_tensor_tensor(A1[0:NS], A1[0:NS], 1.0, NGR[0:NS], ALU.add, ALU.mult))
                        h_scale(i + 2)
                        dve.wait_ge(s["ada_mm"], ADA1 + 1 + i)
                        dve.wait_ge(s["ada_b"], 16 * (i + 1))
                        m2v = mod2.rearrange("p (g c) -> p g c", g=2)
                        nc.vector.tensor_tensor(m2v, psS[0:9, :, 256:512], m2v, ALU.add).then_inc(s["mod_r"], 1)
                    else:
                        normalise(n - 2)
                        if h == 2:
                            h_shift()
                        window_out(n - 2, h - 2, i)
                    weigh(n - 1, h - 1)
                    retention_out(n - 1, h - 1, i)
                n = 4 * i + 3
                rotation(n, 3, i)
                normalise(n - 1)
                window_out(n - 1, 2, i)
                weigh(n, 3)
                nc.vector.tensor_copy(K2[:, 0:P], K2[:, P:2 * P])
                nc.vector.tensor_copy(band[:, :], cst("band")).then_inc(s["kwin"], 1)
                normalise(n)
                retention_out(n, 3, i)
                keys(i + 1, last)
                window_out(n, 3, i)
                nc.vector.tensor_copy(V2[:, 0:P], V2[:, P:2 * P]).then_inc(s["win"], 1)

            with dve.Fori(0, NT - 1) as i:
                link.loop(i, 4 * (6 + 4 + 2) + 1 + 3)
                mix(i, False)
            link.end(NT - 1)
            mix(NT - 1, True)
            def norm_o(t, n):
                dve.wait_ge(s["or_r"], t // NT + 1)
                x = o_all[:, t:t + n, :].rearrange("p t (h c) -> p (t h) c", h=H)
                nc.vector.tensor_tensor(x, x, orstd[:, 4 * t:4 * (t + n)].rearrange("p (h o) -> p h o", o=1)
                                        .to_broadcast([P, H * n, P]), ALU.mult).then_inc(s["on_r"], 1)

            dve.wait_ge(s["k_r"], NT + 1)
            for h in range(H):
                dve.wait_ge(s["spj"], h + 1)
                if h:
                    dve.wait_ge(s["srot"], h)
                bank_ = pj_bank[h % 2][0:NS, :]
                rotate(bank_[:, 0:256], (0, 256), "ret", 0, NS)
                rotate(bank_[:, 384:512], (384, 512), "swa", 256, NS)
                link.wait()
                nc.vector.tensor_tensor(rots[:, h, :], t1[0:NS], t2[0:NS], ALU.add).then_inc(s["srot"], 1)
                if h == 0:
                    dve.wait_ge(s["o_sq"], 1)
                    nc.vector.tensor_reduce(oms[:, 0:4 * NT], osq.rearrange("p (a c) -> p a c", c=P), AX.X, ALU.add
                                            ).then_inc(s["om_r"], 1)
                if h == 2:
                    norm_o(0, NT)
            dve.wait_ge(s["srot"], H)
            dve.wait_ge(s["sv_c"], H)
            for h in range(H):
                link(nc.vector.tensor_scalar(ks8[:, h, :], rots[:, h, P:2 * P], RSC, None, ALU.mult))
                link(nc.vector.tensor_tensor_reduce(junk8, rots[:, h, 0:P], ks8[:, h, :], 1.0, 0.0, ALU.mult, ALU.add,
                                                    qk8[:, h:h + 1]))
                nc.vector.tensor_tensor(vM[:, h], vs[:, h, :].rearrange("p (o c) -> p o c", o=1).to_broadcast([NS, NS, P]),
                                        ident[0:NS, 0:NS].rearrange("p (b o) -> p b o", o=1).to_broadcast([NS, NS, P]),
                                        ALU.mult).then_inc(s["sqm"], 1)
            dve.wait_ge(s["sq_e"], 1)
            e8 = cst("eye8").rearrange("p (b c) -> p b c", b=NS)
            for h in range(H):
                nc.vector.tensor_tensor(qM[:, h], qsT[:, 8 * h:8 * h + 8].rearrange("p (o c) -> p o c", o=1)
                                        .to_broadcast([P, NS, NS]), e8, ALU.mult).then_inc(s["sqm"], 1)
            for g in range(2):
                nc.vector.tensor_scalar(qB[:, :, :, g], qsT[:, 32:64].rearrange("p (h b) -> p b h", h=H),
                                        cst("grp")[:, g:g + 1], None, ALU.mult).then_inc(s["sqm"], 1)
            dve.wait_ge(s["sst_in"], 16)
            dve.wait_ge(s["mod_st"], 16 * (1 + NT))

            def rg(n):
                m = RG_ORDER[n % 4]
                dve.wait_ge(s["rg_s"], n + 1)
                dst = oretT[:, m, (n // 4) * CHUNK:(n // 4 + 1) * CHUNK]
                link(nc.vector.tensor_tensor(sg[:, m, :], rg_bank[m][:, 0:CHUNK], sg[:, m, :], ALU.mult))
                if n == 0:
                    dve.wait_ge(s["g_e"], NT)
                if n == 8:
                    dve.wait_ge(s["g_e"], NT + 1)
                nc.vector.tensor_tensor(dst, dst, sg[:, m, :], ALU.mult).then_inc(s["rg_r"], 1)

            for h in range(H):
                dve.wait_ge(s["socr"], h + 1)
                stv = st[:, h].rearrange("p (a b) e -> p a (b e)", a=2)
                nc.vector.scalar_tensor_tensor(stv, stv, GAMMA[h], psS[:, :, :], ALU.mult, ALU.add
                                               ).then_inc(s["sst_r"], 1)
                link(nc.vector.tensor_scalar(tmp8, p7[0:NS, 0:P], GAMMA[h], None, ALU.mult))
                nc.vector.scalar_tensor_tensor(o_all[0:NS, NT, h * P:(h + 1) * P], vs[:, h, :], qk8[:, h:h + 1], tmp8,
                                               ALU.mult, ALU.add).then_inc(s["so_r"], 1)
                rg(h)
            dve.wait_ge(s["o_sq"], 2)
            nc.vector.tensor_reduce(oms[:, 4 * NT:], osq8.rearrange("p (a c) -> p a c", c=P), AX.X, ALU.add
                                    ).then_inc(s["om_r"], 1)
            rg(4)
            dve.wait_ge(s["ssc"], 1)
            sc8 = psS[0:NS, :, :].rearrange("p a (b c) -> p (a b) c", b=4)
            link(nc.vector.tensor_reduce(mx8, sc8, AX.X, ALU.max))
            link(nc.vector.tensor_scalar(m8, mx8, ASC, sinkc[:, :], ALU.mult, ALU.max))
            link(nc.vector.scalar_tensor_tensor(pS, sc8, ASC, m8.rearrange("p (b o) -> p b o", o=1).to_broadcast([NS, NS, P]),
                                                ALU.mult, ALU.subtract))
            nc.vector.tensor_scalar(es8, m8, -1.0, sinkc[:, :], ALU.mult, ALU.add).then_inc(s["ssm"], 1)
            norm_o(NT, 1)
            dve.wait_ge(s["sex"], 1)
            link(nc.vector.tensor_reduce(den8, pS, AX.X, ALU.add))
            link(nc.vector.tensor_tensor(den8, den8, es8, ALU.add))
            link(nc.vector.reciprocal(rd8, den8))
            nc.vector.tensor_tensor(pS, pS, rd8.rearrange("p (b o) -> p b o", o=1).to_broadcast([NS, NS, P]), ALU.mult
                                    ).then_inc(s["spn"], 1)
            rg(5)
            rg(6)
            rg(7)
            dve.wait_ge(s["spv"], 1)
            pv = p5[:, 64:128].rearrange("p (b h g) -> p h b g", b=NS, h=H)
            for g in range(2):
                r = slice(g * HD, (g + 1) * HD)
                nc.vector.tensor_copy(oswT[r, :, T:TA], pv[r, :, :, g]).then_inc(s["sosw"], 1)
            for n in range(8, 12):
                rg(n)

            def merge(m, slot):
                for c in range(3):
                    g = 3 * m + c
                    q = (3 * slot + c) % 2
                    by = lift[4 * q:]
                    dve.wait_ge(s["mg_s"], 2 * g + 2)
                    for j in range(2):
                        link(nc.vector.tensor_tensor(g2b[:, q, 2 + j, :], by[2 + j][:, 0:CHUNK], g2b[:, q, j, :], ALU.mult))
                    nc.vector.tensor_tensor(mT[:, bass.ds(m, 1), bass.ds(c * CHUNK, CHUNK)],
                                            g2b[:, q, 2:3, :], g2b[:, q, 3:4, :], ALU.add).then_inc(s["mg_r"], 1)

            with dve.Fori(0, KD // 2) as m2_:
                link.loop(m2_, 12)
                merge(2 * m2_, 0)
                merge(2 * m2_ + 1, 1)
            link.end(KD // 2)
            dve.wait_ge(s["tab_in"], 80 + 64)
            link(nc.vector.scalar_tensor_tensor(A2, A2, 1.0, n2row, ALU.add, ALU.mult))
            link(nc.vector.memset(lg[:, NT, :], 0.0))

            def resid(t, rows=P):
                dve.wait_ge(s["wo_mm"], t + 1)
                xd = x1[0:rows, bass.ds(t, 1), :].rearrange("p o c -> p (o c)")
                link(nc.vector.tensor_tensor(xd.rearrange("p (a c) -> p a c", a=2), psS[0:rows, :, :],
                                             G1[0:rows].rearrange("p (a c) -> p a c", a=2), ALU.mult))
                dve.wait_ge(s["xr_in"], 16 * t + 16)
                nc.vector.tensor_tensor(xd, xd, xt[0:rows], ALU.add).then_inc(s["x1_r"], 1)

            def norm2(t, rows=P, first=False):
                dve.wait_ge(s["rs2_r"], t + 1)
                if not first:
                    dve.wait_ge(s["h2_t"], t)
                    dve.wait_ge(s["h2_st"], 16 * t)
                xd = x1[0:rows, bass.ds(t, 1), :].rearrange("p o c -> p (o c)")
                link(nc.vector.scalar_tensor_tensor(hrow[0:rows], xd, rstd[0:rows], A2[0:rows], ALU.mult, ALU.mult))
                nc.vector.tensor_tensor(hrow[0:rows], hrow[0:rows], B2[0:rows], ALU.add).then_inc(s["h2_r"], 1)

            def logits(t, rows=P):
                dve.wait_ge(s["rt_mm"], t + 1)
                nc.vector.tensor_tensor(lg[0:rows, bass.ds(t, 1), :], p7[0:rows, 0:NL].rearrange("p (o c) -> p o c", o=1),
                                        brow[0:rows].rearrange("p (o c) -> p o c", o=1), ALU.add).then_inc(s["lg_r"], 1)

            resid(0)
            norm2(0, first=True)
            with dve.Fori(1, NT) as t:
                link.loop(t - 1, 2)
                resid(t)
                logits(t - 1)
                norm2(t)
            link.end(NT - 1)
            dve.wait_ge(s["tab_in"], 144 + 48)
            link(nc.vector.scalar_tensor_tensor(A2[0:NS], A2[0:NS], 1.0, n2row[0:NS], ALU.add, ALU.mult))
            resid(NT, NS)
            logits(NT - 1)
            norm2(NT, NS)
            logits(NT, NS)

            dve.wait_ge(s["lg_r"], NT + 1)
            dve.wait_ge(s["h2_st"], 16 * (NT + 1))
            tt, n9 = nc.vector.tensor_tensor, NT + 1

            def b3(a, k):
                return a.to_broadcast([P, n9, k])

            iota = cst("iota").rearrange("p (o e) -> p o e", o=1)

            def first_max(x, k, mxv, eq, cn, ix, oh):
                link(nc.vector.tensor_reduce(mxv, x, AX.X, ALU.max))
                link(tt(eq, x, b3(mxv, k), ALU.is_equal))
                link(nc.vector.scalar_tensor_tensor(cn, eq, -64.0, b3(iota[:, :, 0:k], k), ALU.mult, ALU.add))
                link(nc.vector.tensor_reduce(ix, cn, AX.X, ALU.min))
                link(tt(oh, cn, b3(ix, k), ALU.is_equal))

            g4 = lg[:, :, 0:NG]
            first_max(g4, NG, gmx, eq4, cnd4, gix, oh4)
            tt(gsh, g4, b3(gmx, NG), ALU.subtract).then_inc(s["gsh_r"], 1)
            link(tt(ep, lg[:, :, NG:NL].rearrange("p t (g j) -> p t g j", g=NG),
                    oh4.rearrange("p t (g o) -> p t g o", o=1).to_broadcast([P, n9, NG, EPG]), ALU.mult))
            link(nc.vector.tensor_reduce(ein, ep.rearrange("p t g j -> p t j g"), AX.X, ALU.add))
            first_max(ein, EPG, v1, eqv, cnd, i1, oh1)
            link(nc.vector.scalar_tensor_tensor(e2, oh1, NEG, ein, ALU.mult, ALU.add))
            first_max(e2, EPG, v2_, eqv, cnd, i2, oh2)
            tt(dv, v2_, v1, ALU.subtract).then_inc(s["dv_r"], 1)
            for mkj, ohj in ((mk1, oh1), (mk2, oh2)):
                link(tt(mkj.rearrange("p t (g j) -> p t g j", g=NG),
                        oh4.rearrange("p t (g o) -> p t g o", o=1).to_broadcast([P, n9, NG, EPG]),
                        ohj.rearrange("p t (o j) -> p t o j", o=1).to_broadcast([P, n9, NG, EPG]), ALU.mult))
            link(tt(mk, mk1, mk2, ALU.add))
            tt(mk, mk, b3(cst("valid").rearrange("p (t o) -> p t o", o=1), NE), ALU.mult).then_inc(s["mk_r"], 1)
            dve.wait_ge(s["rk_mm"], 1)
            link(nc.vector.memset(pre[:, 0, :], 0.0))
            tot = p1[:, 0:9 * NE].rearrange("p (t e) -> p t e", t=9)
            for t in range(NT):
                link(tt(pre[:, t + 1, :], pre[:, t, :], tot[:, t, :], ALU.add))
            link(tt(cnt, pre[:, NT, :], tot[:, NT, :], ALU.add))
            link(tt(pre, pre, p0[:, 0:9 * NE].rearrange("p (t e) -> p t e", t=9), ALU.add))
            link(tt(thr_t, cnt.rearrange("p (e o) -> p e o", o=1).to_broadcast([P, NE, MAXOV]),
                    cst("thr").rearrange("p (o j) -> p o j", o=1).to_broadcast([P, NE, MAXOV]), ALU.is_gt))
            link(nc.vector.tensor_reduce(nbx, thr_t, AX.X, ALU.add))
            a, b = obx, obc
            link(nc.vector.tensor_copy(a, nbx))
            for sh in (1, 2, 4, 8, 16):
                link(nc.vector.tensor_copy(b[:, 0:sh], a[:, 0:sh]))
                link(tt(b[:, sh:NE], a[:, sh:NE], a[:, 0:NE - sh], ALU.add))
                a, b = b, a
            incl, free = a, b
            link(tt(blk_t, incl[0:1].rearrange("p (o e) -> p o e", o=1).to_broadcast([1, NOVER, NE]),
                    cst("blk", 1).rearrange("p (b o) -> p b o", o=1).to_broadcast([1, NOVER, NE]), ALU.is_le))
            link(nc.vector.tensor_reduce(emap[:, 0:NOVER], blk_t, AX.X, ALU.add))
            link(nc.vector.tensor_scalar(emap[:, 0:NOVER], emap[:, 0:NOVER], float(NE - 1), None, ALU.min))
            link(nc.vector.tensor_copy(emap[:, NOVER:NOVER + 1], incl[0:1, NE - 1:NE]))
            nc.vector.tensor_copy(nover[:, :], emap).then_inc(s["ov_n"], 1)
            link(tt(free, incl, nbx, ALU.subtract))
            link(nc.vector.tensor_scalar(free, free, float(CAP), float((NE - 1) * CAP), ALU.mult, ALU.add))
            link(tt(free, free, cst("ec"), ALU.subtract))
            link(nc.vector.tensor_scalar(ge, pre, float(CAP), None, ALU.is_ge))
            link(tt(adj, ge, free.rearrange("p (o e) -> p o e", o=1).to_broadcast([P, n9, NE]), ALU.mult))
            link(tt(pos, pre, cst("ec").rearrange("p (o e) -> p o e", o=1).to_broadcast([P, n9, NE]), ALU.add))
            link(tt(pos, pos, adj, ALU.add))
            for j, mkj in enumerate((mk1, mk2)):
                link(tt(adj, pos, mkj, ALU.mult))
                link(nc.vector.tensor_reduce(pf[:, :, j:j + 1], adj, AX.X, ALU.add))
            nc.vector.tensor_copy(posu[:, :].rearrange("p (t j) -> p t j", j=2), pf).then_inc(s["pos_r"], 1)
            dve.wait_ge(s["stab_in"], 16)

            def wide(a, k):
                return a.rearrange("p (t o) -> p t o", o=1).to_broadcast([P, N2, k])

            def rows(a, k):
                return a.rearrange("p (o e) -> p o e", o=1).to_broadcast([P, N2, k])

            pf2 = R4[:, 3104:3104 + N2]
            link(tt(past, wide(pf2, NBLK + 1), rows(blk0, NBLK + 1), ALU.is_ge))
            link(nc.vector.tensor_reduce(nblk18, past, AX.X, ALU.add))
            link(nc.vector.scalar_tensor_tensor(place18, nblk18, -float(CAP), pf2, ALU.mult, ALU.add))
            link(tt(atplace, wide(place18, CAP), rows(place, CAP), ALU.is_equal))
            link(tt(inblk, past[:, :, 0:NBLK], past[:, :, 1:NBLK + 1], ALU.subtract))
            tokw = tok[:, :].rearrange("p (t o) -> p t o", o=1).to_broadcast([P, n9, 2 * NBLK])
            in9 = R0[:, o2:o2 + N2 * NBLK].rearrange("p (t e) -> p t e", t=n9)
            tt(in9, in9, tokw, ALU.mult).then_inc(s["oh_r"], 1)
            dve.wait_ge(s["gex_r"], 1)
            link(nc.vector.tensor_reduce(gsum, gsh, AX.X, ALU.add))
            link(nc.vector.reciprocal(pgr, gsum))
            dve.wait_ge(s["dex_r"], 1)
            link(nc.vector.tensor_scalar(v1, dv, 1.0, None, ALU.add))
            link(nc.vector.reciprocal(v2_, v1))
            wv = wsel[:, :].rearrange("p (t j) -> p t j", j=2)
            link(tt(wv[:, :, 0:1], pgr, v2_, ALU.mult))
            tt(wv[:, :, 1:2], wv[:, :, 0:1], dv, ALU.mult).then_inc(s["w_r"], 1)
            dve.wait_ge(s["slotT_t"], 1)
            nc.vector.tensor_copy(slotT[:, :], p2[0:CAP, 0:NBLK]).then_inc(s["slotT_r"], 1)

            def turn_out(b):
                dve.wait_ge(s["xgT_t"], b + 1)
                for j, bk in enumerate((p5, p6)):
                    nc.vector.tensor_copy(xgT[:, 4 * j:4 * j + 4, :], bk[:, 0:4 * CAP].rearrange("p (k t) -> p k t", k=4)
                                          ).then_inc(s["xgT_e"], 1)

            def hidden(b, slot):
                bk = pj_bank[slot][:, 0:4 * CAP].rearrange("p (f t) -> p f t", f=4)
                dve.wait_ge(s["hs"], b + 1)
                nc.vector.tensor_tensor(hid, bk[:, 0:2, :], sgh, ALU.mult).then_inc(s["h_a"], 1)
                dve.wait_ge(s["h_a"], b + 1)
                nc.vector.tensor_tensor(hid, hid, bk[:, 2:4, :], ALU.mult).then_inc(s["hid_r"], 1)

            turn_out(0)
            with dve.Fori(0, NE // 2 - 1) as b2:
                for slot in range(2):
                    hidden(2 * b2 + slot, slot)
                    turn_out(2 * b2 + slot + 1)
            hidden(NE - 2, 0)
            turn_out(NE - 1)
            hidden(NE - 1, 1)
            n_over = dve.value_load(nover[0:1, NOVER:NOVER + 1], min_val=0, max_val=NOVER)
            with dve.If(n_over > 0):
                with dve.Fori(0, NOVER) as b:
                    with dve.If(b < n_over):
                        turn_out(NE + b)
                        hidden(NE + b, 0)
            dve.wait_ge(s["tab_in"], 192 + 48)

            def combine(t):
                r = P if t < NT else NS
                dve.wait_ge(s["y0_r"], t + 1)
                y0, y1, x = yg[0:r, t, 0], yg[0:r, t, 1], x1[0:r, t, :]
                link(nc.vector.scalar_tensor_tensor(y0, y1, wsel[0:r, 2 * t + 1:2 * t + 2], y0, ALU.mult, ALU.add))
                link(nc.vector.tensor_tensor(y0, y0, G2 if t < NT else G2s, ALU.mult))
                nc.vector.tensor_tensor(x, x, y0, ALU.add).then_inc(s["x2_r"], 1)

            def finish(t):
                r = P if t < NT else NS
                dve.wait_ge(s["rs3_r"], t + 1)
                if t >= 2:
                    dve.wait_ge(s[f"out_st{t % 2}"], 16 * (t // 2))
                nc.vector.scalar_tensor_tensor(yo[0:r, t % 2], x1[0:r, t, :], rstd3[0:r, t % 2:t % 2 + 1], FG[0:r],
                                               ALU.mult, ALU.mult).then_inc(s["yo_r"], 1)

            combine(0)
            for t in range(1, NT + 1):
                combine(t)
                finish(t - 1)
            finish(NT)

        @block.tensor
        def _(pe):
            mm = nc.tensor.matmul
            pe.wait_ge(s["const_in"], 16)
            pe.wait_ge(s["c_silu"], 1)
            for k in range(KD):
                last = nc.tensor.transpose(p2[:, 9 * k:9 * k + 9], csig[:, k * P:(k + 1) * P], ident[0:9, 0:9])
            last.then_inc(s["cT_t"], 1)
            pe.wait_ge(s["cT_r"], 1)
            cTv = cT[:, :].rearrange("p (k c) -> p k c", k=KD)

            for j in range(ADA1):
                pe.wait_ge(s[f"ada_in{j}"], 16)
                w = wada1[j].rearrange("p (k c) -> p k c", k=KD)
                for k in range(KD):
                    last = mm(ada_bank[j], cTv[:, k, :], w[:, k, :], start=k == 0, stop=k == KD - 1)
                last.then_inc(s["ada_mm"], 1)

            def h_turn(half):
                for k in range(4):
                    kk = 4 * half + k
                    last = nc.tensor.transpose((p6, p5)[half][:, k * P:(k + 1) * P], hrow[:, kk * P:(kk + 1) * P], ident)
                last.then_inc(s["hT_t"], 1)

            def kv(ks):
                for k in ks:
                    last = mm(p6[:, 0:256], hst[:, k, :], wkv[:, k, :], start=k == 0, stop=k == KD - 1)
                if k == KD - 1:
                    last.then_inc(s["kv_mm"], 1)

            pe.wait_ge(s["h_r"], 1)
            h_turn(0)
            h_turn(1)
            pe.wait_ge(s["hT_e"], 2)
            pe.wait_ge(s["wkv_in"], 16)
            kv(range(KD))

            def turn_qk(n, h):
                pe.wait_ge(s["rot"], n + 1)
                for j in range(3):
                    last = nc.tensor.transpose(p2[:, j * P:(j + 1) * P], rot[:, j * P:(j + 1) * P], ident)
                last.then_inc(s["qk_t"], 1)

            def scores(n, i):
                pe.wait_ge(s["qk_e"], n + 1)
                mm(p2[:, 384:512], qkT[:, P:2 * P], qkT[:, 0:P], start=True, stop=True)
                pe.wait_ge(s["kT_e"], i + 1)
                for g in range(2):
                    r = slice(g * HD, (g + 1) * HD)
                    last = mm(psS[:, g, 0:256], qkT[r, 256:384], K2[r, :], start=True, stop=True)
                last.then_inc(s["att_s"], 1)

            def outputs(n, h):
                pe.wait_ge(s["v_c"], n + 1)
                pe.wait_ge(s["kd_r"], n + 1)
                pe.wait_ge(s["nm_r"], n + 1)
                mm(p7[:, 0:P], attT, vb, start=True, stop=False)
                mm(p7[:, 0:P], qdT, S[:, h, :], start=False, stop=True)
                mm(p7[:, P:2 * P], kd, vb, start=True, stop=True).then_inc(s["oa"], 1)

            def turn_probs(n):
                pe.wait_ge(s["pn_r"], n + 1)
                for g in range(2):
                    for b in range(2):
                        last = nc.tensor.transpose(p5[:, (2 * g + b) * P:(2 * g + b + 1) * P],
                                                   pr[:, g, b * P:(b + 1) * P], ident)
                last.then_inc(s["pT_t"], 1)

            def window(n, i):
                pe.wait_ge(s["pT_e"], n + 1)
                pe.wait_ge(s["st_u"], n + 1)
                pe.wait_ge(s["v_e"], i + 1)
                for g in range(2):
                    r = slice(g * HD, (g + 1) * HD)
                    for b in range(2):
                        last = mm(p7[r, 256:384], V2[:, b * P + g * HD:b * P + (g + 1) * HD], prT[:, g, b, :],
                                  start=b == 0, stop=b == 1)
                last.then_inc(s["osT_t"], 1)

            def project_h(h, ks, rows=P, done="pj"):
                for k in ks:
                    last = mm(pj_bank[h % 2][0:rows, :], hst[:, k, 0:rows], wqh[:, h, k, :], start=k == 0, stop=k == KD - 1)
                if k == KD - 1:
                    last.then_inc(s[done], 1)

            def ada_later(i):
                pe.wait_ge(s["ada_w"], 16 * (i + 1))
                w = wada2.rearrange("p (k c) -> p k c", k=KD)
                for g in range(2):
                    for k in range(KD):
                        last = mm(psS[0:9, g, 256:512], cTv[:, k, :], w[:, k, g * 256:(g + 1) * 256],
                                  start=k == 0, stop=k == KD - 1)
                last.then_inc(s["ada_mm"], 1)

            def mix(i, last_):
                for h in range(1, H):
                    n = 4 * i + h
                    pe.wait_ge(s[f"wq_in{h}"], 16)
                    project_h(h, (0, 1))
                    if h == 1:
                        pe.wait_ge(s["k_r"], i + 1)
                        pe.wait_ge(s["v_e"], i + 1)
                        nc.tensor.transpose(p6[:, 256:384], krot[:, :], ident).then_inc(s["kT_t"], 1)
                    project_h(h, (2, 3))
                    turn_qk(n - 1, h - 1)
                    if h > 1:
                        turn_probs(n - 2)
                    else:
                        ada_later(i)
                    project_h(h, (4, 5))
                    if h > 1:
                        window(n - 2, i)
                    else:
                        pe.wait_ge(s["mod_r"], ADA1 + 1 + i)
                    scores(n - 1, i)
                    project_h(h, (6, 7))
                    outputs(n - 1, h - 1)
                n = 4 * i + 3
                rows, done = (NS, "spj") if last_ else (P, "pj")
                pe.wait_ge(s["h_r"], i + 2)
                h_turn(0)
                h_turn(1)
                pe.wait_ge(s["hT_e"], 2 * i + 3)
                project_h(0, (0, 1), rows, done)
                turn_qk(n, 3)
                project_h(0, (2, 3), rows, done)
                pe.wait_ge(s["hT_e"], 2 * i + 4)
                turn_probs(n - 1)
                project_h(0, (4, 5), rows, done)
                window(n - 1, i)
                scores(n, i)
                kv(range(KD))
                outputs(n, 3)
                project_h(0, (6,), rows, done)
                turn_probs(n)
                project_h(0, (7,), rows, done)
                window(n, i)

            pe.wait_ge(s["wq_in0"], 16)
            project_h(0, range(KD))
            with pe.Fori(0, NT - 1) as i:
                mix(i, False)
            mix(NT - 1, True)
            for h in range(1, H):
                if h >= 2:
                    pe.wait_ge(s["sv_c"], h - 1)
                project_h(h, range(KD), NS, "spj")
            pe.wait_ge(s["srot"], H)
            pe.wait_ge(s["nm_r"], 4 * NT)
            for h in range(H):
                nc.tensor.transpose(p2[:, 8 * h:8 * h + 8], rots[:, h, 0:P], ident[0:NS, 0:NS])
                last = nc.tensor.transpose(p2[:, 32 + 8 * h:40 + 8 * h], rots[:, h, 256:384], ident[0:NS, 0:NS])
            last.then_inc(s["sq_t"], 1)

            def turn_o(t, rows=P):
                pe.wait_ge(s["on_r"], t // NT + 1)
                if t >= 2:
                    pe.wait_ge(s["g_e"], t - 1)
                for h in range(H):
                    last = nc.tensor.transpose(g_bank[t % 2][:, h * P:h * P + rows], o_all[0:rows, t, h * P:(h + 1) * P],
                                               ident[0:rows, 0:rows])
                last.then_inc(s["g_t"], 1)

            def rg(n):
                c, m = n // 4, RG_ORDER[n % 4]
                if n >= 4:
                    pe.wait_ge(s["rg_r"], n - 3)
                if n == 0:
                    pe.wait_ge(s["sv_c"], H)
                    pe.wait_ge(s["rg_in"], 16)
                    pe.wait_ge(s["hT_c"], NT + 1)
                    pe.wait_ge(s["v_e"], NT + 1)
                if n == 3:
                    pe.wait_ge(s["sq_e"], 1)
                for k in range(KD):
                    last = mm(rg_bank[m][:, 0:CHUNK], wrg[:, k, m * P:(m + 1) * P],
                              hT[:, k, c * CHUNK:(c + 1) * CHUNK], start=k == 0, stop=k == KD - 1)
                last.then_inc(s["rg_mm"], 1)

            pe.wait_ge(s["os_r"], 4 * NT)
            for t in range(NT):
                turn_o(t)
            pe.wait_ge(s["sst_in"], 16)
            pe.wait_ge(s["sqm"], 2 * H + 2)
            pe.wait_ge(s["g_e"], NT)
            for h in range(H):
                if h:
                    pe.wait_ge(s["sst_r"], h)
                    pe.wait_ge(s["so_r"], h)
                for b in range(NS):
                    mm(p7[0:NS, 0:P], qM[:, h, b, :], st[:, h, b, :], start=b == 0, stop=b == NS - 1)
                for a in range(2):
                    last = mm(psS[:, a, :], ks8[:, h, :], vM[:, h, 4 * a:4 * a + 4, :], start=True, stop=True)
                last.then_inc(s["socr"], 1)
                rg(h)
            pe.wait_ge(s["swin_c"], 32)
            pe.wait_ge(s["swin_n"], 32)
            pe.wait_ge(s["sst_r"], H)
            for b in range(NS):
                last = nc.tensor.transpose(psS[:, b // 4, (b % 4) * P:(b % 4 + 1) * P], kwin[:, b, :], ident)
            last.then_inc(s["skT_t"], 1)
            rg(4)
            pe.wait_ge(s["skT_e"], 2)
            for b in range(NS):
                last = mm(psS[0:NS, b // 4, (b % 4) * P:(b % 4 + 1) * P], qB[:, b].rearrange("p h g -> p (h g)"),
                          kwT[:, b, :], start=True, stop=True)
            last.then_inc(s["ssc"], 1)
            rg(5)
            rg(6)
            pe.wait_ge(s["spn"], 1)
            for b in range(NS):
                last = nc.tensor.transpose(p5[:, 8 * b:8 * b + 8], pS[:, b, :], ident[0:NS, 0:NS])
            last.then_inc(s["spT_t"], 1)
            rg(7)
            pe.wait_ge(s["spT_e"], 1)
            for b in range(NS):
                last = mm(p5[:, 64 + 8 * b:72 + 8 * b], vwin[:, b, :], pTs[:, b, :], start=True, stop=True)
            last.then_inc(s["spv"], 1)
            turn_o(NT, NS)
            for n in range(8, 12):
                rg(n)

            def merge(m2_, slot, free):
                pe.wait_ge(s[f"lw_in{slot}"], 16 * (m2_ + 1))
                for c in range(3):
                    g = 3 * (2 * m2_ + slot) + c
                    if free or 3 * slot + c >= 2:
                        pe.wait_ge(s["mg_r"], g - 1)
                    elif c == 0:
                        pe.wait_ge(s["rg_r"], 12)
                        pe.wait_ge(s["sosw"], 2)
                    bs = lift[4 * ((3 * slot + c) % 2):]
                    cols = bass.ds(c * CHUNK, CHUNK)
                    for j in range(2):
                        for k in range(KD):
                            mm(bs[j][:, 0:CHUNK], wl[:, slot, 8 * j + k, :], hT[:, k, cols], start=k == 0, stop=k == KD - 1)
                    for j, src in enumerate((oretT, oswT)):
                        for k in range(H):
                            last = mm(bs[2 + j][:, 0:CHUNK], wl[:, slot, 16 + 4 * j + k, :], src[:, k, cols],
                                      start=k == 0, stop=k == H - 1)
                    last.then_inc(s["mg_mm"], 1)

            merge(0, 0, False)
            merge(0, 1, False)
            with pe.Fori(1, KD // 2) as m2_:
                merge(m2_, 0, True)
                merge(m2_, 1, True)

            def project(t, slot, part, rows=P, first=False):
                if part == 0:
                    pe.wait_ge(s["m_c"], t + 1)
                    if not first:
                        pe.wait_ge(s["x1_r"], t)
                for kk in ((0, 1), (2, 3, 4), (5, 6, 7))[part]:
                    if first and kk in (2, 5):
                        pe.wait_ge(s[f"wo_in{part}"], 16)
                    for n in range(2):
                        last = mm(psS[0:rows, n, :], mst[slot][:, kk, 0:rows], wo[kk][:, n * 512:(n + 1) * 512],
                                  start=kk == 0, stop=kk == KD - 1)
                if part == 2:
                    last.then_inc(s["wo_mm"], 1)

            def router_turn(t, rows=P):
                pe.wait_ge(s["h2_r"], t + 1)
                for k in range(KD):
                    last = nc.tensor.transpose((p5, p6)[k // 4][:, (k % 4) * P:(k % 4) * P + rows],
                                               hrow[0:rows, k * P:(k + 1) * P], ident[0:rows, 0:rows])
                last.then_inc(s["h2_t"], 1)

            def router(t, rows=P):
                pe.wait_ge(s["h2_e"], 2 * t + 2)
                for k in range(KD):
                    last = mm(p7[0:rows, 0:NL], h2T[:, k, 0:rows], rwt[:, k * NL:(k + 1) * NL], start=k == 0, stop=k == KD - 1)
                last.then_inc(s["rt_mm"], 1)

            def out(t, slot, rows=P):
                project(t, slot, 0, rows)
                project(t, slot, 1, rows)
                router_turn(t - 1)
                project(t, slot, 2, rows)
                router(t - 1)

            pe.wait_ge(s["mg_r"], 3 * KD)
            pe.wait_ge(s["wo_in0"], 16)
            for part in range(3):
                project(0, 0, part, first=True)
            out(1, 1)
            with pe.Fori(1, NT // 2) as t2_:
                for slot in range(2):
                    out(2 * t2_ + slot, slot)
            out(NT, 0, NS)
            router_turn(NT, NS)
            router(NT, NS)
            pe.wait_ge(s["mk_r"], 1)
            mkf = R4[:, 1536:1536 + 9 * NE]
            mm(p0[:, 0:9 * NE], cst("tri"), mkf, start=True, stop=True)
            mm(p1[:, 0:9 * NE], cst("ones"), mkf, start=True, stop=True).then_inc(s["rk_mm"], 1)
            pe.wait_ge(s["oh_r"], 1)
            for j in range(2 * (NT + 1)):
                last = mm(p2[0:CAP, 0:NBLK], atplace[:, j, :], inblk[:, j, :], start=j == 0, stop=j == 2 * NT + 1)
            last.then_inc(s["slotT_t"], 1)

            def turn(b, slot, n):
                pe.wait_ge(s[f"xg_in{slot}"], 16 * n)
                for k in range(KD):
                    last = nc.tensor.transpose((p5, p6)[k // 4][:, (k % 4) * CAP:(k % 4 + 1) * CAP],
                                               xg[0:CAP, slot, k * P:(k + 1) * P], ident[0:CAP, 0:CAP])
                last.then_inc(s["xgT_t"], 1)

            def up(b, slot, n):
                pe.wait_ge(s[f"w13_in{slot}"], 16 * n)
                pe.wait_ge(s["xgT_e"], 2 * b + 2)
                for f in range(4):
                    for k in range(KD):
                        c0 = (f // 2) * 2048 + k * DE + (f % 2) * P
                        last = mm(pj_bank[slot][:, f * CAP:(f + 1) * CAP], we[slot][:, c0:c0 + P], xgT[:, k, :],
                                  start=k == 0, stop=k == KD - 1)
                last.then_inc(s["s1"], 1)

            def down(b, slot, n):
                pe.wait_ge(s[f"w2_in{slot}"], 16 * n)
                pe.wait_ge(s["hid_r"], b + 1)
                for nn in range(2):
                    for f in range(2):
                        c0 = 4096 + f * D + nn * 512
                        last = mm(psS[0:CAP, nn, :], hid[:, f, :], we[slot][:, c0:c0 + 512], start=f == 0, stop=f == 1)
                last.then_inc(s["s2"], 1)

            turn(0, 0, 1)
            pe.wait_ge(s["ov_n"], 1)
            with pe.Fori(0, NE // 2 - 1) as b2:
                for slot in range(2):
                    b = 2 * b2 + slot
                    up(b, slot, b2 + 1)
                    turn(b + 1, 1 - slot, b2 + 1 + slot)
                    down(b, slot, b2 + 1)
            up(NE - 2, 0, NE // 2)
            turn(NE - 1, 1, NE // 2)
            down(NE - 2, 0, NE // 2)
            up(NE - 1, 1, NE // 2)
            down(NE - 1, 1, NE // 2)
            n_over = pe.value_load(nover[0:1, NOVER:NOVER + 1], min_val=0, max_val=NOVER)
            with pe.If(n_over > 0):
                with pe.Fori(0, NOVER) as b:
                    with pe.If(b < n_over):
                        turn(NE + b, 0, NE // 2 + 1 + b)
                        up(NE + b, 0, NE // 2 + 1 + b)
                        down(NE + b, 0, NE // 2 + 1 + b)


def constants():
    f = np.float32
    c = np.zeros((P, NC), f)

    def put(name, a):
        lo, hi = COLS[name]
        c[:, lo:hi] = a

    i = np.arange(P)
    ld = np.log(np.asarray(GAMMA))
    put("ident", np.eye(P))
    d = i[None, :] - i[:, None]
    put("dmask", np.concatenate([np.where(d >= 0, np.exp(ld[h] * np.maximum(d, 0)) * RSC, 0.0) for h in range(H)], 1))
    put("qdec", np.tile(np.concatenate([np.exp(ld[h] * (i + 1.0)) for h in range(H)])[None], (P, 1)))
    put("kdec", np.stack([np.exp(ld[h] * (P - 1.0 - i)) * RSC for h in range(H)], 1))
    dist = i[:, None] - (np.arange(2 * P)[None, :] - P)
    band = np.where((dist >= 0) & (dist < P), 0.0, NEG).astype(f)
    put("band", band)
    band0 = band.copy()
    band0[:, :P] = NEG
    put("tri", (i[:, None] < i[None, :]).astype(f))
    put("ones", 1.0)
    put("half", -0.5)
    put("ec", np.arange(NE) * CAP)
    put("iota", np.arange(8))
    put("thr", np.arange(1, MAXOV + 1) * CAP)
    valid = np.ones((P, NT + 1), f)
    valid[NS:, NT] = 0
    put("valid", valid)
    put("blk", np.arange(NOVER))
    put("eye8", np.tile(np.eye(8).reshape(1, 64), (P, 1)))
    put("grp", np.stack([(i < HD), (i >= HD)], 1).astype(f))
    put("inv_d", 1.0 / D)
    put("eps", EPS)
    pos = np.full((NT + 1) * P, T, np.float64)
    pos[:T] = np.arange(T)
    inv_r = (1.0 / (f(10000.0) ** np.linspace(0.0, 1.0, 64, dtype=f))).astype(f)
    inv_s = (f(10000.0) ** (-np.arange(0, HD, 2, dtype=f) / f(HD))).astype(f)
    rope = np.zeros(((NT + 1) * P, 384), f)
    ang = (pos.astype(f)[:, None] * inv_r).astype(np.float64)
    rope[:, 0:128] = np.repeat(np.cos(ang), 2, 1)
    rope[:, 128:256] = np.stack([-np.sin(ang), np.sin(ang)], 2).reshape(-1, 128)
    ang = (pos.astype(f)[:, None] * inv_s).astype(np.float64)
    rope[:, 256:320] = np.tile(np.cos(ang), (1, 2))
    rope[:, 320:384] = np.concatenate([-np.sin(ang), np.sin(ang)], 1)
    tok = ((np.arange(NT + 1)[None, :] * P + i[:, None]) * valid).astype(f)
    slots = np.tile(np.concatenate([np.arange(NBLK + 1) * CAP, np.arange(CAP) - CAP])[None], (P, 1)).astype(f)
    return c, band0, rope.reshape(NT + 1, P, 384), tok, slots


def kernel(**x):
    from concourse import bacc
    from concourse.bass_utils import run_bass_kernel_spmd

    x = {k: np.asarray(a) for k, a in x.items()}
    c, band0, rope, tok, slots = constants()
    tiles = np.zeros((NT + 1, P, D), np.float32)
    tiles[:NT] = x["x_prompt"].reshape(NT, P, D)
    tiles[NT, :NS] = x["x_sample"].reshape(NS, D)

    def ktiles(w):
        return w.reshape(-1, P, w.shape[1]).transpose(1, 0, 2)

    w_in = x["w_in"][0]
    rq, rk, rv, rg, sq, sk, sv, za, zb = np.split(w_in, np.cumsum([512, 512, 512, 512, 512, 128, 128, D])[:], axis=1)
    groups = []
    for h in range(H):
        a = slice(h * P, (h + 1) * P)
        groups.append(np.concatenate([rq[:, a], rk[:, a], rv[:, a], sq[:, h * HD:(h + 1) * HD],
                                      sq[:, (h + 4) * HD:(h + 5) * HD]], 1))
    w_qkv = np.concatenate([ktiles(g).reshape(P, -1) for g in groups] +
                           [ktiles(np.concatenate([sk, sv], 1)).reshape(P, -1)], 1)
    up_s = x["w_up_swa"][0].reshape(2, H, HD, D).transpose(1, 0, 2, 3).reshape(H * P, D)
    lift = np.concatenate([ktiles(w).reshape(P, -1, KD, P).transpose(2, 0, 1, 3)
                           for w in (za, zb, x["w_up_ret"][0], up_s)], 2).reshape(KD, P, 24 * P)
    we = np.concatenate([
        x["w1"][0].reshape(NE, KD, P, DE).transpose(0, 2, 1, 3).reshape(NE, P, -1),
        x["w3"][0].reshape(NE, KD, P, DE).transpose(0, 2, 1, 3).reshape(NE, P, -1),
        x["w2"][0].reshape(NE, 2, P, D).transpose(0, 2, 1, 3).reshape(NE, P, -1)], 2)
    sink = x["sink"][0].reshape(2, H).T.reshape(-1)
    ins = {
        "const": c, "band0": band0, "rope": rope, "tok": tok, "slots": slots, "x": tiles,
        "c": np.concatenate([x["c_prompt"], x["c_sample"]], 0),
        "w_ada": x["w_ada"][0].reshape(KD, P, ADA, 512).transpose(2, 1, 0, 3).reshape(ADA, P, KD * 512),
        "b_ada": x["b_ada"],
        "n1": x["norm1_g"], "n2": x["norm2_g"], "fg": x["final_g"].reshape(1, D),
        "w_qkv": w_qkv, "w_rg_gate": ktiles(rg).reshape(P, -1), "lift": lift,
        "w_o": ktiles(x["w_o"][0]).reshape(P, -1), "we": we,
        "rw": ktiles(np.concatenate([x["w_rg"][0], x["w_re"][0]], 1)).reshape(P, -1),
        "brow": np.tile(np.concatenate([x["b_rg"][0], x["b_re"][0]])[None], (P, 1)),
        "sinkr": np.tile(sink[None], (P, 1)), "sinkc": sink.reshape(NS, 1),
        "state": x["state_ret"][0].transpose(2, 1, 0, 3).reshape(P, -1),
        "ck": x["cache_swa_k"][0].transpose(1, 0, 2, 3).reshape(P, NS, P),
        "cv": x["cache_swa_v"][0].transpose(1, 0, 2, 3).reshape(P, NS, P),
    }
    outs = {"y": (TA, D), "st_p": (P, H * P), "st_s": (P, H * NS * P), "kp": (P, P), "vp": (P, P),
            "ks": (P, NS, P), "vs": (P, NS, P)}
    nc = bacc.Bacc("TRN2", target_bir_lowering=False, num_devices=1)
    arrays, A, O = {}, {}, {}
    for name, a in ins.items():
        a = np.ascontiguousarray(a)
        arrays[f"in_{name}"] = a
        A[name] = nc.dram_tensor(f"in_{name}", a.shape, mybir.dt.from_np(a.dtype), kind="ExternalInput").ap()
    for name, shape in outs.items():
        O[name] = nc.dram_tensor(f"out_{name}", shape, F32, kind="ExternalOutput").ap()
    build(nc, A, O)
    r = run_bass_kernel_spmd(nc, [arrays], core_ids=[0]).results[0]
    o = {name: np.asarray(r[f"out_{name}"]) for name in outs}
    return (o["y"][:T].reshape(1, T, D), o["y"][T:].reshape(NS, 1, D),
            np.ascontiguousarray(o["st_p"].reshape(P, H, P).transpose(1, 0, 2)).reshape(1, 1, H, P, P),
            np.ascontiguousarray(o["st_s"].reshape(P, H, NS, P).transpose(2, 1, 0, 3)).reshape(1, NS, H, P, P),
            o["kp"].reshape(1, 1, P, 2, HD), o["vp"].reshape(1, 1, P, 2, HD),
            np.ascontiguousarray(o["ks"].transpose(1, 0, 2)).reshape(1, NS, P, 2, HD),
            np.ascontiguousarray(o["vs"].transpose(1, 0, 2)).reshape(1, NS, P, 2, HD))
```

```python
from contextlib import ExitStack

import numpy as np

import concourse.bass as bass
from concourse import mybir

F32 = mybir.dt.float32
U32 = mybir.dt.uint32
F32R = mybir.dt.float32r
ALU = mybir.AluOpType
ACT = mybir.ActivationFunctionType
AX = mybir.AxisListType

P = 128
D = 1024
KD = D // P
T = 1024
NT = T // P
NS = 8
TA = T + NS
H = 4
HD = 64
NE = 32
NG = 4
EPG = NE // NG
DE = 256
CAP = 96
CHUNK = TA // 3
NOVER = (2 * TA) // CAP
NBLK = NE + NOVER
ZR = 16
MAXOV = (TA - 1) // CAP
EPS = 1e-6
NEG = -1e30
RSC = 128.0 ** -0.5
ASC = HD ** -0.5
ADA = 6 * D // 512
ADA1 = 2 * D // 512
NL = NG + NE
YG = (0, 1, 2, 2, 3, 3, 4, 4, 4)
GAMMA = [1.0 - 2.0 ** (-5.0 - h) for h in range(H)]

COLS, _n = {}, 0
for _name, _w in (("ident", P), ("dmask", H * P), ("qdec", H * P), ("band", 2 * P), ("tri", P), ("ones", P),
                  ("kdec", H), ("half", 36), ("ec", NE), ("iota", 8), ("thr", MAXOV), ("valid", NT + 1),
                  ("blk", NOVER), ("eye8", 64), ("grp", 2), ("inv_d", 1), ("eps", 1)):
    COLS[_name] = (_n, _n + _w)
    _n += _w
NC = _n


def build(nc, A, O):
    with ExitStack() as ctx:
        def sb(name, cols, dt=F32, rows=P):
            return ctx.enter_context(nc.sbuf_tensor(name, [rows, cols], dt))

        h2_dram = nc.dram_tensor("h2_dram", [TA, D], F32, kind="Internal").ap()
        y_dram = nc.dram_tensor("y_dram", [NBLK * CAP, D], F32, kind="Internal").ap()
        mod_dram = nc.dram_tensor("mod_dram", [9, 6 * D], F32, kind="Internal").ap()

        regions = (("R0", KD * TA), ("R1", 2304 * KD), ("R2", 9 * 512 + 2 * H * TA), ("R3", 3 * D), ("R4", 4 * D))
        with ExitStack() as same:
            R0, R1, R2, R3, R4 = (same.enter_context(nc.sbuf_tensor(n, [P, w], F32)) for n, w in regions)
        Q0, Q1, Q2, Q3, Q4 = (ctx.enter_context(nc.sbuf_tensor(n + "_rounded", [P, w], F32R)) for n, w in regions)
        const = sb("const", NC)
        work = sb("work", 3072)
        small = sb("small", 64)
        cT = sb("cT", KD * 9)
        K2 = sb("K2", 2 * P)
        V2 = sb("V2", 2 * P)
        krot = sb("krot", P)
        band = sb("band", 2 * P)
        sinkr = sb("sinkr", 2 * H)
        sinkc = sb("sinkc", 1, F32, NS)
        brow = sb("brow", NL)
        rwt = sb("rwt", KD * NL)
        slotT = sb("slotT", NBLK, U32, CAP)
        posu = sb("posu", 2 * (NT + 1), U32)
        tok = sb("tok", NT + 1)
        wsel = sb("wsel", 2 * (NT + 1))
        nover = sb("nover", NOVER + 1, U32, 1)

        def cst(name, rows=P):
            a, b = COLS[name]
            return const[0:rows, a:b]

        ident = cst("ident")
        mod = R0[0:9, 4096:4096 + 2 * D]
        wada1 = [R2[:, 4096 * j:4096 * (j + 1)] for j in range(3)] + [R0[:, 0:4096]]
        bst = work[0:9, 0:2 * D]
        crow = R4[0:9, 0:D]
        csig = R4[0:9, D:2 * D]
        hT = R0[:, :].rearrange("p (k t) -> p k t", k=KD)
        wqh = R1[:, 0:H * 4096].rearrange("p (h k c) -> p h k c", h=H, k=KD)
        wkv = R1[:, H * 4096:].rearrange("p (k c) -> p k c", k=KD)
        o_all = R2[:, 0:9 * 512].rearrange("p (t c) -> p t c", t=9)
        oswT = R2[:, 4608:4608 + H * TA].rearrange("p (h t) -> p h t", h=H)
        oretT = R2[:, 4608 + H * TA:].rearrange("p (h t) -> p h t", h=H)
        wada2 = R2[:, 4608 + H * TA:4608 + H * TA + 4096]
        mod2 = o_all[0:9, NT, :]
        yzero = R1[0:NOVER * CAP // ZR, 17472:17472 + D // 2]
        A1, B1, NGR = R3[:, 0:D], R3[:, D:2 * D], R3[:, 2 * D:3 * D]
        xt, hrow = R4[:, 0:D], R4[:, D:2 * D]
        hst = R4[:, 2 * D:3 * D].rearrange("p (k t) -> p k t", k=KD)
        rope = R4[:, 3 * D:3 * D + 384]
        S = R4[:, 3 * D + 384:3 * D + 896].rearrange("p (h e) -> p h e", h=H)
        t1, t2, rot = work[:, 0:384], work[:, 384:768], work[:, 768:1152]
        qkT, qdT, attT = work[:, 1152:1536], work[:, 1536:1664], work[:, 1664:1792]
        vb, kd = work[:, 1792:1920], work[:, 1920:2048]
        pr = work[:, 2048:2560].rearrange("p (g s) -> p g s", g=2)
        prT = work[:, 2560:3072].rearrange("p (g b t) -> p g b t", g=2, b=2)
        mneg, mx, es, den, den2, rden, m2 = (small[:, 2 * j:2 * j + 2] for j in range(7))
        ms, msb, rstd = small[:, 14:15], small[:, 15:16], small[:, 16:17]
        rots = R4[0:NS, 0:4 * 384].rearrange("p (h c) -> p h c", h=H)
        vs = R4[0:NS, 1536:2048].rearrange("p (h c) -> p h c", h=H)
        qsT = work[:, 0:64]
        qM = work[:, 64:320].rearrange("p (h b c) -> p h b c", h=H, b=NS)
        qB = work[:, 320:384].rearrange("p (b h g) -> p b h g", b=NS, h=H)
        pTs = work[:, 384:448].rearrange("p (b c) -> p b c", b=NS)
        qk8 = work[0:NS, 448:452]
        tmp8 = work[0:NS, 512:640]
        junk8 = work[0:NS, 640:768]
        ks8 = work[0:NS, 768:1280].rearrange("p (h c) -> p h c", h=H)
        pS = work[0:NS, 2048:3072].rearrange("p (b s) -> p b s", b=NS)
        mx8, m8, es8, den8, rd8 = (work[0:NS, 1280 + 8 * j:1288 + 8 * j] for j in range(5))
        st_all = R1[:, 8192:12288]
        st = st_all.rearrange("p (h b e) -> p h b e", h=H, b=NS)
        vM = R1[0:NS, 4096:8192].rearrange("p (h b e) -> p h b e", h=H, b=NS)
        kwin = R1[:, 14400:15424].rearrange("p (b c) -> p b c", b=NS)
        vwin = R1[:, 15424:16448].rearrange("p (b c) -> p b c", b=NS)
        kwT = R1[:, 16448:17472].rearrange("p (b c) -> p b c", b=NS)
        wrg = R1[:, 0:4096].rearrange("p (k c) -> p k c", k=KD)
        sg = R1[:, 12352:12352 + H * CHUNK].rearrange("p (s c) -> p s c", s=H)
        osq, osq8 = R2[:, 4608 + H * TA:4608 + H * TA + 4096], R1[:, 13760:14272]
        oms, omb, orstd = K2[:, 0:36], K2[:, 36:72], K2[:, 72:108]
        mT = R1[:, 0:KD * TA].rearrange("p (m t) -> p m t", m=KD)
        z_raw = [R1[:, 8256 + 4096 * j:8256 + 4096 * j + 2048] for j in range(2)]
        z_hi = [Q1[:, 8256 + 4096 * j + 2048:8256 + 4096 * (j + 1)] for j in range(2)]
        z_lo = [Q1[:, 8256 + 4096 * j:8256 + 4096 * j + 2048] for j in range(2)]
        wy = [R1[:, 16448:17472], R3[:, TA:TA + D]]
        h_hi = [(0, 4, Q2[:, 0:4 * TA]), (4, 7, Q4[:, 0:3 * TA]), (7, 8, Q3[:, 0:TA])]
        h_hi = [(a, b, r.rearrange("p (k t) -> p k t", t=TA)) for a, b, r in h_hi]
        hT_hi = [r[:, k - a, :] for a, b, r in h_hi for k in range(a, b)]
        hT_lo = Q0[:, :].rearrange("p (k t) -> p k t", k=KD)
        g2b = work[:, 0:2752].rearrange("p (q s c) -> p q s c", q=2, s=4)
        wo_hi = [Q1[:, 8256 + k * D:8256 + (k + 1) * D] for k in range(KD)]
        wo_lo = [Q0[:, k * D:(k + 1) * D] for k in range(KD)]
        m_hi = [r.rearrange("p (k t) -> p k t", k=KD) for r in (Q4[:, 2 * D:3 * D], Q2[:, 10 * D:11 * D])]
        m_lo = [r.rearrange("p (k t) -> p k t", k=KD) for r in (Q2[:, 9 * D:10 * D], Q2[:, 11 * D:12 * D])]
        x1 = R2[:, 0:9 * D].rearrange("p (t c) -> p t c", t=9)
        G1, A2, B2 = A1, B1, NGR
        n2row, ojunk = R1[:, 16448:17472], work[:, D:2 * D]
        h2T = R4[:, 3 * D:4 * D].rearrange("p (k t) -> p k t", k=KD)
        lg = work[:, 2048:2048 + 9 * NL].rearrange("p (t e) -> p t e", t=9)
        def rv(n, k, w=None):
            a = R4[:, n:n + 9 * k]
            return a.rearrange("p (t e) -> p t e", t=9)
        gsh, eq4, cnd4, oh4 = rv(0, 4), rv(36, 4), rv(72, 4), rv(108, 4)
        gmx, gix, gsum, pgr = rv(144, 1), rv(153, 1), rv(162, 1), rv(171, 1)
        ep = R4[:, 180:180 + 288].rearrange("p (t g j) -> p t g j", t=9, g=NG)
        ein, e2, eqv, cnd, oh1, oh2 = rv(468, 8), rv(540, 8), rv(612, 8), rv(684, 8), rv(756, 8), rv(828, 8)
        v1, i1, v2_, i2, dv = rv(900, 1), rv(909, 1), rv(918, 1), rv(927, 1), rv(936, 1)
        mk1, mk2, mk, pos = rv(960, 32), rv(1248, 32), rv(1536, 32), rv(1824, 32)
        pre, ge, adj = rv(2112, 32), rv(2400, 32), rv(2688, 32)
        cnt, nbx = R4[:, 2976:3008], R4[:, 3008:3040]
        SUM_PAD = NE // 2
        sums = [R4[:, 3264 + (SUM_PAD + NE) * j:3264 + (SUM_PAD + NE) * (j + 1)] for j in range(2)]
        pf = R4[:, 3104:3122].rearrange("p (t j) -> p t j", t=9)
        emap = R4[0:1, 3136:3136 + NOVER + 1]
        thr_t = R0[:, 0:NE * MAXOV].rearrange("p (e j) -> p e j", e=NE)
        blk_t = R0[0:1, 2560:2560 + NOVER * NE].rearrange("p (b e) -> p b e", b=NOVER)
        slot_tab = R0[:, 4096:4096 + NBLK + 1 + CAP]
        blk0, place = slot_tab[:, 0:NBLK + 1], slot_tab[:, NBLK + 1:]
        N2 = 2 * (NT + 1)
        def r0(n, k):
            return R0[:, n:n + N2 * k].rearrange("p (t e) -> p t e", t=N2)
        o1 = 4096 + NBLK + 1 + CAP
        o2 = o1 + N2 * (NBLK + 1)
        past, inblk, atplace = r0(o1, NBLK + 1), r0(o2, NBLK), r0(o2 + N2 * NBLK, CAP)
        nblk18, place18 = R4[:, 3200:3200 + N2], R4[:, 3232:3232 + N2]
        we = [R1[:, 6144 * j:6144 * (j + 1)] for j in range(3)]
        xg = R0[:, 4096:6144].rearrange("p (s c) -> p s c", s=2)
        xgT = R0[:, 6144:6144 + KD * CAP].rearrange("p (k t) -> p k t", k=KD)
        hid = R0[:, 6912:6912 + 2 * CAP].rearrange("p (f t) -> p f t", f=2)
        sgh = R0[:, 7104:7104 + 2 * CAP].rearrange("p (f t) -> p f t", f=2)
        yb = R0[:, 0:2048].rearrange("p (s c) -> p s c", s=2)
        G2, FG = A1, B1
        G2s = work[0:NS, 0:D]
        yg = R1[:, :].rearrange("p (t j c) -> p t j c", t=NT + 1, j=2)
        yo = R0[:, 0:2 * D].rearrange("p (s c) -> p s c", s=2)
        cj = R0[:, 2 * D:3 * D]
        ms3, rstd3 = small[:, 24:26], small[:, 26:28]

        def bank(name):
            return ctx.enter_context(nc.psum_tensor(name, [P, 512], F32))

        p0, p1, p2 = bank("p0"), bank("p1"), bank("p2")
        psS = ctx.enter_context(nc.psum_tensor("psS", [P, 2, 512], F32))
        p5, p6, p7 = bank("p5"), bank("p6"), bank("p7")
        pj_bank = (p0, p1)
        ada_bank = (p0[0:9, :], p1[0:9, :], psS[0:9, 0, :], psS[0:9, 1, :])
        rg_bank = (p0, p1, p2, p6)
        g_bank = (p7, p5)
        up_bank = ((p0, p2), (p1, p7))
        o_bank = ((psS[:, 0, :], psS[:, 1, :]), (p0, p1))
        RG_ORDER = (0, 1, 3, 2)
        lift = (p0, p1, p2, psS[:, 0, :], psS[:, 1, :], p5, p6, p7)

        s = {}

        def sem(name):
            if name not in s:
                s[name] = ctx.enter_context(nc.semaphore(name))
            return s[name]

        class Chain:

            def __init__(self, eng, name):
                self.eng, self.sm, self.base, self.n = eng, sem(name), 0, 0

            def __call__(self, ins):
                self.n += 1
                ins.then_inc(self.sm, 1)
                self.wait()

            def mark(self, ins):
                self.n += 1
                ins.then_inc(self.sm, 1)

            def wait(self):
                self.eng.wait_ge(self.sm, self.base + self.n)

            def loop(self, i, per):
                self.base, self.start = self.n + i * per, self.n
                self.at, self.n, self.per = self.n, 0, per

            def end(self, rounds):
                assert self.n == self.per, (self.n, self.per)
                self.base, self.n = 0, self.at + rounds * self.per

        for n in ("const_in misc_in crow_in c_sig c_silu cT_t cT_r ada_in0 ada_in1 ada_in2 ada_in3 ada_w "
                  "ada_b ada_mm mod_r mod_st tab_in wq_in0 wq_in1 wq_in2 wq_in3 wkv_in x_in rope_in x_sq rs_r h_r "
                  "hT_t hT_e hT_c kv_mm k_r v_e kT_t kT_e pj rot v_c kd_r qk_t qk_e att_s nm_r ex_r pn_r pT_e st_u "
                  "osT_t at_r win yz yz_st init cache_st stp_st spj srot sv_c sq_t sq_e sqm sst_in socr so_r sst_r "
                  "sst_st swin_c swin_st skT_t skT_e kwin oa pT_t ssc ssm sex spn spT_t spT_e spv sosw rg_in "
                  "lw_in0 lw_in1 rg_mm rg_s rg_r o_sq om_r or_r on_r g_t g_e wo_in0 wo_in1 wo_in2 mg_mm h_hi h_lo w_hi w_lo mg_s mg_r xr_in m_c m_lo wo_mm x1_r "
                  "x1_sq rs2_r h2_r h2_t h2_e h2_st rt_mm lg_r gsh_r gex_r mk_r "
                  "rk_mm ov_n pos_r slotT_t slotT_r w13_in0 w13_in1 w2_in0 w2_in1 xg_in0 xg_in1 xgT_t xgT_e s1 "
                  "s2 hs h_a hid_r y_e y_st0 y_st1 y_done y0_r w_r stab_in yg_in0 yg_in1 yg_in2 yg_in3 yg_in4 "
                  "x2_r x2_sq rs3_r yo_r out_st0 out_st1").split():
            sem(n)

        block = ctx.enter_context(nc.Block())

        @block.sync
        def _(sp):
            sp.dma_start(crow, A["c"]).then_inc(s["crow_in"], 16)
            sp.dma_start(ident, A["const"][:, 0:P]).then_inc(s["const_in"], 16)
            for j in range(ADA1):
                sp.dma_start(wada1[j], A["w_ada"][j]).then_inc(s[f"ada_in{j}"], 16)
                if j == 0:
                    sp.wait_ge(s["crow_in"], 16)
                    sp.dma_start(bst, A["b_ada"][:, 0:2 * D].to_broadcast([9, 2 * D])).then_inc(s["crow_in"], 16)
            sp.dma_start(NGR, A["n1"].to_broadcast([P, D])).then_inc(s["tab_in"], 16)
            sp.wait_ge(s["cT_r"], 1)
            sp.dma_start(xt, A["x"][0]).then_inc(s["x_in"], 16)
            sp.dma_start(const[:, P:], A["const"][:, P:]).then_inc(s["const_in"], 16)
            sp.dma_start(rope, A["rope"][0]).then_inc(s["rope_in"], 16)

            def qkv_weights(h):
                cols = slice(h * 4096, (h + 1) * 4096)
                sp.dma_start(R1[:, cols], A["w_qkv"][:, cols]).then_inc(s[f"wq_in{h}"], 16)

            def ada_weights(j):
                sp.dma_start(wada2, A["w_ada"][bass.ds(j, 1)].rearrange("o p c -> (o p) c")).then_inc(s["ada_w"], 16)

            def ada_bias(j):
                sp.dma_start(mod2, A["b_ada"][:, bass.ds(j * 512, 512)].to_broadcast([9, 512])).then_inc(s["ada_b"], 16)

            sp.dma_start(R1[:, H * 4096:], A["w_qkv"][:, H * 4096:]).then_inc(s["wkv_in"], 16)
            sp.wait_ge(s["tab_in"], 48)
            qkv_weights(0)
            qkv_weights(1)
            sp.wait_ge(s["h_r"], 1)
            sp.dma_start(xt, A["x"][1]).then_inc(s["x_in"], 16)
            sp.wait_ge(s["ada_mm"], ADA1)
            ada_weights(ADA1)
            sp.wait_ge(s["init"], 4)
            ada_bias(ADA1)
            qkv_weights(2)
            qkv_weights(3)

            def mix(i, last):
                sp.wait_ge(s["mod_r"], ADA1 + 1 + i)
                sp.dma_start(mod_dram[:, bass.ds((ADA1 + i) * 512, 512)], mod2).then_inc(s["mod_st"], 16)
                if not last:
                    ada_weights(ADA1 + 1 + i)
                    sp.wait_ge(s["mod_st"], 16 * (i + 3))
                    ada_bias(ADA1 + 1 + i)
                if not last:
                    sp.wait_ge(s["h_r"], i + 2)
                    sp.dma_start(xt, A["x"][bass.ds(i + 2, 1)].rearrange("o p c -> (o p) c")).then_inc(s["x_in"], 16)
                sp.wait_ge(s["rot"], 4 * i + 4)
                sp.dma_start(rope, A["rope"][bass.ds(i + 1, 1)].rearrange("o p c -> (o p) c")).then_inc(s["rope_in"], 16)

            with sp.Fori(0, NT - 1) as i:
                mix(i, False)
            mix(NT - 1, True)
            sp.wait_ge(s["st_u"], 4 * NT)
            sp.dma_start(O["st_p"], S.rearrange("p h e -> p (h e)")).then_inc(s["stp_st"], 16)
            sp.wait_ge(s["spj"], 1)
            sp.dma_start(R1[:, 0:4096], A["w_rg_gate"]).then_inc(s["rg_in"], 16)
            sp.wait_ge(s["spj"], 3)
            sp.dma_start(st_all, A["state"]).then_inc(s["sst_in"], 16)
            sp.wait_ge(s["spj"], H)
            sp.dma_start(kwin[0:P - 1], A["ck"][1:P]).then_inc(s["swin_c"], 16)
            sp.dma_start(vwin[0:P - 1], A["cv"][1:P]).then_inc(s["swin_c"], 16)
            sp.wait_ge(s["k_r"], NT + 1)
            sp.wait_ge(s["v_e"], NT + 1)
            sp.dma_start(kwin[P - 1:P], krot[0:NS, :]).then_inc(s["swin_c"], 16)
            sp.dma_start(vwin[P - 1:P], V2[0:NS, P:2 * P]).then_inc(s["swin_c"], 16)
            sp.wait_ge(s["swin_c"], 64)
            sp.dma_start(O["ks"], kwin).then_inc(s["swin_st"], 16)
            sp.dma_start(O["vs"], vwin).then_inc(s["swin_st"], 16)
            sp.wait_ge(s["yz"], 1)
            sp.dma_start(y_dram[NE * CAP:, :].rearrange("(p a) (b c) -> p (a b) c", a=ZR, b=2),
                         yzero.rearrange("p (o c) -> p o c", o=1).to_broadcast([NOVER * CAP // ZR, 2 * ZR, D // 2])
                         ).then_inc(s["yz_st"], 16)
            sp.wait_ge(s["sst_r"], H)
            sp.dma_start(O["st_s"], st_all).then_inc(s["sst_st"], 16)

            def lift_in(m, slot):
                for dst, a in ((z_raw[slot], 0), (wy[slot], 2048)):
                    sp.dma_start(dst, A["lift"][bass.ds(m, 1), :, a:a + dst.shape[1]].rearrange("o p c -> (o p) c")
                                 ).then_inc(s[f"lw_in{slot}"], 16)

            sp.wait_ge(s["sst_st"], 16)
            sp.wait_ge(s["sosw"], 2)
            lift_in(0, 0)
            sp.wait_ge(s["rg_r"], 12)
            lift_in(1, 1)
            with sp.Fori(1, KD // 2) as m2_:
                for slot in range(2):
                    sp.wait_ge(s["mg_mm"], 3 * (2 * m2_ + slot - 1))
                    lift_in(2 * m2_ + slot, slot)
            sp.wait_ge(s["mg_mm"], 3 * KD)
            for j in range(3):
                cols = slice(max(3 * j - 1, 0) * D, (3 * j + 2) * D)
                sp.dma_start(R0[:, cols], A["w_o"][:, cols]).then_inc(s[f"wo_in{j}"], 16)
            sp.dma_start(xt, A["x"][0]).then_inc(s["xr_in"], 16)

            def out_rows(t, rows=P):
                sp.wait_ge(s["h2_r"], t + 1)
                sp.dma_start(h2_dram[bass.ds(t * P, rows), :], hrow[0:rows]).then_inc(s["h2_st"], 16)

            with sp.Fori(0, NT) as t:
                sp.wait_ge(s["x1_r"], t + 1)
                sp.dma_start(xt, A["x"][bass.ds(t + 1, 1)].rearrange("o p c -> (o p) c")).then_inc(s["xr_in"], 16)
                out_rows(t)
            out_rows(NT, NS)

            def weights(e, slot):
                sp.dma_start(we[slot][:, 0:4096], A["we"][bass.ds(e, 1), :, 0:4096].rearrange("o p c -> (o p) c")
                             ).then_inc(s[f"w13_in{slot}"], 16)

            def weights2(e, slot):
                sp.dma_start(we[slot][:, 4096:6144], A["we"][bass.ds(e, 1), :, 4096:6144].rearrange("o p c -> (o p) c")
                             ).then_inc(s[f"w2_in{slot}"], 16)

            sp.wait_ge(s["wo_mm"], NT + 1)
            sp.wait_ge(s["m_c"], NT)
            sp.wait_ge(s["lg_r"], NT + 1)
            sp.dma_start(slot_tab, A["slots"]).then_inc(s["stab_in"], 16)
            for slot in range(2):
                weights(slot, slot)
                weights2(slot, slot)
            with sp.Fori(1, NE // 2) as b2:
                for slot in range(2):
                    sp.wait_ge(s["s1"], 2 * (2 * b2 + slot - 1))
                    weights(2 * b2 + slot, slot)
                    sp.wait_ge(s["s2"], 2 * b2 + slot - 1)
                    weights2(2 * b2 + slot, slot)
            sp.wait_ge(s["ov_n"], 1)
            n_over = sp.value_load(nover[0:1, NOVER:NOVER + 1], min_val=0, max_val=NOVER)
            with sp.If(n_over > 0):
                with sp.Fori(0, NOVER) as b:
                    with sp.If(b < n_over):
                        e = sp.value_load(nover[0:1, bass.ds(b, 1)], min_val=0, max_val=NE - 1)
                        sp.wait_ge(s["s2"], NE + b)
                        weights(e, 0)
                        weights2(e, 0)
            def rows_out(t, slot, rows=P):
                sp.wait_ge(s["yo_r"], t + 1)
                dst = O["y"][bass.ds(t * P, rows), :]
                sp.dma_start(dst, yo[0:rows, slot]).then_inc(s[f"out_st{slot}"], 16)

            with sp.Fori(0, NT // 2) as t2_:
                rows_out(2 * t2_, 0)
                rows_out(2 * t2_ + 1, 1)
            rows_out(NT, 0, NS)
            sp.wait_ge(s["out_st0"], 16 * (NT // 2 + 1))
            sp.wait_ge(s["out_st1"], 16 * (NT // 2))
            sp.wait_ge(s["cache_st"], 32)
            sp.wait_ge(s["stp_st"], 16)
            sp.wait_ge(s["swin_st"], 32)
            sp.wait_ge(s["sst_st"], 16)
            sp.wait_ge(s["h2_st"], 16 * (NT + 1))
            sp.wait_ge(s["yz_st"], 16)

        @block.gpsimd
        def _(pool):
            link = Chain(pool, "pool_own")
            pool.dma_start(band[:, :], A["band0"]).then_inc(s["misc_in"], 16)
            pool.dma_start(sinkr[:, :], A["sinkr"]).then_inc(s["misc_in"], 16)
            pool.dma_start(sinkc[:, :], A["sinkc"]).then_inc(s["misc_in"], 16)
            pool.dma_start(tok[:, :], A["tok"]).then_inc(s["misc_in"], 16)
            pool.dma_start(rwt[:, :], A["rw"]).then_inc(s["misc_in"], 16)
            pool.dma_start(brow[:, :], A["brow"]).then_inc(s["misc_in"], 16)
            nc.gpsimd.memset(K2[:, :], 0.0).then_inc(s["init"], 1)
            nc.gpsimd.memset(V2[:, :], 0.0).then_inc(s["init"], 1)
            nc.gpsimd.memset(S, 0.0).then_inc(s["init"], 1)
            pool.wait_ge(s["ada_mm"], ADA1)
            nc.gpsimd.memset(o_all[:, NT, :], 0.0).then_inc(s["init"], 1)
            pool.wait_ge(s["const_in"], 32)

            def rstd_of(rows, done):
                link(nc.gpsimd.tensor_tensor(msb[0:rows], ms[0:rows], cst("inv_d", rows), ALU.mult))
                link(nc.gpsimd.tensor_tensor(msb[0:rows], msb[0:rows], cst("eps", rows), ALU.add))
                nc.gpsimd.tensor_tensor(rstd[0:rows], msb[0:rows], cst("half", rows)[:, 0:1], ALU.pow).then_inc(s[done], 1)

            def rs(n):
                pool.wait_ge(s["x_sq"], n)
                rstd_of(P, "rs_r")

            rs(1)
            pool.wait_ge(s["hT_e"], 2)
            nc.gpsimd.tensor_copy(hT[:, :, 0:P], hst).then_inc(s["hT_c"], 1)

            def mix(i, last):
                rs(i + 2)
                pool.wait_ge(s["hT_e"], 2 * i + 4)
                w = NS if last else P
                nc.gpsimd.tensor_copy(hT[:, :, bass.ds((i + 1) * P, w)], hst[:, :, 0:w]).then_inc(s["hT_c"], 1)

            with pool.Fori(0, NT - 1) as i:
                link.loop(i, 2)
                mix(i, False)
            link.end(NT - 1)
            mix(NT - 1, True)
            for n, (a, b) in enumerate(((0, 4 * NT), (4 * NT, 4 * NT + H))):
                pool.wait_ge(s["om_r"], n + 1)
                link(nc.gpsimd.tensor_scalar(omb[:, a:b], oms[:, a:b], 1.0 / P, EPS, ALU.mult, ALU.add))
                nc.gpsimd.tensor_tensor(orstd[:, a:b], omb[:, a:b], cst("half")[:, a:b], ALU.pow).then_inc(s["or_r"], 1)
                if n == 0:
                    pool.wait_ge(s["spj"], H)
                    nc.gpsimd.memset(yzero, 0.0).then_inc(s["yz"], 1)

            def stage(t, slot, w=P, free=True):
                if free:
                    pool.wait_ge(s["wo_mm"], t - 1)
                nc.gpsimd.tensor_copy(m_hi[slot][:, :, 0:w], mT[:, :, bass.ds(t * P, w)]).then_inc(s["m_c"], 1)

            def rs2(t, rows=P):
                pool.wait_ge(s["x1_sq"], t + 1)
                rstd_of(rows, "rs2_r")

            pool.wait_ge(s["mg_r"], 3 * KD)
            stage(1, 1, free=False)
            with pool.Fori(0, NT // 2 - 1) as t2_:
                link.loop(t2_, 4)
                for slot in range(2):
                    stage(2 * t2_ + slot + 2, slot)
                    rs2(2 * t2_ + slot)
            link.end(NT // 2 - 1)
            stage(NT, 0, NS)
            rs2(NT - 2)
            rs2(NT - 1)
            rs2(NT, NS)
            def gather(dst, src, col, rows, done):
                pool.indirect_dma_start(out=dst, out_offset=None, in_=src,
                                        in_offset=bass.IndirectOffsetOnAxis(ap=col[0:rows], axis=0)
                                        ).then_inc(s[done], 16)

            def gather_block(b, slot):
                gather(xg[0:CAP, slot], h2_dram, slotT[:, b:b + 1], CAP, f"xg_in{slot}")

            pool.wait_ge(s["slotT_r"], 1)
            pool.wait_ge(s["h2_st"], 16 * (NT + 1))
            for b in range(NE):
                if b >= 2:
                    pool.wait_ge(s["xgT_t"], b - 1)
                gather_block(b, b % 2)
            n_over = pool.value_load(nover[0:1, NOVER:NOVER + 1], min_val=0, max_val=NOVER)
            for b in range(NOVER):
                with pool.If(n_over > b):
                    pool.wait_ge(s["s2"], NE + b)
                    gather_block(NE + b, 0)
            pool.wait_ge(s["y_done"], 1)

            pool.wait_ge(s["pos_r"], 1)
            for t in range(NT + 1):
                r = P if t < NT else NS
                for j in range(2):
                    gather(yg[0:r, t, j], y_dram, posu[:, 2 * t + j:2 * t + j + 1], r, f"yg_in{YG[t]}")
            for t in range(NT + 1):
                pool.wait_ge(s["x2_sq"], t + 1)
                r = P if t < NT else NS
                link(nc.gpsimd.tensor_tensor(msb[0:r], ms3[0:r, t % 2:t % 2 + 1], cst("inv_d", r), ALU.mult))
                link(nc.gpsimd.tensor_tensor(msb[0:r], msb[0:r], cst("eps", r), ALU.add))
                nc.gpsimd.tensor_tensor(rstd3[0:r, t % 2:t % 2 + 1], msb[0:r], cst("half", r)[:, 0:1], ALU.pow
                                        ).then_inc(s["rs3_r"], 1)

        @block.scalar
        def _(act):
            act.wait_ge(s["crow_in"], 16)
            nc.scalar.activation(csig, crow, ACT.Sigmoid).then_inc(s["c_sig"], 1)

            def table(dst, col, rows, src=None):
                if rows == P:
                    r = mod_dram[0:1, col * D:(col + 1) * D].to_broadcast([P, D])
                else:
                    r = mod_dram[1:9, col * D:(col + 1) * D]
                act.dma_start(dst[0:rows], r).then_inc(s["tab_in"], 16)

            def square(n, first=False):
                act.wait_ge(s["x_in"], 16 * n)
                if not first:
                    act.wait_ge(s["hT_t"], 2 * (n - 1))
                nc.scalar.activation(hrow, xt, ACT.Square, accum_out=ms).then_inc(s["x_sq"], 1)

            for n, dst in enumerate((B1, A1)):
                act.wait_ge(s["mod_r"], ADA1 // 2 * (n + 1))
                act.dma_start(mod_dram[:, n * D:(n + 1) * D], mod[:, n * D:(n + 1) * D]).then_inc(s["mod_st"], 16)
                act.wait_ge(s["mod_st"], 16 * (n + 1))
                table(dst, n, P)
                if n == 0:
                    square(1, first=True)

            def hT_out(half, n):
                act.wait_ge(s["hT_t"], 2 * n + half + 1)
                nc.scalar.copy(hst[:, 4 * half:4 * half + 4, :], (p6, p5)[half][:, :].rearrange("p (k t) -> p k t", k=4)
                               ).then_inc(s["hT_e"], 1)

            def v_out(n):
                act.wait_ge(s["k_r"], n + 1)
                nc.scalar.copy(V2[:, P:2 * P], p6[:, P:2 * P]).then_inc(s["v_e"], 1)

            hT_out(0, 0)
            hT_out(1, 0)
            act.wait_ge(s["init"], 4)
            v_out(0)
            act.wait_ge(s["const_in"], 32)

            def v_kd(n, h):
                act.wait_ge(s["rot"], n + 1)
                nc.scalar.copy(vb, pj_bank[h % 2][:, 256:384]).then_inc(s["v_c"], 1)
                nc.scalar.mul(kd, rot[:, P:2 * P], cst("kdec")[:, h:h + 1]).then_inc(s["kd_r"], 1)

            def qk_out(n):
                act.wait_ge(s["qk_t"], n + 1)
                nc.scalar.copy(qkT, p2[:, 0:384]).then_inc(s["qk_e"], 1)

            def exps(n):
                act.wait_ge(s["nm_r"], n + 1)
                for g in range(2):
                    nc.scalar.activation(pr[:, g, :], pr[:, g, :], ACT.Exp, bias=mneg[:, g:g + 1], scale=ASC,
                                         accum_out=den[:, g:g + 1])
                nc.scalar.activation(es, es, ACT.Exp).then_inc(s["ex_r"], 1)

            def probs_out(n):
                act.wait_ge(s["pT_t"], n + 1)
                nc.scalar.copy(work[:, 2560:3072], p5[:, :]).then_inc(s["pT_e"], 1)

            def mix(i, first, last):
                if last:
                    act.wait_ge(s["k_r"], NT)
                    act.dma_start(O["kp"], krot[:, :]).then_inc(s["cache_st"], 16)
                    act.wait_ge(s["v_e"], NT)
                    act.dma_start(O["vp"], V2[:, P:2 * P]).then_inc(s["cache_st"], 16)
                    act.wait_ge(s["h_r"], NT)
                    table(A1, 1, NS)
                    table(B1, 0, NS)
                for h in range(1, H):
                    n = 4 * i + h
                    v_kd(n - 1, h - 1)
                    if h == 1:
                        act.wait_ge(s["kT_t"], i + 1)
                        if not first:
                            act.wait_ge(s["kwin"], i)
                        nc.scalar.copy(K2[:, P:2 * P], p6[:, 256:384]).then_inc(s["kT_e"], 1)
                    qk_out(n - 1)
                    if h == 1:
                        square(i + 2)
                    else:
                        probs_out(n - 2)
                    if h == 3:
                        act.wait_ge(s["hT_c"], i + 1)
                        hT_out(0, i + 1)
                        hT_out(1, i + 1)
                    exps(n - 1)
                n = 4 * i + 3
                v_kd(n, 3)
                qk_out(n)
                probs_out(n - 1)
                exps(n)
                probs_out(n)
                act.wait_ge(s["win"], i + 1)
                if last:
                    act.wait_ge(s["cache_st"], 32)
                v_out(i + 1)

            mix(0, True, False)
            with act.Fori(1, NT - 1) as i:
                mix(i, False, False)
            mix(NT - 1, False, True)
            act.wait_ge(s["st_u"], 4 * NT)
            act.wait_ge(s["ada_mm"], ADA)
            nc.scalar.activation(osq, R2[:, 0:4096], ACT.Square).then_inc(s["o_sq"], 1)
            for h in range(H):
                act.wait_ge(s["srot"], h + 1)
                nc.scalar.copy(vs[:, h, :], pj_bank[h % 2][0:NS, 256:384]).then_inc(s["sv_c"], 1)
            act.wait_ge(s["sq_t"], 1)
            nc.scalar.copy(qsT, p2[:, 0:64]).then_inc(s["sq_e"], 1)

            def o_out(t, w=P):
                act.wait_ge(s["g_t"], t + 1)
                nc.scalar.copy(oretT[:, :, t * P:t * P + w], g_bank[t % 2][:, :].rearrange("p (h c) -> p h c", h=H)[:, :, 0:w]
                               ).then_inc(s["g_e"], 1)

            def rg(n):
                act.wait_ge(s["rg_mm"], n + 1)
                m = RG_ORDER[n % 4]
                nc.scalar.activation(sg[:, m, :], rg_bank[m][:, 0:CHUNK], ACT.Sigmoid).then_inc(s["rg_s"], 1)

            for t in range(NT):
                o_out(t)
            for n in range(4):
                rg(n)
            act.wait_ge(s["so_r"], H)
            nc.scalar.activation(osq8, R2[:, 4096:4608], ACT.Square).then_inc(s["o_sq"], 1)
            act.wait_ge(s["skT_t"], 1)
            nc.scalar.copy(kwT[:, 0:4], psS[:, 0, :].rearrange("p (b c) -> p b c", b=4)).then_inc(s["skT_e"], 1)
            nc.scalar.copy(kwT[:, 4:8], psS[:, 1, :].rearrange("p (b c) -> p b c", b=4)).then_inc(s["skT_e"], 1)
            rg(4)
            act.wait_ge(s["ssm"], 1)
            nc.scalar.activation(pS, pS, ACT.Exp)
            nc.scalar.activation(es8, es8, ACT.Exp).then_inc(s["sex"], 1)
            rg(5)
            rg(6)
            act.wait_ge(s["spT_t"], 1)
            nc.scalar.copy(work[:, 384:448], p5[:, 0:64]).then_inc(s["spT_e"], 1)
            rg(7)
            o_out(NT, NS)

            def h_round(c):
                cols = slice(c * CHUNK, (c + 1) * CHUNK)
                for a, b, r in h_hi:
                    last = nc.scalar.copy(r[:, :, cols], hT[:, a:b, cols])
                last.then_inc(s["h_hi"], 1)

            act.wait_ge(s["rg_mm"], 4)
            act.wait_ge(s["sosw"], 2)
            act.wait_ge(s["stp_st"], 16)
            h_round(0)
            rg(8)
            def weights_hi(n, slot, count, free=True):
                act.wait_ge(s[f"lw_in{slot}"], count)
                if free:
                    act.wait_ge(s["mg_mm"], n)
                nc.scalar.copy(z_hi[slot], z_raw[slot]).then_inc(s["w_hi"], 1)

            h_round(1)
            rg(9)
            rg(10)
            weights_hi(0, 0, 32, free=False)
            rg(11)
            h_round(2)
            def merge(m2_, slot, split=True):
                for c in range(3):
                    g = 3 * (2 * m2_ + slot) + c
                    q = (3 * slot + c) % 2
                    bz = lift[4 * q:]
                    act.wait_ge(s["mg_mm"], g + 1)
                    for j in range(2):
                        nc.scalar.activation(g2b[:, q, j, :], bz[j][:, 0:CHUNK], ACT.Sigmoid).then_inc(s["mg_s"], 1)
                    if c == 0 and split:
                        weights_hi(g, 1 - slot, 32 * (m2_ + 1 + slot))

            with act.Fori(0, KD // 2 - 1) as m2_:
                merge(m2_, 0)
                merge(m2_, 1)
            merge(KD // 2 - 1, 0)
            merge(KD // 2 - 1, 1, split=False)

            act.wait_ge(s["mg_r"], 3 * KD)
            nc.scalar.copy(m_hi[0], mT[:, :, 0:P]).then_inc(s["w_hi"], 1)
            for k in range(KD):
                if k == 5:
                    act.wait_ge(s["mod_st"], 16 * (2 + NT))
                    table(G1, 2, P)
                    table(A2, 4, P)
                    table(B2, 3, P)
                    act.dma_start(n2row, A["n2"].to_broadcast([P, D])).then_inc(s["tab_in"], 16)
                act.wait_ge(s[f"wo_in{(k + 1) // 3}"], 16)
                nc.scalar.copy(wo_hi[k], R0[:, k * D:(k + 1) * D]).then_inc(s["w_hi"], 1)

            def h2T_out(t, w=P):
                act.wait_ge(s["h2_t"], t + 1)
                for j, b in enumerate((p5, p6)):
                    nc.scalar.copy(h2T[:, 4 * j:4 * j + 4, 0:w], b[:, :].rearrange("p (k t) -> p k t", k=4)[:, :, 0:w]
                                   ).then_inc(s["h2_e"], 1)

            def square2(t, rows=P, first=False):
                act.wait_ge(s["x1_r"], t + 1)
                if not first:
                    act.wait_ge(s["rs2_r"], t)
                nc.scalar.activation(ojunk[0:rows], x1[0:rows, bass.ds(t, 1), :], ACT.Square, accum_out=ms[0:rows]
                                     ).then_inc(s["x1_sq"], 1)

            square2(0, first=True)
            with act.Fori(1, NT) as t:
                h2T_out(t - 1)
                square2(t)
            act.wait_ge(s["h2_r"], NT)
            table(G1, 2, NS)
            table(A2, 4, NS)
            table(B2, 3, NS)
            h2T_out(NT - 1)
            square2(NT, NS)
            h2T_out(NT, NS)
            act.wait_ge(s["gsh_r"], 1)
            nc.scalar.activation(gsh, gsh, ACT.Exp).then_inc(s["gex_r"], 1)
            act.wait_ge(s["gsh_r"], 2)
            nc.scalar.activation(dv, dv, ACT.Exp).then_inc(s["gex_r"], 1)
            act.wait_ge(s["h2_r"], NT + 1)
            table(G2, 5, P)
            act.dma_start(G2s, mod_dram[1:9, 5 * D:6 * D]).then_inc(s["tab_in"], 16)
            act.dma_start(FG, A["fg"].to_broadcast([P, D])).then_inc(s["tab_in"], 16)

            def expert(b, slot, st):
                for f in range(2):
                    act.wait_ge(s["s1"], 2 * b + f + 1)
                    nc.scalar.activation(sgh[:, f, :], up_bank[slot][f][:, 0:CAP], ACT.Sigmoid).then_inc(s["hs"], 1)
                act.wait_ge(s["s2"], b + 1)
                if st is not None:
                    act.wait_ge(s[f"y_st{slot}"], st)
                nc.scalar.copy(yb[0:CAP, slot].rearrange("p (a c) -> p a c", a=2), psS[0:CAP, :, :]).then_inc(s["y_e"], 1)
                act.wait_ge(s["y_e"], b + 1)
                act.dma_start(y_dram[bass.ds(b * CAP, CAP), :], yb[0:CAP, slot]).then_inc(s[f"y_st{slot}"], 16)

            expert(0, 0, None)
            expert(1, 1, None)
            with act.Fori(1, NE // 2) as b2:
                expert(2 * b2, 0, 16 * b2)
                expert(2 * b2 + 1, 1, 16 * b2)
            n_over = act.value_load(nover[0:1, NOVER:NOVER + 1], min_val=0, max_val=NOVER)
            with act.If(n_over > 0):
                with act.Fori(0, NOVER) as b:
                    with act.If(b < n_over):
                        expert(NE + b, 0, 8 * NE + 16 * b)
            act.wait_ge(s["y_st1"], 8 * NE)
            act.wait_ge(s["y_st0"], n_over * 16 + 8 * NE)
            nc.scalar.copy(small[:, 20:21], small[:, 16:17]).then_inc(s["y_done"], 1)
            def scale_first(t):
                r = P if t < NT else NS
                act.wait_ge(s[f"yg_in{YG[t]}"], 32 * YG.count(YG[t]))
                nc.scalar.mul(yg[0:r, t, 0], yg[0:r, t, 0], wsel[0:r, 2 * t:2 * t + 1]).then_inc(s["y0_r"], 1)

            act.wait_ge(s["w_r"], 1)
            scale_first(0)
            for t in range(NT + 1):
                if t < NT:
                    scale_first(t + 1)
                r = P if t < NT else NS
                act.wait_ge(s["x2_r"], t + 1)
                if t:
                    act.wait_ge(s["rs3_r"], t)
                nc.scalar.activation(cj[0:r], x1[0:r, t, :], ACT.Square, accum_out=ms3[0:r, t % 2:t % 2 + 1]
                                     ).then_inc(s["x2_sq"], 1)

        @block.vector
        def _(dve):
            link = Chain(dve, "dve_own")
            dve.wait_ge(s["c_sig"], 1)
            nc.vector.tensor_tensor(csig, crow, csig, ALU.mult).then_inc(s["c_silu"], 1)
            dve.wait_ge(s["cT_t"], 1)
            nc.vector.tensor_copy(cT[:, :], p2[:, 0:72]).then_inc(s["cT_r"], 1)

            dve.wait_ge(s["crow_in"], 32)
            for j in range(ADA1):
                dve.wait_ge(s["ada_mm"], j + 1)
                cols = slice(j * 512, (j + 1) * 512)
                nc.vector.tensor_tensor(mod[:, cols], ada_bank[j], bst[:, cols], ALU.add).then_inc(s["mod_r"], 1)
            def h_scale(n):
                dve.wait_ge(s["rs_r"], n)
                link(nc.vector.scalar_tensor_tensor(hrow, xt, rstd, A1, ALU.mult, ALU.mult))

            def h_shift():
                nc.vector.tensor_tensor(hrow, hrow, B1, ALU.add).then_inc(s["h_r"], 1)

            def rotate(src, cols, kind, out, rows=P):
                a, b = cols
                n = (b - a) // (P if kind == "ret" else HD)
                w = P if kind == "ret" else HD
                c0 = 0 if kind == "ret" else 256
                cos = rope[0:rows, c0:c0 + w].rearrange("p (o c) -> p o c", o=1).to_broadcast([rows, n, w])
                x = src.rearrange("p (n c) -> p n c", n=n)
                link.mark(nc.vector.tensor_tensor(t1[0:rows, out:out + b - a].rearrange("p (n c) -> p n c", n=n), x, cos,
                                             ALU.mult))
                sin = rope[0:rows, c0 + w:c0 + 2 * w]
                if kind == "ret":
                    x4 = src.rearrange("p (n j t) -> p n j t", n=n, t=2)
                    o4 = t2[0:rows, out:out + b - a].rearrange("p (n j t) -> p n j t", n=n, t=2)
                    s4 = sin.rearrange("p (o j t) -> p o j t", o=1, t=2)
                    for e in range(2):
                        link.mark(nc.vector.tensor_tensor(o4[:, :, :, e], x4[:, :, :, 1 - e],
                                                     s4[:, :, :, e].to_broadcast([rows, n, HD]), ALU.mult))
                else:
                    x4 = src.rearrange("p (n t j) -> p n t j", n=n, t=2)
                    o4 = t2[0:rows, out:out + b - a].rearrange("p (n t j) -> p n t j", n=n, t=2)
                    s4 = sin.rearrange("p (o t j) -> p o t j", o=1, t=2)
                    for e in range(2):
                        link.mark(nc.vector.tensor_tensor(o4[:, :, e, :], x4[:, :, 1 - e, :],
                                                     s4[:, :, e, :].to_broadcast([rows, n, 32]), ALU.mult))

            def keys(n, last=False):
                dve.wait_ge(s["kv_mm"], n + 1)
                dve.wait_ge(s["rope_in"], 16 * (n + 1))
                rotate(p6[:, 0:P], (0, P), "swa", 0)
                link.wait()
                if last:
                    dve.wait_ge(s["cache_st"], 32)
                nc.vector.tensor_tensor(krot[:, :], t1[:, 0:P], t2[:, 0:P], ALU.add).then_inc(s["k_r"], 1)

            dve.wait_ge(s["rs_r"], 1)
            dve.wait_ge(s["tab_in"], 48)
            link(nc.vector.scalar_tensor_tensor(hrow, xt, rstd, NGR, ALU.mult, ALU.mult))
            link(nc.vector.scalar_tensor_tensor(hrow, A1, 1.0, hrow, ALU.add, ALU.mult))
            h_shift()
            link(nc.vector.scalar_tensor_tensor(A1, A1, 1.0, NGR, ALU.add, ALU.mult))
            dve.wait_ge(s["init"], 4)
            dve.wait_ge(s["misc_in"], 96)
            keys(0)

            def rotation(n, h, i):
                dve.wait_ge(s["pj"], n + 1)
                if h == 0:
                    dve.wait_ge(s["k_r"], i + 1)
                bank_ = pj_bank[h % 2]
                rotate(bank_[:, 0:256], (0, 256), "ret", 0)
                rotate(bank_[:, 384:512], (384, 512), "swa", 256)
                link.wait()
                nc.vector.tensor_tensor(rot, t1, t2, ALU.add).then_inc(s["rot"], 1)

            def weigh(n, h):
                dve.wait_ge(s["qk_e"], n + 1)
                link(nc.vector.tensor_tensor(qdT, qkT[:, 0:P], cst("qdec")[:, h * P:(h + 1) * P], ALU.mult))
                dve.wait_ge(s["att_s"], n + 1)
                nc.vector.tensor_tensor(pr, psS[:, :, 0:256],
                                        band[:, :].rearrange("p (o c) -> p o c", o=1).to_broadcast([P, 2, 256]),
                                        ALU.add)
                nc.vector.tensor_tensor(attT, p2[:, 384:512], cst("dmask")[:, h * P:(h + 1) * P], ALU.mult
                                        ).then_inc(s["at_r"], 1)
                dve.wait_ge(s["at_r"], n + 1)
                link(nc.vector.tensor_reduce(mx, pr, AX.X, ALU.max))
                sink = sinkr[:, 2 * h:2 * h + 2]
                link(nc.vector.scalar_tensor_tensor(m2, mx, ASC, sink, ALU.mult, ALU.max))
                nc.vector.tensor_scalar(mneg, m2, -1.0, None, ALU.mult)
                nc.vector.tensor_tensor(es, sink, m2, ALU.subtract).then_inc(s["nm_r"], 1)

            def normalise(n):
                dve.wait_ge(s["ex_r"], n + 1)
                link(nc.vector.tensor_tensor(den2, den, es, ALU.add))
                link(nc.vector.reciprocal(rden, den2))
                nc.vector.tensor_tensor(pr, pr, rden.rearrange("p (g o) -> p g o", o=1).to_broadcast([P, 2, 256]), ALU.mult
                                        ).then_inc(s["pn_r"], 1)

            def retention_out(n, h, i):
                dve.wait_ge(s["oa"], n + 1)
                nc.vector.tensor_copy(o_all[:, bass.ds(i, 1), h * P:(h + 1) * P],
                                      p7[:, 0:P].rearrange("p (o c) -> p o c", o=1))
                nc.vector.scalar_tensor_tensor(S[:, h, :], S[:, h, :], GAMMA[h] ** P, p7[:, P:2 * P],
                                               ALU.mult, ALU.add).then_inc(s["st_u"], 1)

            def window_out(n, h, i):
                dve.wait_ge(s["osT_t"], n + 1)
                nc.vector.tensor_copy(oswT[:, h, bass.ds(i * P, P)], p7[:, 256:384])

            def mix(i, last):
                for h in range(1, H):
                    n = 4 * i + h
                    rotation(n - 1, h - 1, i)
                    if h == 1:
                        if last:
                            dve.wait_ge(s["tab_in"], 80)
                            link(nc.vector.scalar_tensor_tensor(A1[0:NS], A1[0:NS], 1.0, NGR[0:NS], ALU.add, ALU.mult))
                        h_scale(i + 2)
                        dve.wait_ge(s["ada_mm"], ADA1 + 1 + i)
                        dve.wait_ge(s["ada_b"], 16 * (i + 1))
                        m2v = mod2.rearrange("p (g c) -> p g c", g=2)
                        nc.vector.tensor_tensor(m2v, psS[0:9, :, 256:512], m2v, ALU.add).then_inc(s["mod_r"], 1)
                    else:
                        normalise(n - 2)
                        if h == 2:
                            h_shift()
                        window_out(n - 2, h - 2, i)
                    weigh(n - 1, h - 1)
                    retention_out(n - 1, h - 1, i)
                n = 4 * i + 3
                rotation(n, 3, i)
                normalise(n - 1)
                window_out(n - 1, 2, i)
                weigh(n, 3)
                nc.vector.tensor_copy(K2[:, 0:P], K2[:, P:2 * P])
                nc.vector.tensor_copy(band[:, :], cst("band")).then_inc(s["kwin"], 1)
                normalise(n)
                retention_out(n, 3, i)
                keys(i + 1, last)
                window_out(n, 3, i)
                nc.vector.tensor_copy(V2[:, 0:P], V2[:, P:2 * P]).then_inc(s["win"], 1)

            with dve.Fori(0, NT - 1) as i:
                link.loop(i, 4 * (6 + 3 + 2) + 1 + 3)
                mix(i, False)
            link.end(NT - 1)
            mix(NT - 1, True)
            def norm_o(t, n):
                dve.wait_ge(s["or_r"], t // NT + 1)
                x = o_all[:, t:t + n, :].rearrange("p t (h c) -> p (t h) c", h=H)
                nc.vector.tensor_tensor(x, x, orstd[:, 4 * t:4 * (t + n)].rearrange("p (h o) -> p h o", o=1)
                                        .to_broadcast([P, H * n, P]), ALU.mult).then_inc(s["on_r"], 1)

            dve.wait_ge(s["k_r"], NT + 1)
            for h in range(H):
                dve.wait_ge(s["spj"], h + 1)
                if h:
                    dve.wait_ge(s["srot"], h)
                bank_ = pj_bank[h % 2][0:NS, :]
                rotate(bank_[:, 0:256], (0, 256), "ret", 0, NS)
                rotate(bank_[:, 384:512], (384, 512), "swa", 256, NS)
                link.wait()
                nc.vector.tensor_tensor(rots[:, h, :], t1[0:NS], t2[0:NS], ALU.add).then_inc(s["srot"], 1)
                if h == 0:
                    dve.wait_ge(s["o_sq"], 1)
                    nc.vector.tensor_reduce(oms[:, 0:4 * NT], osq.rearrange("p (a c) -> p a c", c=P), AX.X, ALU.add
                                            ).then_inc(s["om_r"], 1)
                if h == 2:
                    norm_o(0, NT)
            dve.wait_ge(s["srot"], H)
            dve.wait_ge(s["sv_c"], H)
            for h in range(H):
                link(nc.vector.tensor_scalar(ks8[:, h, :], rots[:, h, P:2 * P], RSC, None, ALU.mult))
                link(nc.vector.tensor_tensor_reduce(junk8, rots[:, h, 0:P], ks8[:, h, :], 1.0, 0.0, ALU.mult, ALU.add,
                                                    qk8[:, h:h + 1]))
                nc.vector.tensor_tensor(vM[:, h], vs[:, h, :].rearrange("p (o c) -> p o c", o=1).to_broadcast([NS, NS, P]),
                                        ident[0:NS, 0:NS].rearrange("p (b o) -> p b o", o=1).to_broadcast([NS, NS, P]),
                                        ALU.mult).then_inc(s["sqm"], 1)
            dve.wait_ge(s["sq_e"], 1)
            e8 = cst("eye8").rearrange("p (b c) -> p b c", b=NS)
            for h in range(H):
                nc.vector.tensor_tensor(qM[:, h], qsT[:, 8 * h:8 * h + 8].rearrange("p (o c) -> p o c", o=1)
                                        .to_broadcast([P, NS, NS]), e8, ALU.mult).then_inc(s["sqm"], 1)
            for g in range(2):
                nc.vector.tensor_scalar(qB[:, :, :, g], qsT[:, 32:64].rearrange("p (h b) -> p b h", h=H),
                                        cst("grp")[:, g:g + 1], None, ALU.mult).then_inc(s["sqm"], 1)
            dve.wait_ge(s["sst_in"], 16)
            dve.wait_ge(s["mod_st"], 16 * (2 + NT))

            def rg(n):
                m = RG_ORDER[n % 4]
                dve.wait_ge(s["rg_s"], n + 1)
                dst = oretT[:, m, (n // 4) * CHUNK:(n // 4 + 1) * CHUNK]
                link(nc.vector.tensor_tensor(sg[:, m, :], rg_bank[m][:, 0:CHUNK], sg[:, m, :], ALU.mult))
                if n == 0:
                    dve.wait_ge(s["g_e"], NT)
                if n == 8:
                    dve.wait_ge(s["g_e"], NT + 1)
                nc.vector.tensor_tensor(dst, dst, sg[:, m, :], ALU.mult).then_inc(s["rg_r"], 1)

            for h in range(H):
                dve.wait_ge(s["socr"], h + 1)
                stv = st[:, h].rearrange("p (a b) e -> p a (b e)", a=2)
                nc.vector.scalar_tensor_tensor(stv, stv, GAMMA[h], psS[:, :, :], ALU.mult, ALU.add
                                               ).then_inc(s["sst_r"], 1)
                link(nc.vector.tensor_scalar(tmp8, p7[0:NS, 0:P], GAMMA[h], None, ALU.mult))
                nc.vector.scalar_tensor_tensor(o_all[0:NS, NT, h * P:(h + 1) * P], vs[:, h, :], qk8[:, h:h + 1], tmp8,
                                               ALU.mult, ALU.add).then_inc(s["so_r"], 1)
                rg(h)
            dve.wait_ge(s["o_sq"], 2)
            nc.vector.tensor_reduce(oms[:, 4 * NT:], osq8.rearrange("p (a c) -> p a c", c=P), AX.X, ALU.add
                                    ).then_inc(s["om_r"], 1)
            rg(4)
            dve.wait_ge(s["ssc"], 1)
            sc8 = psS[0:NS, :, :].rearrange("p a (b c) -> p (a b) c", b=4)
            link(nc.vector.tensor_reduce(mx8, sc8, AX.X, ALU.max))
            link(nc.vector.tensor_scalar(m8, mx8, ASC, sinkc[:, :], ALU.mult, ALU.max))
            link(nc.vector.scalar_tensor_tensor(pS, sc8, ASC, m8.rearrange("p (b o) -> p b o", o=1).to_broadcast([NS, NS, P]),
                                                ALU.mult, ALU.subtract))
            nc.vector.tensor_scalar(es8, m8, -1.0, sinkc[:, :], ALU.mult, ALU.add).then_inc(s["ssm"], 1)
            norm_o(NT, 1)
            dve.wait_ge(s["sex"], 1)
            link(nc.vector.tensor_reduce(den8, pS, AX.X, ALU.add))
            link(nc.vector.tensor_tensor(den8, den8, es8, ALU.add))
            link(nc.vector.reciprocal(rd8, den8))
            nc.vector.tensor_tensor(pS, pS, rd8.rearrange("p (b o) -> p b o", o=1).to_broadcast([NS, NS, P]), ALU.mult
                                    ).then_inc(s["spn"], 1)
            rg(5)
            rg(6)
            rg(7)
            dve.wait_ge(s["spv"], 1)
            pv = p5[:, 64:128].rearrange("p (b h g) -> p h b g", b=NS, h=H)
            for g in range(2):
                r = slice(g * HD, (g + 1) * HD)
                nc.vector.tensor_copy(oswT[r, :, T:TA], pv[r, :, :, g]).then_inc(s["sosw"], 1)
            def h_rest(c):
                cols = slice(c * CHUNK, (c + 1) * CHUNK)
                dve.wait_ge(s["h_hi"], c + 1)
                dve.wait_ge(s["rg_mm"], 4 * (c + 1))
                for a, b, r in h_hi:
                    last = nc.vector.tensor_tensor(hT_lo[:, a:b, cols], hT[:, a:b, cols], r[:, :, cols], ALU.subtract)
                last.then_inc(s["h_lo"], 1)

            h_rest(0)
            rg(8)
            h_rest(1)
            rg(9)
            rg(10)

            def weights_lo(m, slot):
                dve.wait_ge(s["w_hi"], m + 1)
                nc.vector.tensor_tensor(z_lo[slot], z_raw[slot], z_hi[slot], ALU.subtract).then_inc(s["w_lo"], 1)

            weights_lo(0, 0)
            rg(11)
            h_rest(2)

            def merge(m, slot, split=True):
                for c in range(3):
                    g = 3 * m + c
                    q = (3 * slot + c) % 2
                    by = lift[4 * q:]
                    if c == 1 and split:
                        weights_lo(m + 1, 1 - slot)
                    dve.wait_ge(s["mg_s"], 2 * g + 2)
                    for j in range(2):
                        link(nc.vector.tensor_tensor(g2b[:, q, 2 + j, :], by[2 + j][:, 0:CHUNK], g2b[:, q, j, :], ALU.mult))
                    nc.vector.tensor_tensor(mT[:, bass.ds(m, 1), bass.ds(c * CHUNK, CHUNK)],
                                            g2b[:, q, 2:3, :], g2b[:, q, 3:4, :], ALU.add).then_inc(s["mg_r"], 1)

            with dve.Fori(0, KD // 2 - 1) as m2_:
                link.loop(m2_, 12)
                merge(2 * m2_, 0)
                merge(2 * m2_ + 1, 1)
            link.end(KD // 2 - 1)
            merge(KD - 2, 0)
            merge(KD - 1, 1, split=False)
            def merged_lo(t, slot, w=P, first=False):
                if first:
                    dve.wait_ge(s["w_hi"], KD + 1)
                else:
                    dve.wait_ge(s["m_c"], t)
                nc.vector.tensor_tensor(m_lo[slot][:, :, 0:w], mT[:, :, bass.ds(t * P, w)], m_hi[slot][:, :, 0:w],
                                        ALU.subtract).then_inc(s["m_lo"], 1)

            merged_lo(0, 0, first=True)
            for k in range(KD):
                dve.wait_ge(s["w_hi"], KD + k + 2)
                nc.vector.tensor_tensor(wo_lo[k], R0[:, k * D:(k + 1) * D], wo_hi[k], ALU.subtract
                                        ).then_inc(s["w_lo"], 1)
            dve.wait_ge(s["tab_in"], 80 + 64)
            link(nc.vector.scalar_tensor_tensor(A2, A2, 1.0, n2row, ALU.add, ALU.mult))
            link(nc.vector.memset(lg[:, NT, :], 0.0))

            def resid(t, slot, rows=P):
                dve.wait_ge(s["wo_mm"], t + 1)
                xd = x1[0:rows, bass.ds(t, 1), :].rearrange("p o c -> p (o c)")
                for n in range(2):
                    cols = slice(n * 512, (n + 1) * 512)
                    link.mark(nc.vector.tensor_tensor(xd[:, cols], o_bank[slot][n][0:rows], G1[0:rows, cols], ALU.mult))
                link.wait()
                dve.wait_ge(s["xr_in"], 16 * t + 16)
                nc.vector.tensor_tensor(xd, xd, xt[0:rows], ALU.add).then_inc(s["x1_r"], 1)

            def norm2(t, rows=P, first=False):
                dve.wait_ge(s["rs2_r"], t + 1)
                if not first:
                    dve.wait_ge(s["h2_t"], t)
                    dve.wait_ge(s["h2_st"], 16 * t)
                xd = x1[0:rows, bass.ds(t, 1), :].rearrange("p o c -> p (o c)")
                link(nc.vector.scalar_tensor_tensor(hrow[0:rows], xd, rstd[0:rows], A2[0:rows], ALU.mult, ALU.mult))
                nc.vector.tensor_tensor(hrow[0:rows], hrow[0:rows], B2[0:rows], ALU.add).then_inc(s["h2_r"], 1)

            def logits(t, rows=P):
                dve.wait_ge(s["rt_mm"], t + 1)
                nc.vector.tensor_tensor(lg[0:rows, bass.ds(t, 1), :], p7[0:rows, 0:NL].rearrange("p (o c) -> p o c", o=1),
                                        brow[0:rows].rearrange("p (o c) -> p o c", o=1), ALU.add).then_inc(s["lg_r"], 1)

            merged_lo(1, 1)
            resid(0, 0)
            norm2(0, first=True)
            with dve.Fori(0, NT // 2 - 1) as t2_:
                link.loop(t2_, 6)
                for t, slot in ((2 * t2_ + 1, 1), (2 * t2_ + 2, 0)):
                    merged_lo(t + 1, 1 - slot)
                    resid(t, slot)
                    logits(t - 1)
                    norm2(t)
            link.end(NT // 2 - 1)
            merged_lo(NT, 0, NS)
            resid(NT - 1, 1)
            logits(NT - 2)
            norm2(NT - 1)
            dve.wait_ge(s["tab_in"], 144 + 48)
            link(nc.vector.scalar_tensor_tensor(A2[0:NS], A2[0:NS], 1.0, n2row[0:NS], ALU.add, ALU.mult))
            resid(NT, 0, NS)
            logits(NT - 1)
            norm2(NT, NS)
            logits(NT, NS)

            dve.wait_ge(s["lg_r"], NT + 1)
            dve.wait_ge(s["h2_st"], 16 * (NT + 1))
            tt, n9 = nc.vector.tensor_tensor, NT + 1

            def b3(a, k):
                return a.to_broadcast([P, n9, k])

            iota = cst("iota").rearrange("p (o e) -> p o e", o=1)

            def first_max(x, k, mxv, eq, cn, ix, oh):
                link(nc.vector.tensor_reduce(mxv, x, AX.X, ALU.max))
                link(tt(eq, x, b3(mxv, k), ALU.is_equal))
                link(nc.vector.scalar_tensor_tensor(cn, eq, -64.0, b3(iota[:, :, 0:k], k), ALU.mult, ALU.add))
                link(nc.vector.tensor_reduce(ix, cn, AX.X, ALU.min))
                link(tt(oh, cn, b3(ix, k), ALU.is_equal))

            g4 = lg[:, :, 0:NG]
            first_max(g4, NG, gmx, eq4, cnd4, gix, oh4)
            tt(gsh, g4, b3(gmx, NG), ALU.subtract).then_inc(s["gsh_r"], 1)
            link(tt(ep, lg[:, :, NG:NL].rearrange("p t (g j) -> p t g j", g=NG),
                    oh4.rearrange("p t (g o) -> p t g o", o=1).to_broadcast([P, n9, NG, EPG]), ALU.mult))
            link(nc.vector.tensor_reduce(ein, ep.rearrange("p t g j -> p t j g"), AX.X, ALU.add))
            first_max(ein, EPG, v1, eqv, cnd, i1, oh1)
            link(nc.vector.scalar_tensor_tensor(e2, oh1, NEG, ein, ALU.mult, ALU.add))
            first_max(e2, EPG, v2_, eqv, cnd, i2, oh2)
            tt(dv, v2_, v1, ALU.subtract).then_inc(s["gsh_r"], 1)
            for mkj, ohj in ((mk1, oh1), (mk2, oh2)):
                link.mark(tt(mkj.rearrange("p t (g j) -> p t g j", g=NG),
                             oh4.rearrange("p t (g o) -> p t g o", o=1).to_broadcast([P, n9, NG, EPG]),
                             ohj.rearrange("p t (o j) -> p t o j", o=1).to_broadcast([P, n9, NG, EPG]), ALU.mult))
            link.wait()
            link(tt(mk, mk1, mk2, ALU.add))
            tt(mk, mk, b3(cst("valid").rearrange("p (t o) -> p t o", o=1), NE), ALU.mult).then_inc(s["mk_r"], 1)
            link.mark(nc.vector.memset(pre[:, 0, :], 0.0))
            for sums_j in sums:
                link.mark(nc.vector.memset(sums_j[:, 0:SUM_PAD], 0.0))
            link.wait()
            dve.wait_ge(s["rk_mm"], 1)
            tot = p1[:, 0:9 * NE].rearrange("p (t e) -> p t e", t=9)
            for t in range(NT):
                link(tt(pre[:, t + 1, :], pre[:, t, :], tot[:, t, :], ALU.add))
            link.mark(tt(cnt, pre[:, NT, :], tot[:, NT, :], ALU.add))
            link.wait()
            link.mark(tt(pre, pre, p0[:, 0:9 * NE].rearrange("p (t e) -> p t e", t=9), ALU.add))
            link(tt(thr_t, cnt.rearrange("p (e o) -> p e o", o=1).to_broadcast([P, NE, MAXOV]),
                    cst("thr").rearrange("p (o j) -> p o j", o=1).to_broadcast([P, NE, MAXOV]), ALU.is_gt))
            link(nc.vector.tensor_reduce(nbx, thr_t, AX.X, ALU.add))
            a, b = sums
            link(nc.vector.tensor_copy(a[:, SUM_PAD:], nbx))
            for sh in (1, 2, 4, 8, 16):
                link(tt(b[:, SUM_PAD:], a[:, SUM_PAD:], a[:, SUM_PAD - sh:SUM_PAD - sh + NE], ALU.add))
                a, b = b, a
            incl, free = a[:, SUM_PAD:], b[:, SUM_PAD:]
            link.mark(nc.vector.tensor_scalar(ge, pre, float(CAP), None, ALU.is_ge))
            link.mark(tt(pos, pre, cst("ec").rearrange("p (o e) -> p o e", o=1).to_broadcast([P, n9, NE]), ALU.add))
            link(tt(free, incl, nbx, ALU.subtract))
            link(nc.vector.tensor_scalar(free, free, float(CAP), float((NE - 1) * CAP), ALU.mult, ALU.add))
            link(tt(free, free, cst("ec"), ALU.subtract))
            link(tt(adj, ge, free.rearrange("p (o e) -> p o e", o=1).to_broadcast([P, n9, NE]), ALU.mult))
            link(tt(pos, pos, adj, ALU.add))
            for mkj in (mk1, mk2):
                link.mark(tt(mkj, pos, mkj, ALU.mult))
            link.wait()
            for j, mkj in enumerate((mk1, mk2)):
                link.mark(nc.vector.tensor_reduce(pf[:, :, j:j + 1], mkj, AX.X, ALU.add))
            link.wait()
            nc.vector.tensor_copy(posu[:, :].rearrange("p (t j) -> p t j", j=2), pf).then_inc(s["pos_r"], 1)
            dve.wait_ge(s["stab_in"], 16)

            def wide(a, k):
                return a.rearrange("p (t o) -> p t o", o=1).to_broadcast([P, N2, k])

            def rows(a, k):
                return a.rearrange("p (o e) -> p o e", o=1).to_broadcast([P, N2, k])

            pf2 = R4[:, 3104:3104 + N2]
            link(tt(past, wide(pf2, NBLK + 1), rows(blk0, NBLK + 1), ALU.is_ge))
            link(nc.vector.tensor_reduce(nblk18, past, AX.X, ALU.add))
            link(nc.vector.scalar_tensor_tensor(place18, nblk18, -float(CAP), pf2, ALU.mult, ALU.add))
            link(tt(atplace, wide(place18, CAP), rows(place, CAP), ALU.is_equal))
            link(tt(inblk, past[:, :, 0:NBLK], past[:, :, 1:NBLK + 1], ALU.subtract))
            tokw = tok[:, :].rearrange("p (t o) -> p t o", o=1).to_broadcast([P, n9, 2 * NBLK])
            in9 = R0[:, o2:o2 + N2 * NBLK].rearrange("p (t e) -> p t e", t=n9)
            tt(in9, in9, tokw, ALU.mult).then_inc(s["mk_r"], 1)
            link(tt(blk_t, incl[0:1].rearrange("p (o e) -> p o e", o=1).to_broadcast([1, NOVER, NE]),
                    cst("blk", 1).rearrange("p (b o) -> p b o", o=1).to_broadcast([1, NOVER, NE]), ALU.is_le))
            link(nc.vector.tensor_reduce(emap[:, 0:NOVER], blk_t, AX.X, ALU.add))
            link(nc.vector.tensor_scalar(emap[:, 0:NOVER], emap[:, 0:NOVER], float(NE - 1), None, ALU.min))
            link(nc.vector.tensor_copy(emap[:, NOVER:NOVER + 1], incl[0:1, NE - 1:NE]))
            nc.vector.tensor_copy(nover[:, :], emap).then_inc(s["ov_n"], 1)
            dve.wait_ge(s["gex_r"], 1)
            link(nc.vector.tensor_reduce(gsum, gsh, AX.X, ALU.add))
            link(nc.vector.reciprocal(pgr, gsum))
            dve.wait_ge(s["gex_r"], 2)
            link(nc.vector.tensor_scalar(v1, dv, 1.0, None, ALU.add))
            link(nc.vector.reciprocal(v2_, v1))
            wv = wsel[:, :].rearrange("p (t j) -> p t j", j=2)
            link(tt(wv[:, :, 0:1], pgr, v2_, ALU.mult))
            tt(wv[:, :, 1:2], wv[:, :, 0:1], dv, ALU.mult).then_inc(s["w_r"], 1)
            dve.wait_ge(s["slotT_t"], 1)
            nc.vector.tensor_copy(slotT[:, :], p2[0:CAP, 0:NBLK]).then_inc(s["slotT_r"], 1)

            def turn_out(b):
                dve.wait_ge(s["xgT_t"], b + 1)
                for j, bk in enumerate((p5, p6)):
                    nc.vector.tensor_copy(xgT[:, 4 * j:4 * j + 4, :], bk[:, 0:4 * CAP].rearrange("p (k t) -> p k t", k=4)
                                          ).then_inc(s["xgT_e"], 1)

            def hidden(b, slot):
                for f in range(2):
                    bk = up_bank[slot][f]
                    dve.wait_ge(s["hs"], 2 * b + f + 1)
                    nc.vector.tensor_tensor(hid[:, f, :], bk[:, 0:CAP], sgh[:, f, :], ALU.mult).then_inc(s["h_a"], 1)
                    dve.wait_ge(s["h_a"], 2 * b + f + 1)
                    nc.vector.tensor_tensor(hid[:, f, :], hid[:, f, :], bk[:, CAP:2 * CAP], ALU.mult).then_inc(s["hid_r"], 1)

            turn_out(0)
            with dve.Fori(0, NE // 2 - 1) as b2:
                for slot in range(2):
                    hidden(2 * b2 + slot, slot)
                    turn_out(2 * b2 + slot + 1)
            hidden(NE - 2, 0)
            turn_out(NE - 1)
            hidden(NE - 1, 1)
            n_over = dve.value_load(nover[0:1, NOVER:NOVER + 1], min_val=0, max_val=NOVER)
            with dve.If(n_over > 0):
                with dve.Fori(0, NOVER) as b:
                    with dve.If(b < n_over):
                        turn_out(NE + b)
                        hidden(NE + b, 0)
            dve.wait_ge(s["tab_in"], 192 + 48)

            def combine(t):
                r = P if t < NT else NS
                dve.wait_ge(s["y0_r"], t + 1)
                y0, y1, x = yg[0:r, t, 0], yg[0:r, t, 1], x1[0:r, t, :]
                link(nc.vector.scalar_tensor_tensor(y0, y1, wsel[0:r, 2 * t + 1:2 * t + 2], y0, ALU.mult, ALU.add))
                link(nc.vector.tensor_tensor(y0, y0, G2 if t < NT else G2s, ALU.mult))
                nc.vector.tensor_tensor(x, x, y0, ALU.add).then_inc(s["x2_r"], 1)

            def finish(t):
                r = P if t < NT else NS
                dve.wait_ge(s["rs3_r"], t + 1)
                if t >= 2:
                    dve.wait_ge(s[f"out_st{t % 2}"], 16 * (t // 2))
                nc.vector.scalar_tensor_tensor(yo[0:r, t % 2], x1[0:r, t, :], rstd3[0:r, t % 2:t % 2 + 1], FG[0:r],
                                               ALU.mult, ALU.mult).then_inc(s["yo_r"], 1)

            combine(0)
            for t in range(1, NT + 1):
                combine(t)
                finish(t - 1)
            finish(NT)

        @block.tensor
        def _(pe):
            mm = nc.tensor.matmul
            pe.wait_ge(s["const_in"], 16)
            pe.wait_ge(s["c_silu"], 1)
            for k in range(KD):
                last = nc.tensor.transpose(p2[:, 9 * k:9 * k + 9], csig[:, k * P:(k + 1) * P], ident[0:9, 0:9])
            last.then_inc(s["cT_t"], 1)
            pe.wait_ge(s["cT_r"], 1)
            cTv = cT[:, :].rearrange("p (k c) -> p k c", k=KD)

            for j in range(ADA1):
                pe.wait_ge(s[f"ada_in{j}"], 16)
                w = wada1[j].rearrange("p (k c) -> p k c", k=KD)
                for k in range(KD):
                    last = mm(ada_bank[j], cTv[:, k, :], w[:, k, :], start=k == 0, stop=k == KD - 1)
                last.then_inc(s["ada_mm"], 1)

            def h_turn(half):
                for k in range(4):
                    kk = 4 * half + k
                    last = nc.tensor.transpose((p6, p5)[half][:, k * P:(k + 1) * P], hrow[:, kk * P:(kk + 1) * P], ident)
                last.then_inc(s["hT_t"], 1)

            def kv(ks):
                for k in ks:
                    last = mm(p6[:, 0:256], hst[:, k, :], wkv[:, k, :], start=k == 0, stop=k == KD - 1)
                if k == KD - 1:
                    last.then_inc(s["kv_mm"], 1)

            pe.wait_ge(s["h_r"], 1)
            h_turn(0)
            h_turn(1)
            pe.wait_ge(s["hT_e"], 2)
            pe.wait_ge(s["wkv_in"], 16)
            kv(range(KD))

            def turn_qk(n, h):
                pe.wait_ge(s["rot"], n + 1)
                for j in range(3):
                    last = nc.tensor.transpose(p2[:, j * P:(j + 1) * P], rot[:, j * P:(j + 1) * P], ident)
                last.then_inc(s["qk_t"], 1)

            def scores(n, i):
                pe.wait_ge(s["qk_e"], n + 1)
                mm(p2[:, 384:512], qkT[:, P:2 * P], qkT[:, 0:P], start=True, stop=True)
                pe.wait_ge(s["kT_e"], i + 1)
                for g in range(2):
                    r = slice(g * HD, (g + 1) * HD)
                    last = mm(psS[:, g, 0:256], qkT[r, 256:384], K2[r, :], start=True, stop=True)
                last.then_inc(s["att_s"], 1)

            def outputs(n, h):
                pe.wait_ge(s["v_c"], n + 1)
                pe.wait_ge(s["kd_r"], n + 1)
                pe.wait_ge(s["at_r"], n + 1)
                mm(p7[:, 0:P], attT, vb, start=True, stop=False)
                mm(p7[:, 0:P], qdT, S[:, h, :], start=False, stop=True)
                mm(p7[:, P:2 * P], kd, vb, start=True, stop=True).then_inc(s["oa"], 1)

            def turn_probs(n):
                pe.wait_ge(s["pn_r"], n + 1)
                for g in range(2):
                    for b in range(2):
                        last = nc.tensor.transpose(p5[:, (2 * g + b) * P:(2 * g + b + 1) * P],
                                                   pr[:, g, b * P:(b + 1) * P], ident)
                last.then_inc(s["pT_t"], 1)

            def window(n, i):
                pe.wait_ge(s["pT_e"], n + 1)
                pe.wait_ge(s["st_u"], n + 1)
                pe.wait_ge(s["v_e"], i + 1)
                for g in range(2):
                    r = slice(g * HD, (g + 1) * HD)
                    for b in range(2):
                        last = mm(p7[r, 256:384], V2[:, b * P + g * HD:b * P + (g + 1) * HD], prT[:, g, b, :],
                                  start=b == 0, stop=b == 1)
                last.then_inc(s["osT_t"], 1)

            def project_h(h, ks, rows=P, done="pj"):
                for k in ks:
                    last = mm(pj_bank[h % 2][0:rows, :], hst[:, k, 0:rows], wqh[:, h, k, :], start=k == 0, stop=k == KD - 1)
                if k == KD - 1:
                    last.then_inc(s[done], 1)

            def ada_later(i):
                pe.wait_ge(s["ada_w"], 16 * (i + 1))
                w = wada2.rearrange("p (k c) -> p k c", k=KD)
                for g in range(2):
                    for k in range(KD):
                        last = mm(psS[0:9, g, 256:512], cTv[:, k, :], w[:, k, g * 256:(g + 1) * 256],
                                  start=k == 0, stop=k == KD - 1)
                last.then_inc(s["ada_mm"], 1)

            def mix(i, last_):
                for h in range(1, H):
                    n = 4 * i + h
                    pe.wait_ge(s[f"wq_in{h}"], 16)
                    project_h(h, (0, 1))
                    if h == 1:
                        pe.wait_ge(s["k_r"], i + 1)
                        pe.wait_ge(s["v_e"], i + 1)
                        nc.tensor.transpose(p6[:, 256:384], krot[:, :], ident).then_inc(s["kT_t"], 1)
                    project_h(h, (2, 3))
                    turn_qk(n - 1, h - 1)
                    if h > 1:
                        turn_probs(n - 2)
                    else:
                        ada_later(i)
                    project_h(h, (4, 5))
                    if h > 1:
                        window(n - 2, i)
                    else:
                        pe.wait_ge(s["mod_r"], ADA1 + 1 + i)
                    scores(n - 1, i)
                    project_h(h, (6, 7))
                    outputs(n - 1, h - 1)
                n = 4 * i + 3
                rows, done = (NS, "spj") if last_ else (P, "pj")
                pe.wait_ge(s["h_r"], i + 2)
                h_turn(0)
                h_turn(1)
                pe.wait_ge(s["hT_e"], 2 * i + 3)
                project_h(0, (0, 1), rows, done)
                turn_qk(n, 3)
                project_h(0, (2, 3), rows, done)
                pe.wait_ge(s["hT_e"], 2 * i + 4)
                turn_probs(n - 1)
                project_h(0, (4, 5), rows, done)
                window(n - 1, i)
                scores(n, i)
                kv(range(KD))
                outputs(n, 3)
                project_h(0, (6,), rows, done)
                turn_probs(n)
                project_h(0, (7,), rows, done)
                window(n, i)

            pe.wait_ge(s["wq_in0"], 16)
            project_h(0, range(KD))
            with pe.Fori(0, NT - 1) as i:
                mix(i, False)
            mix(NT - 1, True)
            for h in range(1, H):
                if h >= 2:
                    pe.wait_ge(s["sv_c"], h - 1)
                project_h(h, range(KD), NS, "spj")
            pe.wait_ge(s["srot"], H)
            pe.wait_ge(s["nm_r"], 4 * NT)
            for h in range(H):
                nc.tensor.transpose(p2[:, 8 * h:8 * h + 8], rots[:, h, 0:P], ident[0:NS, 0:NS])
                last = nc.tensor.transpose(p2[:, 32 + 8 * h:40 + 8 * h], rots[:, h, 256:384], ident[0:NS, 0:NS])
            last.then_inc(s["sq_t"], 1)

            def turn_o(t, rows=P):
                pe.wait_ge(s["on_r"], t // NT + 1)
                if t >= 2:
                    pe.wait_ge(s["g_e"], t - 1)
                for h in range(H):
                    last = nc.tensor.transpose(g_bank[t % 2][:, h * P:h * P + rows], o_all[0:rows, t, h * P:(h + 1) * P],
                                               ident[0:rows, 0:rows])
                last.then_inc(s["g_t"], 1)

            def rg(n):
                c, m = n // 4, RG_ORDER[n % 4]
                if n >= 4:
                    pe.wait_ge(s["rg_r"], n - 3)
                if n == 0:
                    pe.wait_ge(s["sv_c"], H)
                    pe.wait_ge(s["rg_in"], 16)
                    pe.wait_ge(s["hT_c"], NT + 1)
                    pe.wait_ge(s["v_e"], NT + 1)
                if n == 3:
                    pe.wait_ge(s["sq_e"], 1)
                for k in range(KD):
                    last = mm(rg_bank[m][:, 0:CHUNK], wrg[:, k, m * P:(m + 1) * P],
                              hT[:, k, c * CHUNK:(c + 1) * CHUNK], start=k == 0, stop=k == KD - 1)
                last.then_inc(s["rg_mm"], 1)

            pe.wait_ge(s["win"], NT)
            for t in range(NT):
                turn_o(t)
            pe.wait_ge(s["sst_in"], 16)
            pe.wait_ge(s["sqm"], 2 * H + 2)
            pe.wait_ge(s["g_e"], NT)
            for h in range(H):
                if h:
                    pe.wait_ge(s["sst_r"], h)
                    pe.wait_ge(s["so_r"], h)
                for b in range(NS):
                    mm(p7[0:NS, 0:P], qM[:, h, b, :], st[:, h, b, :], start=b == 0, stop=b == NS - 1)
                for a in range(2):
                    last = mm(psS[:, a, :], ks8[:, h, :], vM[:, h, 4 * a:4 * a + 4, :], start=True, stop=True)
                last.then_inc(s["socr"], 1)
                rg(h)
            pe.wait_ge(s["swin_c"], 64)
            pe.wait_ge(s["sst_r"], H)
            for b in range(NS):
                last = nc.tensor.transpose(psS[:, b // 4, (b % 4) * P:(b % 4 + 1) * P], kwin[:, b, :], ident)
            last.then_inc(s["skT_t"], 1)
            rg(4)
            pe.wait_ge(s["skT_e"], 2)
            for b in range(NS):
                last = mm(psS[0:NS, b // 4, (b % 4) * P:(b % 4 + 1) * P], qB[:, b].rearrange("p h g -> p (h g)"),
                          kwT[:, b, :], start=True, stop=True)
            last.then_inc(s["ssc"], 1)
            rg(5)
            rg(6)
            pe.wait_ge(s["spn"], 1)
            for b in range(NS):
                last = nc.tensor.transpose(p5[:, 8 * b:8 * b + 8], pS[:, b, :], ident[0:NS, 0:NS])
            last.then_inc(s["spT_t"], 1)
            rg(7)
            pe.wait_ge(s["spT_e"], 1)
            for b in range(NS):
                last = mm(p5[:, 64 + 8 * b:72 + 8 * b], vwin[:, b, :], pTs[:, b, :], start=True, stop=True)
            last.then_inc(s["spv"], 1)
            turn_o(NT, NS)
            for n in range(8, 12):
                rg(n)

            def merge(m2_, slot, free):
                pe.wait_ge(s["w_lo"], 2 * m2_ + slot + 1)
                for c in range(3):
                    g = 3 * (2 * m2_ + slot) + c
                    if free or 3 * slot + c >= 2:
                        pe.wait_ge(s["mg_r"], g - 1)
                    elif c == 0:
                        pe.wait_ge(s["rg_r"], 12)
                    if not free and slot == 0:
                        pe.wait_ge(s["h_lo"], c + 1)
                    bs = lift[4 * ((3 * slot + c) % 2):]
                    cols = slice(c * CHUNK, (c + 1) * CHUNK)
                    for j in range(2):
                        for k in range(KD):
                            wc = slice((KD * j + k) * P, (KD * j + k + 1) * P)
                            for n, (w, x) in enumerate(((z_hi, hT_hi[k]), (z_hi, hT_lo[:, k, :]), (z_lo, hT_hi[k]))):
                                mm(bs[j][:, 0:CHUNK], w[slot][:, wc], x[:, cols], start=k == 0 and n == 0,
                                   stop=k == KD - 1 and n == 2)
                    for j, src in enumerate((oretT, oswT)):
                        for k in range(H):
                            last = mm(bs[2 + j][:, 0:CHUNK], wy[slot][:, (4 * j + k) * P:(4 * j + k + 1) * P], src[:, k, cols],
                                      start=k == 0, stop=k == H - 1)
                    last.then_inc(s["mg_mm"], 1)

            merge(0, 0, False)
            merge(0, 1, False)
            with pe.Fori(1, KD // 2) as m2_:
                merge(m2_, 0, True)
                merge(m2_, 1, True)

            def project(t, slot, part, rows=P, first=False, w_new=False):
                if part == 0:
                    pe.wait_ge(s["m_lo"], t + 1)
                    if not first:
                        pe.wait_ge(s["x1_r"], t - 1)
                for k in ((0, 1), (2, 3, 4), (5, 6, 7))[part]:
                    if w_new:
                        pe.wait_ge(s["w_lo"], KD + k + 1)
                    for n in range(2):
                        cols = slice(n * 512, (n + 1) * 512)
                        for j, (m, w) in enumerate(((m_hi, wo_hi), (m_hi, wo_lo), (m_lo, wo_hi))):
                            last = mm(o_bank[slot][n][0:rows], m[slot][:, k, 0:rows], w[k][:, cols],
                                      start=k == 0 and j == 0, stop=k == KD - 1 and j == 2)
                if part == 2:
                    last.then_inc(s["wo_mm"], 1)

            def router_turn(t, rows=P):
                pe.wait_ge(s["h2_r"], t + 1)
                for k in range(KD):
                    last = nc.tensor.transpose((p5, p6)[k // 4][:, (k % 4) * P:(k % 4) * P + rows],
                                               hrow[0:rows, k * P:(k + 1) * P], ident[0:rows, 0:rows])
                last.then_inc(s["h2_t"], 1)

            def router(t, rows=P):
                pe.wait_ge(s["h2_e"], 2 * t + 2)
                for k in range(KD):
                    last = mm(p7[0:rows, 0:NL], h2T[:, k, 0:rows], rwt[:, k * NL:(k + 1) * NL], start=k == 0, stop=k == KD - 1)
                last.then_inc(s["rt_mm"], 1)

            def out(t, slot, rows=P, first=False):
                project(t, slot, 0, rows, first)
                project(t, slot, 1, rows)
                router_turn(t - 1)
                project(t, slot, 2, rows)
                router(t - 1)

            pe.wait_ge(s["mg_r"], 3 * KD)
            for part in range(3):
                project(0, 0, part, first=True, w_new=True)
            out(1, 1, first=True)
            with pe.Fori(1, NT // 2) as t2_:
                for slot in range(2):
                    out(2 * t2_ + slot, slot)
            out(NT, 0, NS)
            router_turn(NT, NS)
            router(NT, NS)
            pe.wait_ge(s["mk_r"], 1)
            mkf = R4[:, 1536:1536 + 9 * NE]
            mm(p0[:, 0:9 * NE], cst("tri"), mkf, start=True, stop=True)
            mm(p1[:, 0:9 * NE], cst("ones"), mkf, start=True, stop=True).then_inc(s["rk_mm"], 1)
            pe.wait_ge(s["mk_r"], 2)
            for j in range(2 * (NT + 1)):
                last = mm(p2[0:CAP, 0:NBLK], atplace[:, j, :], inblk[:, j, :], start=j == 0, stop=j == 2 * NT + 1)
            last.then_inc(s["slotT_t"], 1)

            def turn(b, slot, n):
                pe.wait_ge(s[f"xg_in{slot}"], 16 * n)
                for k in range(KD):
                    last = nc.tensor.transpose((p5, p6)[k // 4][:, (k % 4) * CAP:(k % 4 + 1) * CAP],
                                               xg[0:CAP, slot, k * P:(k + 1) * P], ident[0:CAP, 0:CAP])
                last.then_inc(s["xgT_t"], 1)

            def up(b, slot, n):
                pe.wait_ge(s[f"w13_in{slot}"], 16 * n)
                pe.wait_ge(s["xgT_e"], 2 * b + 2)
                for f in range(2):
                    for w in range(2):
                        for k in range(KD):
                            c0 = w * 2048 + k * DE + f * P
                            last = mm(up_bank[slot][f][:, w * CAP:(w + 1) * CAP], we[slot][:, c0:c0 + P], xgT[:, k, :],
                                      start=k == 0, stop=k == KD - 1)
                    last.then_inc(s["s1"], 1)

            def down(b, slot, n):
                pe.wait_ge(s[f"w2_in{slot}"], 16 * n)
                for f in range(2):
                    pe.wait_ge(s["hid_r"], 2 * b + f + 1)
                    for nn in range(2):
                        c0 = 4096 + f * D + nn * 512
                        last = mm(psS[0:CAP, nn, :], hid[:, f, :], we[slot][:, c0:c0 + 512], start=f == 0, stop=f == 1)
                last.then_inc(s["s2"], 1)

            turn(0, 0, 1)
            with pe.Fori(0, NE // 2 - 1) as b2:
                for slot in range(2):
                    b = 2 * b2 + slot
                    up(b, slot, b2 + 1)
                    turn(b + 1, 1 - slot, b2 + 1 + slot)
                    down(b, slot, b2 + 1)
            up(NE - 2, 0, NE // 2)
            turn(NE - 1, 1, NE // 2)
            down(NE - 2, 0, NE // 2)
            up(NE - 1, 1, NE // 2)
            down(NE - 1, 1, NE // 2)
            n_over = pe.value_load(nover[0:1, NOVER:NOVER + 1], min_val=0, max_val=NOVER)
            with pe.If(n_over > 0):
                with pe.Fori(0, NOVER) as b:
                    with pe.If(b < n_over):
                        turn(NE + b, 0, NE // 2 + 1 + b)
                        up(NE + b, 0, NE // 2 + 1 + b)
                        down(NE + b, 0, NE // 2 + 1 + b)


def constants():
    f = np.float32
    c = np.zeros((P, NC), f)

    def put(name, a):
        lo, hi = COLS[name]
        c[:, lo:hi] = a

    i = np.arange(P)
    ld = np.log(np.asarray(GAMMA))
    put("ident", np.eye(P))
    d = i[None, :] - i[:, None]
    put("dmask", np.concatenate([np.where(d >= 0, np.exp(ld[h] * np.maximum(d, 0)) * RSC, 0.0) for h in range(H)], 1))
    put("qdec", np.tile(np.concatenate([np.exp(ld[h] * (i + 1.0)) for h in range(H)])[None], (P, 1)))
    put("kdec", np.stack([np.exp(ld[h] * (P - 1.0 - i)) * RSC for h in range(H)], 1))
    dist = i[:, None] - (np.arange(2 * P)[None, :] - P)
    band = np.where((dist >= 0) & (dist < P), 0.0, NEG).astype(f)
    put("band", band)
    band0 = band.copy()
    band0[:, :P] = NEG
    put("tri", (i[:, None] < i[None, :]).astype(f))
    put("ones", 1.0)
    put("half", -0.5)
    put("ec", np.arange(NE) * CAP)
    put("iota", np.arange(8))
    put("thr", np.arange(1, MAXOV + 1) * CAP)
    valid = np.ones((P, NT + 1), f)
    valid[NS:, NT] = 0
    put("valid", valid)
    put("blk", np.arange(NOVER))
    put("eye8", np.tile(np.eye(8).reshape(1, 64), (P, 1)))
    put("grp", np.stack([(i < HD), (i >= HD)], 1).astype(f))
    put("inv_d", 1.0 / D)
    put("eps", EPS)
    pos = np.full((NT + 1) * P, T, np.float64)
    pos[:T] = np.arange(T)
    inv_r = (1.0 / (10000.0 ** (np.arange(64, dtype=f) * f(1.0 / 63)).astype(np.float64)).astype(f)).astype(f)
    inv_s = (10000.0 ** (-np.arange(0, HD, 2) / HD)).astype(f)
    rope = np.zeros(((NT + 1) * P, 384), f)
    ang = (pos.astype(f)[:, None] * inv_r).astype(np.float64)
    rope[:, 0:128] = np.repeat(np.cos(ang), 2, 1)
    rope[:, 128:256] = np.stack([-np.sin(ang), np.sin(ang)], 2).reshape(-1, 128)
    ang = (pos.astype(f)[:, None] * inv_s).astype(np.float64)
    rope[:, 256:320] = np.tile(np.cos(ang), (1, 2))
    rope[:, 320:384] = np.concatenate([-np.sin(ang), np.sin(ang)], 1)
    tok = ((np.arange(NT + 1)[None, :] * P + i[:, None]) * valid).astype(f)
    slots = np.tile(np.concatenate([np.arange(NBLK + 1) * CAP, np.arange(CAP) - CAP])[None], (P, 1)).astype(f)
    return c, band0, rope.reshape(NT + 1, P, 384), tok, slots


def kernel(**x):
    from concourse import bacc
    from concourse.bass_utils import run_bass_kernel_spmd

    x = {k: np.asarray(a) for k, a in x.items()}
    c, band0, rope, tok, slots = constants()
    tiles = np.zeros((NT + 1, P, D), np.float32)
    tiles[:NT] = x["x_prompt"].reshape(NT, P, D)
    tiles[NT, :NS] = x["x_sample"].reshape(NS, D)

    def ktiles(w):
        return w.reshape(-1, P, w.shape[1]).transpose(1, 0, 2)

    w_in = x["w_in"][0]
    rq, rk, rv, rg, sq, sk, sv, za, zb = np.split(w_in, np.cumsum([512, 512, 512, 512, 512, 128, 128, D])[:], axis=1)
    groups = []
    for h in range(H):
        a = slice(h * P, (h + 1) * P)
        groups.append(np.concatenate([rq[:, a], rk[:, a], rv[:, a], sq[:, h * HD:(h + 1) * HD],
                                      sq[:, (h + 4) * HD:(h + 5) * HD]], 1))
    w_qkv = np.concatenate([ktiles(g).reshape(P, -1) for g in groups] +
                           [ktiles(np.concatenate([sk, sv], 1)).reshape(P, -1)], 1)
    up_s = x["w_up_swa"][0].reshape(2, H, HD, D).transpose(1, 0, 2, 3).reshape(H * P, D)
    lift = np.concatenate([ktiles(w).reshape(P, -1, KD, P).transpose(2, 0, 1, 3)
                           for w in (za, zb, x["w_up_ret"][0], up_s)], 2).reshape(KD, P, 24 * P)
    we = np.concatenate([
        x["w1"][0].reshape(NE, KD, P, DE).transpose(0, 2, 1, 3).reshape(NE, P, -1),
        x["w3"][0].reshape(NE, KD, P, DE).transpose(0, 2, 1, 3).reshape(NE, P, -1),
        x["w2"][0].reshape(NE, 2, P, D).transpose(0, 2, 1, 3).reshape(NE, P, -1)], 2)
    sink = x["sink"][0].reshape(2, H).T.reshape(-1)
    ins = {
        "const": c, "band0": band0, "rope": rope, "tok": tok, "slots": slots, "x": tiles,
        "c": np.concatenate([x["c_prompt"], x["c_sample"]], 0),
        "w_ada": x["w_ada"][0].reshape(KD, P, ADA, 512).transpose(2, 1, 0, 3).reshape(ADA, P, KD * 512),
        "b_ada": x["b_ada"],
        "n1": x["norm1_g"], "n2": x["norm2_g"], "fg": x["final_g"].reshape(1, D),
        "w_qkv": w_qkv, "w_rg_gate": ktiles(rg).reshape(P, -1), "lift": lift,
        "w_o": ktiles(x["w_o"][0]).reshape(P, -1), "we": we,
        "rw": ktiles(np.concatenate([x["w_rg"][0], x["w_re"][0]], 1)).reshape(P, -1),
        "brow": np.tile(np.concatenate([x["b_rg"][0], x["b_re"][0]])[None], (P, 1)),
        "sinkr": np.tile(sink[None], (P, 1)), "sinkc": sink.reshape(NS, 1),
        "state": x["state_ret"][0].transpose(2, 1, 0, 3).reshape(P, -1),
        "ck": x["cache_swa_k"][0].transpose(1, 0, 2, 3).reshape(P, NS, P),
        "cv": x["cache_swa_v"][0].transpose(1, 0, 2, 3).reshape(P, NS, P),
    }
    outs = {"y": (TA, D), "st_p": (P, H * P), "st_s": (P, H * NS * P), "kp": (P, P), "vp": (P, P),
            "ks": (P, NS, P), "vs": (P, NS, P)}
    nc = bacc.Bacc("TRN2", target_bir_lowering=False, num_devices=1)
    arrays, A, O = {}, {}, {}
    for name, a in ins.items():
        a = np.ascontiguousarray(a)
        arrays[f"in_{name}"] = a
        A[name] = nc.dram_tensor(f"in_{name}", a.shape, mybir.dt.from_np(a.dtype), kind="ExternalInput").ap()
    for name, shape in outs.items():
        O[name] = nc.dram_tensor(f"out_{name}", shape, F32, kind="ExternalOutput").ap()
    build(nc, A, O)
    r = run_bass_kernel_spmd(nc, [arrays], core_ids=[0]).results[0]
    o = {name: np.asarray(r[f"out_{name}"]) for name in outs}
    return (o["y"][:T].reshape(1, T, D), o["y"][T:].reshape(NS, 1, D),
            np.ascontiguousarray(o["st_p"].reshape(P, H, P).transpose(1, 0, 2)).reshape(1, 1, H, P, P),
            np.ascontiguousarray(o["st_s"].reshape(P, H, NS, P).transpose(2, 1, 0, 3)).reshape(1, NS, H, P, P),
            o["kp"].reshape(1, 1, P, 2, HD), o["vp"].reshape(1, 1, P, 2, HD),
            np.ascontiguousarray(o["ks"].transpose(1, 0, 2)).reshape(1, NS, P, 2, HD),
            np.ascontiguousarray(o["vs"].transpose(1, 0, 2)).reshape(1, NS, P, 2, HD))
```
